# Optimizing a Trainium2 kernel written in Bass

```python
import jax
import jax.numpy as jnp
from jax import lax
import numpy as np

D_MODEL = 1024
BATCH = 1
SEQ = 512
DEPTH = 1

D_FF = 2816
MACARON_WEIGHT = 0.5
NORM_EPS = 1e-6
CONV_WIDTH = 4
MLSTM_HEADS = 4
MLSTM_HEAD_DIM = 128
MLSTM_WIDTH = MLSTM_HEADS * MLSTM_HEAD_DIM
MLSTM_CHUNK = 64
NSA_HEADS = 8
NSA_KV_GROUPS = 2
NSA_HEADS_PER_GROUP = NSA_HEADS // NSA_KV_GROUPS
NSA_HEAD_DIM = 64
NSA_WIDTH = NSA_HEADS * NSA_HEAD_DIM
NSA_KV_WIDTH = NSA_KV_GROUPS * NSA_HEAD_DIM
CMP_BLOCK = 32
CMP_STRIDE = 16
CMP_HIDDEN = 256
SEL_BLOCK = 64
N_SELECT = 16
WINDOW = 256
NSA_QUERY_BLOCK = 32
FORCE_SCORE = 1e4
NEG_BIG = -1e30
IN_SPLITS = (MLSTM_WIDTH, MLSTM_WIDTH, MLSTM_WIDTH, MLSTM_WIDTH, 2 * MLSTM_HEADS,
             NSA_WIDTH, NSA_KV_WIDTH, NSA_KV_WIDTH, NSA_KV_WIDTH, NSA_KV_WIDTH, NSA_KV_WIDTH, NSA_KV_WIDTH,
             3 * NSA_HEADS, D_MODEL, D_MODEL)
D_IN = sum(IN_SPLITS)

kernel_name = "hybrid_mlstm_nsa_macaron_block"

def rmsnorm(x, gain):
    x32 = x.astype(jnp.float32)
    y = x32 * lax.rsqrt(jnp.mean(x32 * x32, axis=-1, keepdims=True) + NORM_EPS)
    return (y * gain.astype(jnp.float32)).astype(x.dtype)

def swiglu(u, wg, wu, wd):
    return (jax.nn.silu(u @ wg) * (u @ wu)) @ wd

def sandwich(h, fn, ada, s, g_pre, g_post, resid):
    shift, scale, gate = ada[:, s, 0, None, :], ada[:, s, 1, None, :], ada[:, s, 2, None, :]
    u = rmsnorm(h, g_pre) * (1 + scale) + shift
    return h + resid * gate * rmsnorm(fn(u), g_post)

def causal_depthwise_conv(x, w, b):
    y = lax.conv_general_dilated(x, w, window_strides=(1,), padding=[(CONV_WIDTH - 1, 0)],
                                 dimension_numbers=('NWC', 'WIO', 'NWC'),
                                 feature_group_count=x.shape[-1])
    return y + b

def masked_softmax(s, mask):
    s = jnp.where(mask, s.astype(jnp.float32), NEG_BIG)
    m = jnp.max(s, axis=-1, keepdims=True)
    e = jnp.where(mask, jnp.exp(s - m), 0.0)
    return e / jnp.maximum(jnp.sum(e, axis=-1, keepdims=True), 1e-30)

def mlstm_chunkwise(q, k, v, ig, logf):
    B, H, S, dh = q.shape
    L = MLSTM_CHUNK
    nc = S // L

    def chunks(t):
        return jnp.moveaxis(t.reshape(t.shape[:2] + (nc, L) + t.shape[3:]), 2, 0)

    causal = jnp.tril(jnp.ones((L, L), dtype=bool))

    def step(carry, xs):
        C, n, m = carry
        qc, kc, vc, ic, fc = xs
        b = jnp.cumsum(fc, axis=-1)
        log_d = jnp.where(causal, b[..., :, None] - b[..., None, :] + ic[..., None, :], -jnp.inf)
        a = b + m[..., None]
        m_t = jnp.maximum(a, jnp.max(log_d, axis=-1))
        s = jnp.einsum('bhtd,bhsd->bhts', qc, kc) * jnp.exp(log_d - m_t[..., None])
        w_inter = jnp.exp(a - m_t)
        num = jnp.einsum('bhts,bhsd->bhtd', s, vc) + w_inter[..., None] * jnp.einsum('bhtd,bhde->bhte', qc, C)
        den = jnp.sum(s, axis=-1) + w_inter * jnp.einsum('bhtd,bhd->bht', qc, n)
        h = num / jnp.maximum(jnp.abs(den), jnp.exp(-m_t))[..., None]
        b_last = b[..., -1]
        g = b_last[..., None] - b + ic
        m_new = jnp.maximum(b_last + m, jnp.max(g, axis=-1))
        decay = jnp.exp(b_last + m - m_new)
        w = jnp.exp(g - m_new[..., None])
        C_new = decay[..., None, None] * C + jnp.einsum('bhs,bhsd,bhse->bhde', w, kc, vc)
        n_new = decay[..., None] * n + jnp.einsum('bhs,bhsd->bhd', w, kc)
        return (C_new, n_new, m_new), h

    init = (jnp.zeros((B, H, dh, dh), jnp.float32), jnp.zeros((B, H, dh), jnp.float32),
            jnp.zeros((B, H), jnp.float32))
    _, hs = lax.scan(step, init, (chunks(q), chunks(k), chunks(v), chunks(ig), chunks(logf)))
    return jnp.moveaxis(hs, 0, 2).reshape(B, H, S, dh)

def mlstm_mixer(q, k, v, o_pre, if_pre, conv_w, conv_b, gate_b, head_gain):
    B, S, _ = q.shape
    qk = jax.nn.silu(causal_depthwise_conv(jnp.concatenate([q, k], axis=-1), conv_w, conv_b))
    q, k = jnp.split(qk, 2, axis=-1)

    def heads(t):
        return t.reshape(B, S, MLSTM_HEADS, MLSTM_HEAD_DIM).transpose(0, 2, 1, 3).astype(jnp.float32)

    gates = (if_pre + gate_b).astype(jnp.float32)
    ig = gates[..., :MLSTM_HEADS].transpose(0, 2, 1)
    logf = jax.nn.log_sigmoid(gates[..., MLSTM_HEADS:]).transpose(0, 2, 1)
    h = mlstm_chunkwise(heads(q), heads(k) * (MLSTM_HEAD_DIM ** -0.5), heads(v), ig, logf)
    h = h.transpose(0, 2, 1, 3)
    h = h * lax.rsqrt(jnp.mean(h * h, axis=-1, keepdims=True) + NORM_EPS)
    h = h.reshape(B, S, MLSTM_WIDTH) * head_gain.astype(jnp.float32)
    return (jax.nn.sigmoid(o_pre.astype(jnp.float32)) * h).astype(q.dtype)

def compress(k, pe, w1, b1, w2, b2):
    B, S, G, dh = k.shape
    r = CMP_BLOCK // CMP_STRIDE
    nch = S // CMP_STRIDE
    ch = k.reshape(B, nch, CMP_STRIDE, G, dh)
    blocks = jnp.concatenate([ch[:, j:nch - r + 1 + j] for j in range(r)], axis=2)
    blocks = blocks + pe[:, None, :]
    n_cmp = blocks.shape[1]
    flat = blocks.transpose(0, 1, 3, 2, 4).reshape(B, n_cmp, G, CMP_BLOCK * dh)
    hid = jax.nn.silu(flat @ w1 + b1)
    return (hid @ w2 + b2).transpose(0, 2, 1, 3)

def nsa_mixer(q, kc, vc, ks, vs, kw, vw, g, cmp_pe, cmp_w1, cmp_b1, cmp_w2, cmp_b2):
    B, S, _ = q.shape
    G, HG, dh, QB = NSA_KV_GROUPS, NSA_HEADS_PER_GROUP, NSA_HEAD_DIM, NSA_QUERY_BLOCK
    qh = q.reshape(B, S, G, HG, dh).transpose(0, 2, 3, 1, 4) * (dh ** -0.5)
    gates = jax.nn.sigmoid(g.astype(jnp.float32)).reshape(B, S, G, HG, 3).transpose(0, 2, 3, 1, 4)

    def kv(t):
        return t.reshape(B, S, G, dh)

    k_cmp = compress(kv(kc), cmp_pe[0], cmp_w1[0], cmp_b1[0], cmp_w2[0], cmp_b2[0])
    v_cmp = compress(kv(vc), cmp_pe[1], cmp_w1[1], cmp_b1[1], cmp_w2[1], cmp_b2[1])
    n_cmp = k_cmp.shape[2]
    cmp_start = jnp.arange(n_cmp) * CMP_STRIDE
    cmp_end = cmp_start + CMP_BLOCK - 1
    n_sel = S // SEL_BLOCK
    n_top = min(N_SELECT, n_sel)
    sel_start = jnp.arange(n_sel) * SEL_BLOCK
    overlap = ((cmp_start[:, None] < sel_start[None, :] + SEL_BLOCK)
               & (cmp_start[:, None] + CMP_BLOCK > sel_start[None, :])).astype(jnp.float32)

    def sel_blocks(t):
        return kv(t).reshape(B, n_sel, SEL_BLOCK, G, dh).transpose(0, 3, 1, 2, 4)

    k_sel, v_sel = sel_blocks(ks), sel_blocks(vs)

    def win_pad(t):
        return jnp.pad(kv(t).transpose(0, 2, 1, 3), ((0, 0), (0, 0), (WINDOW, 0), (0, 0)))

    k_win, v_win = win_pad(kw), win_pad(vw)
    b_idx = jnp.arange(B)[:, None, None, None]
    g_idx = jnp.arange(G)[None, :, None, None]
    sel_offsets = jnp.arange(SEL_BLOCK)
    win_offsets = jnp.arange(WINDOW + QB)
    blk = jnp.arange(n_sel)

    def query_block(qi):
        q0 = qi * QB
        t = q0 + jnp.arange(QB)
        qb = lax.dynamic_slice_in_dim(qh, q0, QB, axis=3)
        gb = lax.dynamic_slice_in_dim(gates, q0, QB, axis=3)
        p_cmp = masked_softmax(jnp.einsum('bghqd,bgnd->bghqn', qb, k_cmp), cmp_end[None, :] <= t[:, None])
        o_cmp = jnp.einsum('bghqn,bgnd->bghqd', p_cmp, v_cmp)
        imp = jnp.einsum('bghqn,nj->bgqj', p_cmp, overlap)
        cur = t // SEL_BLOCK
        forced = (blk[None, :] == 0) | (blk[None, :] == cur[:, None]) | (blk[None, :] == cur[:, None] - 1)
        causal_blk = blk[None, :] * SEL_BLOCK <= t[:, None]
        imp = jnp.where(causal_blk, jnp.where(forced, FORCE_SCORE, imp), -1.0)
        _, idx = lax.top_k(imp, n_top)
        k_g = k_sel[b_idx, g_idx, idx].reshape(B, G, QB, n_top * SEL_BLOCK, dh)
        v_g = v_sel[b_idx, g_idx, idx].reshape(B, G, QB, n_top * SEL_BLOCK, dh)
        pos = (idx[..., None] * SEL_BLOCK + sel_offsets).reshape(B, G, QB, n_top * SEL_BLOCK)
        p_sel = masked_softmax(jnp.einsum('bghqd,bgqnd->bghqn', qb, k_g), (pos <= t[:, None])[:, :, None])
        o_sel = jnp.einsum('bghqn,bgqnd->bghqd', p_sel, v_g)
        k_w = lax.dynamic_slice_in_dim(k_win, q0, WINDOW + QB, axis=2)
        v_w = lax.dynamic_slice_in_dim(v_win, q0, WINDOW + QB, axis=2)
        pos_w = q0 - WINDOW + win_offsets
        mask_w = (pos_w[None, :] >= 0) & (pos_w[None, :] <= t[:, None]) & (pos_w[None, :] > t[:, None] - WINDOW)
        p_w = masked_softmax(jnp.einsum('bghqd,bgnd->bghqn', qb, k_w), mask_w)
        o_w = jnp.einsum('bghqn,bgnd->bghqd', p_w, v_w)
        return gb[..., 0:1] * o_cmp + gb[..., 1:2] * o_sel + gb[..., 2:3] * o_w

    out = lax.map(query_block, jnp.arange(S // QB))
    return out.transpose(1, 0, 4, 2, 3, 5).reshape(B, S, NSA_WIDTH)

def token_mixer(u, w_in, conv_w, conv_b, gate_b, head_gain, cmp_pe, cmp_w1, cmp_b1, cmp_w2, cmp_b2,
                w_up_m, w_up_n, w_out):
    proj = u @ w_in
    offsets = [int(o) for o in np.cumsum(IN_SPLITS)[:-1]]
    (q_m, k_m, v_m, o_m, if_m, q_n, kc, vc, ks, vs, kw, vw, g_n, gate_m, gate_n) = jnp.split(proj, offsets, axis=-1)
    y_m = mlstm_mixer(q_m, k_m, v_m, o_m, if_m, conv_w, conv_b, gate_b, head_gain) @ w_up_m
    y_n = nsa_mixer(q_n, kc, vc, ks, vs, kw, vw, g_n, cmp_pe, cmp_w1, cmp_b1, cmp_w2, cmp_b2).astype(u.dtype) @ w_up_n
    merged = jax.nn.sigmoid(gate_m) * y_m + jax.nn.sigmoid(gate_n) * y_n
    return merged @ w_out

def setup_inputs(seed: int = 0) -> dict:
    key = jax.random.key(seed)
    ks = jax.random.split(key, 24)

    def nrm(k, shape, scale):
        return jax.random.normal(k, shape, jnp.float32) * scale

    L, D, F = DEPTH, D_MODEL, D_FF
    gate_b = jnp.concatenate([nrm(ks[10], (L, MLSTM_HEADS), 0.1),
                              jnp.linspace(3.0, 6.0, MLSTM_HEADS)[None, :] + nrm(ks[11], (L, MLSTM_HEADS), 0.1)], axis=-1)
    return {
        "x": nrm(ks[0], (BATCH, SEQ, D), 1.0),
        "c": nrm(ks[1], (BATCH, D), 1.0),
        "w_ada": nrm(ks[2], (L, D, 9 * D), D ** -0.5),
        "b_ada": nrm(ks[3], (L, 9 * D), 0.02),
        "norm_gains": 1.0 + nrm(ks[4], (L, 6, D), 0.05),
        "ffn_wg": nrm(ks[5], (L, 2, D, F), D ** -0.5),
        "ffn_wu": nrm(ks[6], (L, 2, D, F), D ** -0.5),
        "ffn_wd": nrm(ks[7], (L, 2, F, D), F ** -0.5),
        "w_in": nrm(ks[8], (L, D, D_IN), D ** -0.5),
        "mlstm_conv_w": nrm(ks[9], (L, CONV_WIDTH, 1, 2 * MLSTM_WIDTH), CONV_WIDTH ** -0.5),
        "mlstm_conv_b": nrm(ks[12], (L, 2 * MLSTM_WIDTH), 0.02),
        "mlstm_gate_b": gate_b,
        "mlstm_head_gain": 1.0 + nrm(ks[13], (L, MLSTM_WIDTH), 0.05),
        "cmp_pe": nrm(ks[14], (L, 2, CMP_BLOCK, NSA_HEAD_DIM), 0.1),
        "cmp_w1": nrm(ks[15], (L, 2, CMP_BLOCK * NSA_HEAD_DIM, CMP_HIDDEN), (CMP_BLOCK * NSA_HEAD_DIM) ** -0.5),
        "cmp_b1": nrm(ks[16], (L, 2, CMP_HIDDEN), 0.02),
        "cmp_w2": nrm(ks[17], (L, 2, CMP_HIDDEN, NSA_HEAD_DIM), CMP_HIDDEN ** -0.5),
        "cmp_b2": nrm(ks[18], (L, 2, NSA_HEAD_DIM), 0.02),
        "w_up_mlstm": nrm(ks[19], (L, MLSTM_WIDTH, D), MLSTM_WIDTH ** -0.5),
        "w_up_nsa": nrm(ks[20], (L, NSA_WIDTH, D), NSA_WIDTH ** -0.5),
        "w_out": nrm(ks[21], (L, D, D), D ** -0.5),
    }

def reference(x, c, w_ada, b_ada, norm_gains, ffn_wg, ffn_wu, ffn_wd, w_in, mlstm_conv_w, mlstm_conv_b,
              mlstm_gate_b, mlstm_head_gain, cmp_pe, cmp_w1, cmp_b1, cmp_w2, cmp_b2, w_up_mlstm, w_up_nsa, w_out):
    B = x.shape[0]
    h = x
    for l in range(DEPTH):
        ada = (jax.nn.silu(c) @ w_ada[l] + b_ada[l]).reshape(B, 3, 3, D_MODEL)
        h = sandwich(h, lambda u: swiglu(u, ffn_wg[l, 0], ffn_wu[l, 0], ffn_wd[l, 0]), ada, 0,
                     norm_gains[l, 0], norm_gains[l, 1], MACARON_WEIGHT)
        h = sandwich(h, lambda u: token_mixer(u, w_in[l], mlstm_conv_w[l], mlstm_conv_b[l], mlstm_gate_b[l],
                                               mlstm_head_gain[l], cmp_pe[l], cmp_w1[l], cmp_b1[l], cmp_w2[l],
                                               cmp_b2[l], w_up_mlstm[l], w_up_nsa[l], w_out[l]),
                     ada, 1, norm_gains[l, 2], norm_gains[l, 3], 1.0)
        h = sandwich(h, lambda u: swiglu(u, ffn_wg[l, 1], ffn_wu[l, 1], ffn_wd[l, 1]), ada, 2,
                     norm_gains[l, 4], norm_gains[l, 5], MACARON_WEIGHT)
    return h.astype(x.dtype)


_drawn_inputs = setup_inputs


def setup_inputs(seed=0):
    import zlib

    import numpy as np

    out = dict(_drawn_inputs(seed))
    spreads = {}
    factors = {'mlstm_conv_b': 8.0,
     'mlstm_head_gain': 3.198,
     'cmp_pe': 3.454,
     'cmp_b1': 30.289,
     'cmp_b2': 8.0}
    for name, (base, spread) in spreads.items():
        noise = np.random.default_rng([zlib.crc32(name.encode()), seed]).standard_normal(out[name].shape)
        drawn = base * np.exp(spread * noise) if base else spread * noise
        out[name] = jnp.asarray(drawn.astype(out[name].dtype))
    for name, factor in factors.items():
        out[name] = (out[name] * factor).astype(out[name].dtype)
    return out
```

```python
import concourse.bass as bass
from concourse import mybir
from contextlib import ExitStack

F32 = mybir.dt.float32
F32R = mybir.dt.float32r
BF16 = mybir.dt.bfloat16
ALU = mybir.AluOpType
ACT = mybir.ActivationFunctionType
AX = mybir.AxisListType

P = 128
T = 512
TT = T // P
D = 1024
DC = D // P
FF = 2816
FC = FF // P
COLS = 256
UP_ITERS = FF // COLS
DOWN_UNITS = 3
DOWN_K = (0, 8, 16, FC)
EPS_SUM = 1e-6 * D
ROOT_D = float(D) ** 0.5
NEG = -1.0e30
ADA_FIRST = 8

MH, MD = 4, 128
NH, ND, NG, HG = 8, 64, 2, 4
NCMP = 31
CB = 32
WINDOW = 256
GATE_N = 3 * NH
OFF_Q, OFF_K, OFF_V, OFF_O, OFF_IF = 0, 512, 1024, 1536, 2048
OFF_QN = 2056
OFF_KC, OFF_VC, OFF_KS, OFF_VS, OFF_KW, OFF_VW = (2568 + 128 * j for j in range(6))
OFF_GN, OFF_GA, OFF_GB = 3336, 3360, 4384


class Count:

    def __init__(self, sem):
        self.sem, self.n, self.off, self.mark = sem, 0, 0, 0

    def tick(self, ins):
        ins.then_inc(self.sem, 1)
        self.n += 1
        return self.n

    def wait(self, eng, n=None):
        eng.wait_ge(self.sem, (self.n if n is None else n) + self.off)

    def begin(self, i, stride):
        self.mark, self.off, self.stride = self.n, i * stride, stride

    def end(self, iters):
        assert self.n - self.mark == self.stride, (self.n, self.mark)
        self.n, self.off = self.mark + self.stride * iters, 0


class Plan:

    def __init__(self):
        self.bank_count = [0] * 8
        self.jobs = {}
        self.landed_count = [0, 0]
        self.raw_count = 0
        self.raws = {}
        self.weight_count = 0
        self.weights = {}

    def job(self, name, bank):
        assert name not in self.jobs, name
        self.jobs[name] = (bank, self.bank_count[bank], 0)
        self.bank_count[bank] += 1

    def loop_jobs(self, iters, body):
        before = list(self.bank_count)
        for name, bank in body:
            self.job(name, bank)
        step = [a - b for a, b in zip(self.bank_count, before)]
        for name, bank in body:
            self.jobs[name] = self.jobs[name][:2] + (step[bank],)
        self.bank_count = [b + s * iters for b, s in zip(before, step)]

    def unit(self, name, dmas=1):
        slot = self.raw_count % 2
        self.landed_count[slot] += 16 * dmas
        self.raws[name] = (slot, self.landed_count[slot], 0)
        self.raw_count += 1
        if name[0] != "ada":
            self.weights[name] = (self.weight_count, 0)
            self.weight_count += 1

    def loop_units(self, iters, body):
        before, w0, r0 = list(self.landed_count), self.weight_count, self.raw_count
        for name in body:
            self.unit(name)
        step = [a - b for a, b in zip(self.landed_count, before)]
        wstep = self.weight_count - w0
        assert (self.raw_count - r0) % 2 == 0 and wstep % 2 == 0
        for name in body:
            slot, value, _ = self.raws[name]
            self.raws[name] = (slot, value, step[slot])
            if name in self.weights:
                self.weights[name] = (self.weights[name][0], wstep)
        self.landed_count = [b + s * iters for b, s in zip(before, step)]
        self.weight_count = w0 + wstep * iters
        self.raw_count = r0 + (self.raw_count - r0) * iters


def build_layer(nc, x, c, w_ada, b_ada, norm_gains, ffn_wg, ffn_wu, ffn_wd, w_in, mlstm_conv_w, mlstm_conv_b,
                mlstm_gate_b, mlstm_head_gain, cmp_pe, cmp_w1, cmp_b1, cmp_w2, cmp_b2, w_up_mlstm, w_up_nsa,
                w_out, out):
    with ExitStack() as ctx:
        base = nc.sbuf_base + (-nc.sbuf_base) % 32
        at = [base]

        def sem(name):
            return ctx.enter_context(nc.semaphore(name))

        def place(name, shape, dt, offset=None):
            size = mybir.dt.size(dt)
            for n in shape[1:]:
                size *= n
            size += -size % 32
            if offset is None:
                offset = at[0]
                at[0] += size
            return nc.alloc_sbuf_tensor_at(name, shape, dt, offset=offset), offset + size

        h, _ = place("h", [P, DC, T], F32)
        u_at = at[0]
        u_hi, _ = place("u_hi", [P, DC, T], F32R)
        u_lo_at = at[0]
        u_lo, _ = place("u_lo", [P, DC, T], F32R)
        raw = [place(f"raw{s}", [P, DC * COLS], F32)[0] for s in range(2)]
        w_hi = [place(f"w_hi{s}", [P, DC * COLS], F32R)[0] for s in range(2)]
        w_lo = [place(f"w_lo{s}", [P, DC * COLS], F32R)[0] for s in range(2)]
        ident, _ = place("ident", [P, P], F32)
        ones, _ = place("ones", [P, P], F32)
        col1, _ = place("col1", [P, 120], F32)
        col2, _ = place("col2", [P, 81], F32)
        ada, _ = place("ada", [P, 9 * DC], F32)
        eps_col, _ = place("eps_col", [P, 1], F32)
        silu_c, _ = place("silu_c", [P, DC], F32)
        gain_a, _ = place("gain_a", [P, DC], F32)
        gain_g, _ = place("gain_g", [P, DC], F32)
        sq_at = at[0]
        sq = [place(f"sq{s}", [P, T], F32)[0] for s in range(2)]
        wt_at = at[0]
        wt = [place(f"wt{s}", [P, T], F32)[0] for s in range(2)]
        rs_at = at[0]
        rs, _ = place("rs", [P, T], F32)
        region = at[0]

        mid_hi, e = place("mid_hi", [P, FC, T], F32R, region)
        mid_lo, e = place("mid_lo", [P, FC, T], F32R, e)
        ada_acc, e = place("ada_acc", [P, COLS], F32, e)
        ffn_end = e
        y_ffn, _ = place("y_ffn", [P, DC, T], F32, u_lo_at)
        ada_w, e = place("ada_w", [P, DC, ADA_FIRST * COLS], F32, region)
        x_tok, e = place("x_tok", [P, TT, D], F32, e)
        ada_acc0, e = place("ada_acc0", [P, ADA_FIRST * COLS], F32, e)
        c_col, e = place("c_col", [P, DC], F32, e)
        rows1, e = place("rows1", [120, P], F32, e)
        rows2, e = place("rows2", [81, P], F32, e)
        first_end = e
        out_tok, _ = place("out_tok", [P, TT, D], F32, region)

        qkc, e = place("qkc", [P, 2 * MH, T], F32, region)
        sig_o, e = place("sig_o", [P, MH, T], F32, e)
        v_aug, e = place("v_aug", [P, TT, MH, MD + 1], F32, e)
        p_m, e = place("p_m", [P, TT, T], F32, e)
        o_acc, a = place("o_acc", [P, TT, NH * ND], F32, region)
        p_s, a = zip(*[place(f"p_s{n}", [P, T], F32, a + 2048 * n) for n in range(2)])
        p_w, a = zip(*[place(f"p_w{n}", [P, 384], F32, a[1] + 1536 * n) for n in range(2)])
        pt_s, a = zip(*[place(f"pt_s{n}", [P, T], F32, a[1] + 2048 * n) for n in range(2)])
        pt_w, a = zip(*[place(f"pt_w{n}", [P, 384], F32, a[1] + 1536 * n) for n in range(2)])
        o_hi, a = place("o_hi", [P, 4, T], F32R, a[1])
        o_lo, a = place("o_lo", [P, 4, T], F32R, a)
        assert a <= e
        hm_hi, a = place("hm_hi", [P, MH, T], F32R, region)
        hm_lo, a = place("hm_lo", [P, MH, T], F32R, a)
        hm, e = place("hm", [P, MH, T], F32, e)
        qn_at = e
        qn, e = place("qn", [P, 4, T], F32, e)
        ksw, e = place("ksw", [P, 2, T], F32, e)
        vsw, e = place("vsw", [P, TT, 2, P], F32, e)
        sig_b, a = place("sig_b", [P, DC, T], F32, qn_at)
        assert a <= e
        sig_a_at = e
        sig_a, e = place("sig_a", [P, DC, T], F32, e)
        y_mix, _ = place("y_mix", [P, DC, T], F32, sig_a_at)
        late_at = e
        kv_2, a = place("kv_2", [P, 2, NG, T // 2], F32, sig_a_at)
        blk, a = place("blk", [P, 16, NG, 32], F32, a)
        blk_hi, a = place("blk_hi", [P, 16, NG, 32], F32R, a)
        kv_t, _ = place("kv_t", [P, 2, 2, T // 2], F32, a)
        blk_lo, a = place("blk_lo", [P, 16, NG, 32], F32R, a)
        assert a <= late_at
        row_i, a = place("row_i", [MH, T], F32, late_at)
        row_f, a = place("row_f", [MH, T], F32, a)
        row_t, a = place("row_t", [MH, T], F32, a)
        row_z, a = place("row_z", [MH, T], F32, a)
        row_s, late = place("row_s", [MH, T], F32, a)
        row_m, _ = place("row_m", [MH, T], F32, rs_at)
        v_bd, a = place("v_bd", [P, NG, HG, ND], F32, late_at)
        p_c, a = place("p_c", [P, NH, 32], F32, a)
        pt_c, a = place("pt_c", [P, NG, P], F32, a)
        hid_rep, a = place("hid_rep", [P, 2, NG, HG, 32], F32, a)
        o_tmp, a = place("o_tmp", [P, HG, 2, ND], F32, a)
        v_tmp, a = place("v_tmp", [P, NG, ND], F32, a)
        hid, a = place("hid", [P, 2, 2, 64], F32, a)
        assert a <= late
        w2, late = place("w2", [P, 2, 2, ND], F32, late)
        k_cmp, late = place("k_cmp", [P, 32], F32, late)
        b2_row, late = place("b2_row", [P, ND], F32, late)
        mask_row, late = place("mask_row", [P, T], F32, late)
        add_c, late = place("add_c", [P, TT, 32], F32, late)
        keep_c, late = place("keep_c", [P, TT, 32], F32, late)
        bd, late = place("bd", [P, HG], F32, late)
        ident_b, late = place("ident_b", [P, P], BF16, late)
        diag_b, late = place("diag_b", [P, P], BF16, late)
        left_b, late = place("left_b", [P, P], BF16, late)
        pick, late = place("pick", [MH, MH, P], F32, late)
        g_bias, late = place("g_bias", [MH, 2], F32, late)
        g_tok, late = place("g_tok", [P, TT, 32], F32, late)
        sig_n, late = place("sig_n", [P, TT, NH, 3], F32, late)
        cols, late = place("cols", [P, 2, TT, MH], F32, late)
        den, late = place("den", [P, MH, TT], F32, late)
        ssm, late = place("ssm", [P, MH, TT], F32, late)
        max_c, late = place("max_c", [P, NH], F32, late)
        sum_c, late = place("sum_c", [P, NH], F32, late)
        n_max, late = place("n_max", [P, 32, 2], F32, late)
        sums, late = place("sums", [P, 32, 2], F32, late)
        w_sw, late = place("w_sw", [P, HG, 2], F32, late)
        eps_m, late = place("eps_m", [P, 1], F32, late)

        PS = ctx.enter_context(nc.psum_tensor("PS", [P, 8, 512], F32))

        bank_full = [sem(f"bank_full{b}") for b in range(8)]
        bank_free = [sem(f"bank_free{b}") for b in range(8)]
        raw_landed = [sem(f"raw_landed{s}") for s in range(2)]
        hi_ready = sem("hi_ready")
        lo_ready = sem("lo_ready")
        w_used = sem("w_used")
        ada_summed = sem("ada_summed")
        consts_ready = sem("consts_ready")
        rows_landed = sem("rows_landed")
        c_landed = sem("c_landed")
        x_landed = sem("x_landed")
        ada_first_landed = [sem(f"ada_first_landed{j}") for j in range(DC)]
        silu_c_ready = sem("silu_c_ready")
        h_ready = sem("h_ready")
        sq_ready = sem("sq_ready")
        sq_used = sem("sq_used")
        w_scaled = sem("w_scaled")
        u_hi_ready = sem("u_hi_ready")
        u_ready = sem("u_ready")
        mid_hi_ready = sem("mid_hi_ready")
        mid_ready = sem("mid_ready")
        ysum_ready = sem("ysum_ready")
        ysum_used = sem("ysum_used")
        delta_ready = sem("delta_ready")
        stored = sem("stored")
        small_landed = sem("small_landed")
        mixer_consts = sem("mixer_consts")
        soft_ready = sem("soft_ready")
        conv_first = sem("conv_first")
        qk_ready = sem("qk_ready")
        m_ready = sem("m_ready")
        em_ready = sem("em_ready")
        arg_ready = sem("arg_ready")
        e_ready = sem("e_ready")
        kv_moved = sem("kv_moved")
        ssm_ready = sem("ssm_ready")
        ssm_root = sem("ssm_root")
        blk_ready = sem("blk_ready")
        blk_hi_ready = sem("blk_hi_ready")
        blk_lo_ready = sem("blk_lo_ready")
        hm_normed = sem("hm_normed")
        hid_rep_ready = sem("hid_rep_ready")
        v_bd_ready = sem("v_bd_ready")
        arg_c_ready = sem("arg_c_ready")
        e_c_ready = sem("e_c_ready")
        p_c_ready = sem("p_c_ready")
        sig_n_ready = sem("sig_n_ready")
        n_max_ready = sem("n_max_ready")
        o_hi_ready = sem("o_hi_ready")
        o_acc_ready = sem("o_acc_ready")
        hm_lo_ready = sem("hm_lo_ready")
        merged = sem("merged")
        dve_step = sem("dve_step")
        act_step = sem("act_step")
        pool_step = sem("pool_step")

        plan = Plan()
        plan.job(("cols", 1), 0)
        plan.job(("cols", 2), 1)
        for cch in range(DC):
            plan.job(("x", cch), 2 + cch % 4)
        plan.job(("ada0",), 7)
        plan.job(("pre", 0), 6)

        def plan_ffn_up(f):
            has_ada = f == 0
            plan.unit(("g0", f))
            plan.loop_units(UP_ITERS, [("up", f), ("ada", "a"), ("gate", f), ("ada", "b")] if has_ada
                            else [("up", f), ("gate", f)])
            plan.loop_jobs(UP_ITERS, [(("g", f, 0), 0), (("g", f, 1), 1), (("u", f, 0), 2), (("u", f, 1), 3)]
                           + ([(("ada", "a"), 7), (("ada", "b"), 7)] if has_ada else []))

        def plan_ffn_down(f, following):
            for it in range(2):
                for n in range(6):
                    if (it, n) != (0, 0):
                        plan.unit(("d", f, it, n))
                    if f == 0 and n in (2, 5):
                        plan.unit(("ada", it, n))
            for name, dmas in following:
                plan.unit(name, dmas)
            plan.loop_jobs(2, [(("y", f, n), n) for n in range(4)]
                           + ([(("ada", 2), 7), (("ada", 5), 7)] if f == 0 else []))

        unit_end = {}

        def plan_unit(name, dmas, jobs, ends=True):
            plan.unit(name, dmas)
            for job, bank in jobs:
                plan.job(job, bank)
            unit_end[name] = jobs[-1][0] if ends else None

        MIX = ([("t0",), ("t1",), ("v", 0), ("v", 1)] + [("qk", n) for n in range(4)] + [("o", 0), ("o", 1), ("kcvc",), ("kk",),
               ("qn", 0), ("qn", 1)] + [("c1", kv, a) for kv in range(2) for a in range(2)] + [("ga", n) for n in range(4)]
               + [("gb", n) for n in range(4)] + [("um", 0), ("un", 0), ("um", 1), ("un", 1)] + [("wo", n) for n in range(4)])
        STEPS = [(t, g, hh) for t in range(TT) for g in range(NG) for hh in range(HG)]
        FILL = len(STEPS) // 8

        def plan_head(hd):
            plan.job(("negM", hd), 4)
            for j in range(TT):
                plan.job(("S", hd, j), j)

        def plan_mixer():
            plan_unit(("t0",), 3, [(("t0", 0), 0), (("t0", 1), 1)])
            plan_unit(("t1",), 1, [(("t1",), 2)])
            plan_unit(("v", 0), 1, [(("v", 0, 0), 3), (("v", 0, 1), 4)])
            plan_unit(("v", 1), 1, [(("v", 1, 0), 5), (("v", 1, 1), 6)])
            plan.job(("ifT", 0), 0)
            plan.job(("ifT", 1), 1)
            for n in range(4):
                plan_unit(("qk", n), 1, [(("qk", 2 * n), 2 + 2 * n % 4), (("qk", 2 * n + 1), 2 + (2 * n + 1) % 4)])
            plan.job(("colT",), 0)
            for n in range(2):
                if n:
                    for a in range(2):
                        plan.unit(("ada", "m", a))
                        plan.job(("ada", "m", a), 7)
                plan_unit(("o", n), 1, [(("o", 2 * n), 1 + 2 * n), (("o", 2 * n + 1), 2 + 2 * n)])
            plan_head(0)
            for hd, (name, dmas) in enumerate([(("kcvc",), 1), (("kk",), 2), (("qn", 0), 4), (("qn", 1), 4)]):
                plan_unit(name, dmas, [(name + ("a",), 4), (name + ("b",), 7)])
                plan.job(("num", hd, 0), 5)
                plan.job(("num", hd, 1), 6)
                if hd < MH - 1:
                    plan_head(hd + 1)
            for kv in range(2):
                plan_unit(("c1", kv, 0), 1, [(("hid", kv, 0), 2 * kv), (("hid", kv, 1), 2 * kv + 1)], ends=False)
                if kv == 0:
                    for hd in range(MH):
                        plan.job(("hT", hd), 4 + hd)
                plan.unit(("c1", kv, 1))
                unit_end[("c1", kv, 1)] = ("hid", kv, 1)
            plan.job(("kcmp",), 4)
            plan.job(("vcmp",), 5)
            for t in range(TT):
                plan.job(("sc", t, 0), 2 * (t % 2))
                plan.job(("sc", t, 1), 2 * (t % 2) + 1)
                plan.job(("pcT", t), 4 + t % 2)
                plan.job(("oc", t), 6)
            for s, (t, g, hh) in enumerate(STEPS):
                plan.job(("ss", s), 2 * (s % 2))
                plan.job(("sw", s), 2 * (s % 2) + 1)
                plan.job(("ts", s), 4)
                plan.job(("tw", s), 5)
                if hh == 0:
                    plan.job(("o_nsa", t, g), 6)
            for n in range(4):
                plan_unit(("ga", n), 1, [(("ga", 2 * n), 7), (("ga", 2 * n + 1), 7)])
            for n in range(4):
                plan_unit(("gb", n), 1, [(("gb", 2 * n), 2 * (n % 2)), (("gb", 2 * n + 1), 2 * (n % 2) + 1)])
            for fc in range(4):
                plan.job(("oT", fc), 4 + fc)
            for j in range(2):
                plan_unit(("um", j), 1, [(("ym", 4 * j + n), n) for n in range(4)])
                plan_unit(("un", j), 1, [(("yn", 4 * j + n), 4 + n) for n in range(4)])
            for n in range(4):
                plan_unit(("wo", n), 1, [(("y1", 2 * n), 2 * (n % 2)), (("y1", 2 * n + 1), 2 * (n % 2) + 1)])
            plan.job(("post", 1), 6)

        plan_ffn_up(0)
        plan_ffn_down(0, [])
        plan.job(("post", 0), 6)
        plan.job(("pre", 1), 6)
        plan_mixer()
        plan.job(("pre", 2), 6)
        plan_ffn_up(1)
        plan_ffn_down(1, [])
        plan.job(("post", 2), 6)
        for cch in range(DC):
            plan.job(("out", cch), 2 + cch % 4)
        assert [n for n in plan.weights if n in MIX] == MIX

        def after(name):
            n = MIX.index(name) + 1
            return MIX[n] if n < len(MIX) else ("g0", 1)

        def blocks_of(t):
            return range(0, t + 1), range(max(0, t - WINDOW // P), t + 1)

        def job_start(eng, name, i=0):
            bank, k, step = plan.jobs[name]
            eng.wait_ge(bank_free[bank], k + 1 + i * step)
            return PS[:, bank, :]

        def job_end(ins, name):
            ins.then_inc(bank_full[plan.jobs[name][0]], 1)

        def job_result(eng, name, i=0):
            bank, k, step = plan.jobs[name]
            eng.wait_ge(bank_full[bank], k + 1 + i * step)
            return PS[:, bank, :]

        def job_read(ins, name):
            ins.then_inc(bank_free[plan.jobs[name][0]], 1)

        job_done = job_result
        mixer_used = 2

        def taken(eng, name, i=0, before=0):
            bank, k, step = plan.jobs[name]
            eng.wait_ge(bank_free[bank], k + 2 - before + i * step)

        def unit_landed(eng, name, i=0):
            slot, value, step = plan.raws[name]
            eng.wait_ge(raw_landed[slot], value + i * step)
            return raw[slot]

        def w_number(name, i=0):
            n, step = plan.weights[name]
            return n + 1 + i * step, n % 2

        def chunk(t, j):
            return t[:, j * P:(j + 1) * P]

        block = ctx.enter_context(nc.Block())

        dve_misc = sem("dve_misc")
        @block.sync
        def _(sp):
            sp.dma_start(c_col[:], c.rearrange("b (p j) -> p (b j)", j=DC)).then_inc(c_landed, 16)
            ada_rows = w_ada[0].rearrange("(p j) n -> p j n", j=DC)
            for j in range(DC):
                sp.dma_start(ada_w[:, j, :], ada_rows[:, j, 0:ADA_FIRST * COLS]).then_inc(ada_first_landed[j], 16)
                if j == 0:
                    sp.dma_start(rows1[0:72, :], b_ada.rearrange("l (r n) -> (l r) n", n=P)).then_inc(rows_landed, 16)
                    sp.dma_start(rows1[72:120, :], norm_gains.rearrange("l g (r n) -> (l g r) n", n=P)).then_inc(rows_landed, 16)
                    sp.dma_start(rows2[0:32, :], mlstm_conv_w.rearrange("l w o (r n) -> (l w o r) n", n=P)).then_inc(rows_landed, 16)
                    sp.dma_start(rows2[32:40, :], mlstm_conv_b.rearrange("l (r n) -> (l r) n", n=P)).then_inc(rows_landed, 16)
                    sp.dma_start(rows2[40:44, :], mlstm_head_gain.rearrange("l (r n) -> (l r) n", n=P)).then_inc(rows_landed, 16)
                    sp.dma_start(rows2[44:48, :], cmp_b1.rearrange("l k (r n) -> (l k r) n", n=P)).then_inc(rows_landed, 16)
                    sp.dma_start(rows2[48:80, :], cmp_pe.rearrange("l k (r a) n -> (l k r) (a n)", a=2)).then_inc(rows_landed, 16)
                    sp.dma_start(rows2[80:81, 0:ND], cmp_b2[:, 0, :]).then_inc(rows_landed, 16)
                    sp.dma_start(rows2[80:81, ND:P], cmp_b2[:, 0, :]).then_inc(rows_landed, 16)
            sp.dma_start(x_tok[:], x[0].rearrange("(t p) d -> p t d", p=P)).then_inc(x_landed, 16)

            last = {0: None, 1: None}

            def slot_empty(name):
                slot = plan.raws[name][0]
                if last[slot] is not None:
                    sp.wait_ge(*last[slot])
                return slot

            def load(name, pieces):
                slot = slot_empty(name)
                for dst, src in pieces:
                    sp.dma_start(raw[slot][:, dst[0]:dst[1]].rearrange("p (k n) -> p k n", n=dst[2]), src).then_inc(raw_landed[slot], 16)
                if name[0] == "ada":
                    ada_seen[0] += 1
                    last[slot] = (ada_summed, ada_seen[0])
                else:
                    last[slot] = (lo_ready, w_number(name)[0])

            ada_seen = [1]

            def rows_of(w, r0, r1, c0, cn):
                return w[r0 * P:r1 * P, bass.ds(c0, cn)].rearrange("(k p) n -> p k n", p=P)

            def dense(kn, n):
                return (0, kn * n, n)

            def ada_src(a):
                return ada_rows[:, :, bass.ds(a * COLS, COLS)]

            def load_ffn_up(f):
                load(("g0", f), [(dense(DC, COLS), rows_of(ffn_wg[0, f], 0, DC, 0, COLS))])
                wslot = plan.raws[("up", f)][0]
                gslot = plan.raws[("gate", f)][0]
                g_n = w_number(("g0", f))[0]

                def raw3(slot):
                    return raw[slot][:].rearrange("p (k n) -> p k n", n=COLS)

                def iteration(i, last_one):
                    sp.wait_ge(lo_ready, g_n + 2 * i - f)
                    sp.dma_start(raw3(wslot), rows_of(ffn_wu[0, f], 0, DC, i * COLS, COLS)).then_inc(raw_landed[wslot], 16)
                    if f == 0:
                        aslot = plan.raws[("ada", "a")][0]
                        sp.wait_ge(ada_summed, 2 * i + 1)
                        sp.dma_start(raw3(aslot), ada_src(ADA_FIRST + 2 * i)).then_inc(raw_landed[aslot], 16)
                        sp.wait_ge(lo_ready, g_n + 1 + 2 * i)
                    else:
                        sp.wait_ge(lo_ready, g_n + 2 * i)
                    src = rows_of(ffn_wd[0, f], DOWN_K[0], DOWN_K[1], 0, COLS) if last_one else \
                        rows_of(ffn_wg[0, f], 0, DC, i * COLS + COLS, COLS)
                    sp.dma_start(raw3(gslot), src).then_inc(raw_landed[gslot], 16)
                    if f == 0:
                        sp.wait_ge(ada_summed, 2 * i + 2)
                        sp.dma_start(raw3(aslot), ada_src(ADA_FIRST + 1 + 2 * i)).then_inc(raw_landed[aslot], 16)

                with sp.Fori(0, UP_ITERS - 1) as i:
                    iteration(i, False)
                iteration(UP_ITERS - 1, True)
                n_last = g_n + 2 * UP_ITERS
                if f == 0:
                    ada_seen[0] = 1 + 2 * UP_ITERS
                    last[gslot] = (lo_ready, n_last)
                    last[1 - gslot] = (ada_summed, ada_seen[0])
                else:
                    last[gslot] = (lo_ready, n_last)
                    last[1 - gslot] = (lo_ready, n_last - 1)

            def load_ffn_down(f):
                for it in range(2):
                    for n in range(6):
                        if (it, n) != (0, 0):
                            k0, k1 = DOWN_K[n % 3], DOWN_K[n % 3 + 1]
                            c0 = (2 * it + n // 3) * COLS
                            load(("d", f, it, n), [(dense(k1 - k0, COLS), rows_of(ffn_wd[0, f], k0, k1, c0, COLS))])
                        if f == 0 and n in (2, 5):
                            load(("ada", it, n), [(dense(DC, COLS), ada_src(ADA_FIRST + 2 * UP_ITERS + 2 * it + n // 3))])

            def load_mixer():
                w3 = w_in[0].rearrange("(k p) n -> p k n", p=P)

                def columns(c0, cn):
                    return w3[:, :, c0:c0 + cn]

                def load_parts(name, n, parts):
                    slot = slot_empty(name)
                    for view, src in parts(raw[slot]):
                        sp.dma_start(view, src).then_inc(raw_landed[slot], 16)
                    last[slot] = (lo_ready, w_number(name)[0])

                def t0_parts(slot):
                    s3 = slot[:, 0:DC * 160].rearrange("p (k n) -> p k n", n=160)
                    return [(s3[:, :, 0:8], columns(OFF_IF, 8)), (s3[:, :, 8:32], columns(OFF_GN, GATE_N)),
                            (s3[:, :, 32:160], columns(OFF_VS, P))]

                def kk_parts(slot):
                    s3 = slot[:].rearrange("p (k n) -> p k n", n=COLS)
                    return [(s3[:, :, 0:P], columns(OFF_KS, P)), (s3[:, :, P:COLS], columns(OFF_KW, P))]

                def qn_parts(n):
                    def parts(slot):
                        s3 = slot[:].rearrange("p (k n) -> p k n", n=COLS)
                        return [(s3[:, :, (2 * cc + g) * ND:(2 * cc + g + 1) * ND],
                                 columns(OFF_QN + (g * HG + 2 * n + cc) * ND, ND)) for cc in range(2) for g in range(NG)]
                    return parts

                load_parts(("t0",), 160, t0_parts)
                load(("t1",), [(dense(DC, P), columns(OFF_VW, P))])
                job_done(sp, ("y", 0, 3), 1)
                for kv in range(2):
                    sp.dma_start(w2[:, kv, :, :], cmp_w2[0, kv].rearrange("(h p) e -> p h e", p=P)).then_inc(small_landed, 16)
                sp.dma_start(b2_row[:], cmp_b2[0, 1:2, :].broadcast_to([P, ND])).then_inc(small_landed, 16)
                for a in range(2):
                    sp.dma_start(g_bias[:, a:a + 1], mlstm_gate_b[0, a * MH:(a + 1) * MH].rearrange("(p o) -> p o", o=1)).then_inc(small_landed, 16)
                for n in range(2):
                    load(("v", n), [(dense(DC, COLS), columns(OFF_V + n * COLS, COLS))])
                for n in range(4):
                    load(("qk", n), [(dense(DC, COLS), columns(OFF_Q + n * COLS, COLS))])
                for n in range(2):
                    if n:
                        for a in range(2):
                            load(("ada", "m", a), [(dense(DC, COLS), ada_src(34 + a))])
                    load(("o", n), [(dense(DC, COLS), columns(OFF_O + n * COLS, COLS))])
                load(("kcvc",), [(dense(DC, COLS), columns(OFF_KC, COLS))])
                load_parts(("kk",), COLS, kk_parts)
                for n in range(2):
                    load_parts(("qn", n), COLS, qn_parts(n))
                for kv in range(2):
                    for a in range(2):
                        load(("c1", kv, a), [(dense(DC, COLS), rows_of(cmp_w1[0, kv], a * DC, (a + 1) * DC, 0, COLS))])
                for n in range(4):
                    load(("ga", n), [(dense(DC, COLS), columns(OFF_GA + n * COLS, COLS))])
                for n in range(4):
                    load(("gb", n), [(dense(DC, COLS), columns(OFF_GB + n * COLS, COLS))])
                for j in range(2):
                    load(("um", j), [(dense(4, T), rows_of(w_up_mlstm[0], 0, 4, j * T, T))])
                    load(("un", j), [(dense(4, T), rows_of(w_up_nsa[0], 0, 4, j * T, T))])
                for n in range(4):
                    load(("wo", n), [(dense(DC, COLS), rows_of(w_out[0], 0, DC, n * COLS, COLS))])

            load_ffn_up(0)
            load_ffn_down(0)
            load_mixer()
            load_ffn_up(1)
            load_ffn_down(1)
            for cch in range(DC):
                taken(sp, ("out", cch))
            for t in range(TT):
                sp.dma_start(out[0, t * P:(t + 1) * P, :], out_tok[:, t, :]).then_inc(stored, 16)
            sp.wait_ge(stored, 16 * TT)

        @block.gpsimd
        def _(pool):
            step = Count(pool_step)
            step.tick(pool.memset(ident[:], 0.0))
            step.tick(pool.memset(ones[:], 1.0))
            step.tick(pool.memset(eps_col[:], EPS_SUM))
            step.wait(pool)
            for b in range(8):
                pool.sem_inc(bank_free[b], 1)
            pool.affine_select(out=ident[:], in_=ident[:], compare_op=ALU.not_equal, fill=1.0, base=0,
                               pattern=[[-1, P]], channel_multiplier=1).then_inc(consts_ready, 1)

            def sum_y_squares(sums, y_job):
                for cch in range(DC):
                    n = sums * DC + cch + 1
                    taken(pool, *y_job(cch))
                    if cch == 0:
                        ins = pool.tensor_copy(rs[:], sq[cch % 2][:])
                    else:
                        pool.wait_ge(ysum_ready, n - 1)
                        ins = pool.tensor_tensor(rs[:], rs[:], sq[cch % 2][:], ALU.add)
                    ins.then_inc(ysum_ready, 1)

            def add_to_h(adds):
                for cch in range(DC):
                    pool.wait_ge(delta_ready, adds * DC + cch + 1)
                    pool.tensor_tensor(h[:, cch, :], h[:, cch, :], wt[cch % 2][:], ALU.add).then_inc(h_ready, 1)

            def ffn_y(f):
                return lambda cch: (("y", f, cch % 4), cch // 4)

            def mixer_constants():
                for dst, value in ((mask_row, 0.0), (add_c, 0.0), (keep_c, 1.0), (bd, 0.0), (diag_b, 0.0), (left_b, 0.0),
                                   (pick, 0.0), (row_z, 0.0), (blk, 0.0), (v_aug, 1.0), (eps_m, 1e-6)):
                    step.tick(pool.memset(dst[:], value))
                step.wait(pool)
                step.tick(pool.affine_select(out=mask_row[:, 0:P], in_=mask_row[:, 0:P], compare_op=ALU.is_ge, fill=NEG,
                                             base=0, pattern=[[1, P]], channel_multiplier=-1))
                step.tick(pool.affine_select(out=diag_b[:], in_=diag_b[:], compare_op=ALU.is_ge, fill=NEG, base=0,
                                             pattern=[[-1, P]], channel_multiplier=1))
                step.tick(pool.affine_select(out=left_b[:], in_=left_b[:], compare_op=ALU.is_gt, fill=NEG, base=0,
                                             pattern=[[1, P]], channel_multiplier=-1))
                for dst, fill in ((add_c, NEG), (keep_c, 0.0)):
                    step.tick(pool.affine_select(out=dst[:], in_=dst[:], compare_op=ALU.is_ge, fill=fill, base=-(CB - 1),
                                                 pattern=[[P, TT], [-CB // 2, 32]], channel_multiplier=1))
                step.wait(pool)
                step.tick(pool.memset(add_c[:, :, 31:32], NEG))
                step.tick(pool.memset(keep_c[:, :, 31:32], 0.0))
                for n in range(HG):
                    step.wait(pool)
                    step.tick(pool.memset(bd[32 * n:32 * n + 32, n:n + 1], 1.0))
                step.wait(pool)
                step.tick(pool.affine_select(out=pick[:], in_=pick[:], compare_op=ALU.not_equal, fill=-1.0, base=0,
                                             pattern=[[-1, MH], [0, P]], channel_multiplier=1))
                step.tick(pool.tensor_copy(ident_b[:], ident[:]))
                step.wait(pool)
                pool.sem_inc(mixer_consts, 1)

            sum_y_squares(0, ffn_y(0))
            add_to_h(0)
            mixer_constants()
            sum_y_squares(1, lambda cch: (("y1", cch),))
            add_to_h(1)
            sum_y_squares(2, ffn_y(1))
            add_to_h(2)

        @block.scalar
        def _(act):
            step = Count(act_step)

            def split_high(name, i=0, used=None, size=DC * COLS):
                n, slot = w_number(name, i)
                src = unit_landed(act, name, i)
                if used is not None:
                    act.wait_ge(w_used, used)
                act.activation(w_hi[slot][:, 0:size], src[:, 0:size], ACT.Copy).then_inc(hi_ready, 1)

            def pre_norm_squares(s):
                for cch in range(DC):
                    act.wait_ge(h_ready, (s - 1) * DC + cch + 1)
                    if cch >= 2:
                        act.wait_ge(sq_used, s * (DC - 1) + cch - 1)
                    act.activation(sq[cch % 2][:], h[:, cch, :], ACT.Square).then_inc(sq_ready, 1)

            def root(job):
                src = job_result(act, job)
                job_read(act.activation(rs[:], src, ACT.Sqrt, bias=eps_col[:, 0:1]), job)

            def modulate_high(s):
                shift = s * 3 * DC
                for cch in range(DC):
                    act.wait_ge(w_scaled, s * DC + cch + 1)
                    act.activation(u_hi[:, cch, :], wt[cch % 2][:], ACT.Identity,
                                   bias=ada[:, shift + cch:shift + cch + 1]).then_inc(u_hi_ready, 1)

            def ffn_up(f):
                with act.Fori(0, UP_ITERS) as i:
                    split_high(("up", f), i)
                    for j in range(2):
                        src = job_result(act, ("g", f, j), i)
                        taken(act, ("u", f, j), i, before=1)
                        job_read(act.activation(sq[j][:], src, ACT.Silu), ("g", f, j))
                    split_high(("gate", f), i)
                    for j in range(2):
                        taken(act, ("u", f, j), i)
                        act.activation(mid_hi[:, bass.ds(2 * i + j, 1), :], wt[j][:].rearrange("p (a t) -> p a t", a=1),
                                       ACT.Copy).then_inc(mid_hi_ready, 1)

            def take_y(job, sums, cch, y):
                src = job_result(act, job[0], job[1])
                if cch == 0 and sums != 1:
                    act.wait_ge(mid_ready, (sums // 2 + 1) * FC)
                act.activation(y[:, cch, :], src, ACT.Copy)
                if cch >= 2:
                    act.wait_ge(ysum_ready, sums * DC + cch - 1)
                job_read(act.activation(sq[cch % 2][:], src, ACT.Square), job[0])

            def ffn_down(f, sums, y, next_name):
                for it in range(2):
                    for n in range(6):
                        if (it, n) != (1, 5):
                            nxt = ("d", f, it, n + 1) if n < 5 else ("d", f, 1, 0)
                            kk = (n + 1) % 3
                            used = None if n % 3 == 0 else f * 8 + mixer_used * f + it * 4 + n - n // 3
                            split_high(nxt, 0, used, (DOWN_K[kk + 1] - DOWN_K[kk]) * COLS)
                        elif next_name is not None:
                            split_high(next_name, used=8, size=160 * DC)
                        if n % 3 == 2:
                            for j in range(2):
                                name = ("y", f, n // 3 * 2 + j)
                                take_y((name, it), sums, (it * 2 + n // 3) * 2 + j, y)

            def split_after(name):
                n = MIX.index(name)
                if n:
                    before = MIX[n - 1]
                    if unit_end[before] is not None:
                        job_done(act, unit_end[before])
                        used = None
                    else:
                        used = 8 + 1 + before[1]
                else:
                    used = None
                size = 160 * DC if after(name) == ("t0",) else P * DC if after(name) == ("t1",) else DC * COLS
                split_high(after(name), 0, used=used, size=size)

            def copy_out(job, dst, scale=None):
                src = job_result(act, job)
                return job_read(act.activation(dst, src, ACT.Copy) if scale is None else
                                act.activation(dst, src, ACT.Copy, scale=scale), job)

            def mixer():
                split_after(("t0",))
                split_after(("t1",))
                for n in range(2):
                    split_after(("v", n))
                    for b in range(2):
                        src = job_result(act, ("v", n, b))
                        if (n, b) == (0, 0):
                            act.wait_ge(mixer_consts, 1)
                        job_read(act.activation(v_aug[:, 2 * b:2 * b + 2, 2 * n:2 * n + 2, 0:MD],
                                                src.rearrange("p (t h e) -> p t h e", t=2, h=2), ACT.Copy), ("v", n, b))
                act.wait_ge(small_landed, 80)
                src = job_result(act, ("ifT", 0))
                job_read(act.activation(row_i[:], src[0:MH, :], ACT.Identity, bias=g_bias[:, 0:1]), ("ifT", 0))
                src = job_result(act, ("ifT", 1))
                job_read(act.activation(row_f[:], src[0:MH, :], ACT.Identity, bias=g_bias[:, 1:2]), ("ifT", 1))
                taken(act, ("ifT", 1))
                step.tick(act.activation(row_t[:], row_f[:], ACT.Abs))
                step.wait(act)
                step.tick(act.activation(row_t[:], row_t[:], ACT.Exp, scale=-1.0))
                step.wait(act)
                act.activation(row_t[:], row_t[:], ACT.Ln, bias=1.0).then_inc(soft_ready, 1)
                for n in range(4):
                    split_after(("qk", n))
                    for j in range(2):
                        cch = 2 * n + j
                        src = job_result(act, ("qk", cch))
                        act.activation(qkc[:, cch, :], src, ACT.Identity, bias=col2[:, 32 + cch:33 + cch],
                                       scale=col2[:, 24 + cch:25 + cch]).then_inc(conv_first, 1)
                    for j in range(2):
                        cch = 2 * n + j
                        taken(act, ("qk", cch))
                        act.activation(qkc[:, cch, :], qkc[:, cch, :], ACT.Silu).then_inc(qk_ready, 1)
                act.wait_ge(m_ready, 1)
                act.activation(row_t[:], row_t[:], ACT.Exp, scale=-1.0).then_inc(em_ready, 1)
                for n in range(2):
                    split_after(("o", n))
                    for j in range(2):
                        src = job_result(act, ("o", 2 * n + j))
                        job_read(act.activation(sig_o[:, 2 * n + j, :], src, ACT.Sigmoid), ("o", 2 * n + j))

                def head_exps(hd):
                    for j in range(TT):
                        act.wait_ge(arg_ready, hd * TT + j + 1)
                        act.activation(sq[j % 2][:, 0:T - j * P], sq[j % 2][:, 0:T - j * P], ACT.Exp,
                                       bias=cols[:, 0, j, hd:hd + 1]).then_inc(e_ready, 1)

                head_exps(0)
                for hd, name in enumerate([("kcvc",), ("kk",), ("qn", 0), ("qn", 1)]):
                    split_after(name)
                    for j, ab in enumerate("ab"):
                        job = name + (ab,)
                        if hd == 0:
                            src = job_result(act, job)
                            job_read(act.activation(kv_t[:, j, :, :], src.rearrange("p (n par) -> p par n", par=2), ACT.Copy), job)
                        elif hd == 1:
                            copy_out(job, ksw[:, j, :])
                        else:
                            copy_out(job, qn[:, 2 * name[1] + j, :], scale=ND ** -0.5)
                    if hd == 0:
                        taken(act, ("kcvc", "b"))
                        for par in range(2):
                            for g in range(NG):
                                act.dma_start(kv_2[par * ND:(par + 1) * ND, :, g, :],
                                              kv_t[g * ND:(g + 1) * ND, :, par, :]).then_inc(kv_moved, 16)
                    if hd < MH - 1:
                        head_exps(hd + 1)
                act.wait_ge(ssm_ready, 1)
                act.activation(ssm[:], ssm[:], ACT.Sqrt, bias=eps_m[:, 0:1], scale=1.0 / MD).then_inc(ssm_root, 1)
                for kv in range(2):
                    act.wait_ge(blk_ready, kv + 1)
                    act.activation(blk_hi[:], blk[:], ACT.Copy).then_inc(blk_hi_ready, 1)
                    for a in range(2):
                        split_after(("c1", kv, a))
                    for half in range(2):
                        src = job_result(act, ("hid", kv, half))
                        b1 = 44 + 2 * kv + half
                        job_read(act.activation(hid[:, kv, half, :], src[:, 0:64], ACT.Silu, bias=col2[:, b1:b1 + 1]), ("hid", kv, half))
                src = job_result(act, ("kcmp",))
                job_read(act.activation(k_cmp[:], src[:, 0:32], ACT.Identity, bias=col2[:, 80:81]), ("kcmp",))
                taken(act, ("t0", 0))
                taken(act, ("t0", 1))
                act.activation(sig_n[:], g_tok[:, :, 8:32].rearrange("p t (h b) -> p t h b", b=3), ACT.Sigmoid).then_inc(sig_n_ready, 1)
                for t in range(TT):
                    act.wait_ge(arg_c_ready, t + 1)
                    act.activation(p_c[:], p_c[:], ACT.Exp).then_inc(e_c_ready, 1)
                    src = job_result(act, ("pcT", t))
                    if t:
                        job_done(act, ("oc", t - 1))
                    job_read(act.activation(pt_c[:].rearrange("p g t -> p (g t)"), src[:, 0:NG * P], ACT.Copy), ("pcT", t))
                for s, (t, g, hh) in enumerate(STEPS):
                    if s % (2 * FILL) == 0:
                        split_after(("ga", s // (2 * FILL)))
                    for br, (name, p) in enumerate((("ss", p_s), ("sw", p_w))):
                        n = P * len(blocks_of(t)[br])
                        act.wait_ge(n_max_ready, s + 1)
                        src = job_result(act, (name, s))
                        if s >= 2:
                            job_done(act, ("ts" if br == 0 else "tw", s - 2))
                        job_read(act.activation(p[s % 2][:, 0:n], src[:, 0:n], ACT.Exp, bias=n_max[:, s, br:br + 1],
                                                accum_out=sums[:, s, br:br + 1]), (name, s))
                    if s % FILL == FILL // 2:
                        cch = s // FILL
                        src = job_result(act, ("ga", cch))
                        job_read(act.activation(sig_a[:, cch, :], src, ACT.Sigmoid), ("ga", cch))
                    n = P * len(blocks_of(t)[1])
                    src = job_result(act, ("tw", s))
                    job_read(act.activation(pt_w[s % 2][:, 0:n], src[:, 0:n], ACT.Copy), ("tw", s))
                for n in range(4):
                    split_after(("gb", n))
                    for j in range(2):
                        src = job_result(act, ("gb", 2 * n + j))
                        job_read(act.activation(sig_b[:, 2 * n + j, :], src, ACT.Sigmoid), ("gb", 2 * n + j))
                for fc in range(4):
                    src = job_result(act, ("oT", fc))
                    act.activation(o_hi[:, fc, :], src, ACT.Copy).then_inc(o_hi_ready, 1)
                act.activation(hm_hi[:], hm[:], ACT.Copy).then_inc(o_hi_ready, 1)
                for j in range(2):
                    split_after(("um", j))
                    split_after(("un", j))
                    for n in range(4):
                        act.wait_ge(merged, 4 * j + n + 1)
                        act.activation(u_hi[:, 4 * j + n, :], wt[n % 2][:], ACT.Copy).then_inc(u_hi_ready, 1)
                for n in range(4):
                    split_after(("wo", n))
                    for j in range(2):
                        take_y((("y1", 2 * n + j), 0), 1, 2 * n + j, y_mix)

            act.wait_ge(c_landed, 16)
            act.activation(silu_c[:], c_col[:], ACT.Silu).then_inc(silu_c_ready, 1)
            for cch in range(DC):
                job_read(act.activation(h[:, cch, :], job_result(act, ("x", cch)), ACT.Copy), ("x", cch))
            for cch in range(DC):
                taken(act, ("x", cch))
                if cch >= 2:
                    act.wait_ge(sq_used, cch - 1)
                act.activation(sq[cch % 2][:], h[:, cch, :], ACT.Square).then_inc(sq_ready, 1)
            split_high(("g0", 0))
            root(("pre", 0))
            modulate_high(0)
            ffn_up(0)
            ffn_down(0, 0, y_ffn, ("t0",))
            root(("post", 0))
            pre_norm_squares(1)
            root(("pre", 1))
            modulate_high(1)
            mixer()
            root(("post", 1))
            pre_norm_squares(2)
            root(("pre", 2))
            modulate_high(2)
            ffn_up(1)
            ffn_down(1, 2, y_ffn, None)
            root(("post", 2))
            for cch in range(DC):
                src = job_result(act, ("out", cch))
                job_read(act.activation(out_tok[:, :, cch * P:(cch + 1) * P], src.rearrange("p (t n) -> p t n", t=TT),
                                        ACT.Copy), ("out", cch))

        @block.vector
        def _(dve):
            step = Count(dve_step)

            def split_low(name, i=0, size=DC * COLS):
                n, slot = w_number(name, i)
                dve.wait_ge(hi_ready, n)
                dve.tensor_tensor(w_lo[slot][:, 0:size], raw[plan.raws[name][0]][:, 0:size],
                                  w_hi[slot][:, 0:size].bitcast(F32), ALU.subtract).then_inc(lo_ready, 1)

            def sum_ada(name, i, number):
                src = unit_landed(dve, name, i)
                for j in range(DC):
                    part = src[:, j * COLS:(j + 1) * COLS]
                    if j:
                        dve.wait_ge(dve_step, (DC - 1) * number + j)
                        ins = dve.scalar_tensor_tensor(ada_acc[:], part, silu_c[:, j:j + 1], ada_acc[:], ALU.mult, ALU.add)
                    else:
                        ins = dve.tensor_scalar(ada_acc[:], part, silu_c[:, 0:1], None, ALU.mult)
                    ins.then_inc(dve_step if j < DC - 1 else ada_summed, 1)

            def take_ada(name, i, number):
                src = job_result(dve, name, i)
                at_ = bass.ds(2 * (number + ADA_FIRST), 2)
                job_read(dve.tensor_tensor(ada[:, at_], src[:, 0:2], col1[:, at_], ALU.add), name)

            def inverse_rms(job):
                taken(dve, job)
                misc.tick(dve.reciprocal(rs[:], rs[:]))
                misc.wait(dve)

            misc = Count(dve_misc)

            def gains(s):
                shift, scale, gate = (ada[:, (3 * s + j) * DC:(3 * s + j + 1) * DC] for j in range(3))
                pre = col1[:, 72 + 2 * s * DC:72 + (2 * s + 1) * DC]
                misc.tick(dve.scalar_tensor_tensor(gain_a[:], scale, 1.0, pre, ALU.add, ALU.mult))
                misc.wait(dve)
                misc.tick(dve.tensor_scalar(gain_a[:], gain_a[:], ROOT_D, None, ALU.mult))
                misc.wait(dve)

            def gains_post(s, weight):
                gate = ada[:, (3 * s + 2) * DC:(3 * s + 3) * DC]
                post = col1[:, 72 + (2 * s + 1) * DC:72 + (2 * s + 2) * DC]
                misc.tick(dve.scalar_tensor_tensor(gain_g[:], gate, weight * ROOT_D, post, ALU.mult, ALU.mult))
                misc.wait(dve)

            def modulate(s):
                shift = s * 3 * DC

                base = (0, DC, 3 * DC)[s]

                def low(cch):
                    dve.wait_ge(u_hi_ready, base + cch + 1)
                    dve.scalar_tensor_tensor(u_lo[:, cch, :], wt[cch % 2][:], ada[:, shift + cch:shift + cch + 1],
                                             u_hi[:, cch, :].bitcast(F32), ALU.add, ALU.subtract).then_inc(u_ready, 1)
                for cch in range(DC):
                    if cch >= 2:
                        low(cch - 2)
                        dve.wait_ge(u_ready, base + cch - 1)
                    dve.scalar_tensor_tensor(wt[cch % 2][:], h[:, cch, :], gain_a[:, cch:cch + 1], rs[:],
                                             ALU.mult, ALU.mult).then_inc(w_scaled, 1)
                low(DC - 2)
                low(DC - 1)

            def ffn_up(f):
                with dve.Fori(0, UP_ITERS) as i:
                    split_low(("up", f), i)
                    if f == 0:
                        sum_ada(("ada", "a"), i, 2 * i)
                    split_low(("gate", f), i)
                    if f == 0:
                        take_ada(("ada", "a"), i, 2 * i)
                        sum_ada(("ada", "b"), i, 2 * i + 1)
                    for j in range(2):
                        taken(dve, ("g", f, j), i)
                        src = job_result(dve, ("u", f, j), i)
                        job_read(dve.tensor_tensor(wt[j][:], src, sq[j][:], ALU.mult), ("u", f, j))
                    if f == 0:
                        take_ada(("ada", "b"), i, 2 * i + 1)
                    for j in range(2):
                        dve.wait_ge(mid_hi_ready, (i + f * UP_ITERS) * 2 + j + 1)
                        at_ = bass.ds(2 * i + j, 1)
                        dve.tensor_tensor(mid_lo[:, at_, :], wt[j][:].rearrange("p (a t) -> p a t", a=1),
                                          mid_hi[:, at_, :].bitcast(F32), ALU.subtract).then_inc(mid_ready, 1)

            def ffn_down(f, next_name):
                for it in range(2):
                    for n in range(6):
                        if f == 0 and n == 3:
                            take_ada(("ada", 2), it, 2 * UP_ITERS + 2 * it)
                        if (it, n) != (1, 5):
                            nxt = ("d", f, it, n + 1) if n < 5 else ("d", f, 1, 0)
                            kk = (n + 1) % 3
                            split_low(nxt, 0, (DOWN_K[kk + 1] - DOWN_K[kk]) * COLS)
                        elif next_name is not None:
                            split_low(next_name, 0, 160 * DC)
                        if f == 0 and n in (1, 4):
                            number = 2 * UP_ITERS + 2 * it + n // 3
                            sum_ada(("ada", it, n + 1), 0, number)
                    if f == 0:
                        take_ada(("ada", 5), it, 2 * UP_ITERS + 2 * it + 1)

            def update_h(post, y):
                for cch in range(DC):
                    if cch >= 2:
                        dve.wait_ge(h_ready, post * DC + cch - 1)
                    dve.scalar_tensor_tensor(wt[cch % 2][:], y[:, cch, :], gain_g[:, cch:cch + 1], rs[:],
                                             ALU.mult, ALU.mult).then_inc(delta_ready, 1)

            def mixer_low(name):
                nxt = after(name)
                size = 160 * DC if nxt == ("t0",) else P * DC if nxt == ("t1",) else DC * COLS
                split_low(nxt, 0, size=size)

            def bcast(ap, shape):
                return ap.broadcast_to(shape)

            def mixer():
                mixer_low(("t0",))
                for b in range(2):
                    src = job_result(dve, ("t0", b))[:, 0:320].rearrange("p (t n) -> p t n", t=2)
                    dve.wait_ge(mixer_consts, 1)
                    misc.tick(dve.tensor_copy(g_tok[:, 2 * b:2 * b + 2, :], src[:, :, 0:32]))
                    job_read(dve.tensor_copy(vsw[:, 2 * b:2 * b + 2, 0, :], src[:, :, 32:160]), ("t0", b))
                mixer_low(("t1",))
                src = job_result(dve, ("t1",)).rearrange("p (t n) -> p t n", t=TT)
                job_read(dve.tensor_copy(vsw[:, :, 1, :], src), ("t1",))
                for n in range(2):
                    mixer_low(("v", n))
                dve.wait_ge(soft_ready, 1)
                misc.tick(dve.scalar_tensor_tensor(row_f[:], row_f[:], 0.0, row_t[:], ALU.min, ALU.subtract))
                misc.wait(dve)
                misc.tick(dve.tensor_tensor_scan(row_s[:], row_f[:], row_z[:], 0.0, ALU.add, ALU.add))
                misc.wait(dve)
                misc.tick(dve.tensor_tensor(row_i[:], row_i[:], row_s[:], ALU.subtract))
                misc.wait(dve)
                misc.tick(dve.tensor_tensor_scan(row_m[:], row_i[:], row_i[:], 0.0, ALU.max, ALU.max))
                misc.wait(dve)
                dve.tensor_tensor(row_t[:], row_s[:], row_m[:], ALU.add).then_inc(m_ready, 1)
                for n in range(4):
                    mixer_low(("qk", n))
                    for tap in (2, 1, 0):
                        for j in range(2):
                            cch = 2 * n + j
                            dve.wait_ge(conv_first, cch + 1)
                            if tap < 2:
                                misc.wait(dve, misc.n - 1 if tap == 1 or j == 0 else misc.n)
                            src = PS[:, plan.jobs[("qk", cch)][0], :]
                            lag = 3 - tap
                            w = 8 * tap + cch
                            ins = dve.scalar_tensor_tensor(qkc[:, cch, lag:T], src[:, 0:T - lag], col2[:, w:w + 1],
                                                           qkc[:, cch, lag:T], ALU.mult, ALU.add)
                            if tap:
                                misc.tick(ins)
                            else:
                                job_read(ins, ("qk", cch))
                for n in range(2):
                    sum_ada(("ada", "m", n), 0, 26 + n)
                    take_ada(("ada", "m", n), 0, 26 + n)
                src = job_result(dve, ("colT",))
                job_read(dve.tensor_copy(cols[:].rearrange("p a t h -> p (a t h)"), src[:, 0:2 * TT * MH]), ("colT",))
                mixer_low(("o", 0))
                mixer_low(("o", 1))

                def head_weights(hd):
                    neg = job_result(dve, ("negM", hd))
                    for j in range(TT + 1):
                        if j < TT:
                            n = T - j * P
                            if j >= 2:
                                taken(dve, ("S", hd, j - 2))
                            elif hd:
                                taken(dve, ("S", hd - 1, j + 2))
                            ins = dve.tensor_tensor(sq[j % 2][:, 0:n], neg[:, j * P:T], mask_row[:, 0:n], ALU.add)
                            ins.then_inc(arg_ready, 1)
                        if j:
                            i, n = j - 1, T - (j - 1) * P
                            src = job_result(dve, ("S", hd, i))
                            dve.wait_ge(e_ready, hd * TT + j)
                            job_read(dve.scalar_tensor_tensor(p_m[:, i, 0:n], src[:, 0:n], MD ** -0.5, sq[i % 2][:, 0:n],
                                                              ALU.mult, ALU.mult), ("S", hd, i))
                    dve.wait_ge(arg_ready, hd * TT + TT)
                    dve.sem_inc(bank_free[plan.jobs[("negM", hd)][0]], 1)

                def head_output(hd):
                    for b in range(2):
                        num = job_result(dve, ("num", hd, b))[:, 0:2 * (MD + 1)].rearrange("p (t e) -> p t e", t=2)
                        misc.tick(dve.tensor_copy(den[:, hd, 2 * b:2 * b + 2], num[:, :, MD]))
                    misc.wait(dve)
                    misc.tick(dve.scalar_tensor_tensor(max_c[:, 0:TT], den[:, hd, :], -1.0, cols[:, 1, :, hd], ALU.mult, ALU.max))
                    misc.wait(dve)
                    misc.tick(dve.tensor_tensor(den[:, hd, :], den[:, hd, :], max_c[:, 0:TT], ALU.max))
                    misc.wait(dve)
                    misc.tick(dve.reciprocal(den[:, hd, :], den[:, hd, :]))
                    misc.wait(dve)
                    h3 = hm[:, hd, :].rearrange("p (t e) -> p t e", t=TT)
                    for b in range(2):
                        num = job_result(dve, ("num", hd, b))[:, 0:2 * (MD + 1)].rearrange("p (t e) -> p t e", t=2)
                        job_read(dve.tensor_tensor(h3[:, 2 * b:2 * b + 2, :], num[:, :, 0:MD],
                                                   bcast(den[:, hd, 2 * b:2 * b + 2].unsqueeze(2), [P, 2, MD]), ALU.mult), ("num", hd, b))
                        taken(dve, ("num", hd, b))
                    misc.tick(dve.tensor_tensor(wt[0][:], hm[:, hd, :], hm[:, hd, :], ALU.mult))
                    misc.wait(dve)
                    misc.tick(dve.tensor_reduce(ssm[:, hd, :], wt[0][:].rearrange("p (t e) -> p t e", t=TT), AX.X, ALU.add))
                    misc.wait(dve)

                head_weights(0)
                for hd, name in enumerate([("kcvc",), ("kk",), ("qn", 0), ("qn", 1)]):
                    mixer_low(name)
                    head_output(hd)
                    if hd < MH - 1:
                        head_weights(hd + 1)
                dve.sem_inc(ssm_ready, 1)
                dve.wait_ge(kv_moved, 64)

                def make_blocks(kv):
                    for a in range(2):
                        src = kv_2[:, kv, :, 8 * a:8 * a + 8 * NCMP].rearrange("p g (n l) -> p l g n", l=8)
                        pe_at = 48 + 16 * kv + 8 * a
                        pe = bcast(col2[:, pe_at:pe_at + 8].unsqueeze(2).unsqueeze(3), [P, 8, NG, NCMP])
                        misc.tick(dve.tensor_tensor(blk[:, 8 * a:8 * a + 8, :, 0:NCMP], src, pe, ALU.add))
                    misc.wait(dve)
                    dve.sem_inc(blk_ready, 1)

                def blocks_low(kv):
                    dve.wait_ge(blk_hi_ready, kv + 1)
                    dve.tensor_tensor(blk_lo[:], blk[:], blk_hi[:].bitcast(F32), ALU.subtract).then_inc(blk_lo_ready, 1)

                make_blocks(0)
                blocks_low(0)
                mixer_low(("c1", 0, 0))
                dve.wait_ge(ssm_root, 1)
                misc.tick(dve.reciprocal(ssm[:], ssm[:]))
                misc.wait(dve)
                for hd in range(MH):
                    h3 = hm[:, hd, :].rearrange("p (t e) -> p t e", t=TT)
                    dve.tensor_tensor(h3, h3, bcast(ssm[:, hd, :].unsqueeze(2), [P, TT, MD]), ALU.mult).then_inc(hm_normed, 1)
                for hd in range(MH):
                    src = job_result(dve, ("hT", hd))
                    job_read(dve.scalar_tensor_tensor(hm[:, hd, :], src, col2[:, 40 + hd:41 + hd], sig_o[:, hd, :],
                                                      ALU.mult, ALU.mult), ("hT", hd))
                mixer_low(("c1", 0, 1))
                dve.wait_ge(blk_lo_ready, 1)
                job_done(dve, ("hid", 0, 1))
                make_blocks(1)
                blocks_low(1)
                mixer_low(("c1", 1, 0))
                mixer_low(("c1", 1, 1))
                taken(dve, ("hid", 1, 0))
                taken(dve, ("hid", 1, 1))
                for g in range(NG):
                    src = hid[:, 1, :, g * 32:(g + 1) * 32].unsqueeze(2)
                    misc.tick(dve.tensor_copy(hid_rep[:, :, g, :, :], bcast(src, [P, 2, HG, 32])))
                misc.wait(dve)
                dve.sem_inc(hid_rep_ready, 1)
                src = job_result(dve, ("vcmp",))[:, 0:NG * ND].rearrange("p (g e) -> p g e", g=NG)
                job_read(dve.tensor_tensor(v_tmp[:], src, bcast(b2_row[:].unsqueeze(1), [P, NG, ND]), ALU.add), ("vcmp",))
                taken(dve, ("vcmp",))
                for n in range(HG):
                    misc.tick(dve.tensor_scalar(v_bd[:, :, n, :], v_tmp[:], bd[:, n:n + 1], None, ALU.mult))
                misc.wait(dve)
                dve.sem_inc(v_bd_ready, 1)
                def take_oc(t):
                    src = job_result(dve, ("oc", t))
                    job_read(dve.tensor_copy(o_acc[:, t, :], src), ("oc", t))

                for t in range(TT):
                    for g in range(NG):
                        src = job_result(dve, ("sc", t, g))[:, 0:P].rearrange("p (h n) -> p h n", n=32)
                        if t and g == 0:
                            job_done(dve, ("pcT", t - 1))
                        job_read(dve.tensor_tensor(p_c[:, 4 * g:4 * g + 4, :], src, bcast(add_c[:, t:t + 1, :], [P, HG, 32]), ALU.add), ("sc", t, g))
                        taken(dve, ("sc", t, g))
                    misc.tick(dve.tensor_reduce(max_c[:], p_c[:], AX.X, ALU.max))
                    misc.wait(dve)
                    dve.tensor_tensor(p_c[:], p_c[:], bcast(max_c[:].unsqueeze(2), [P, NH, 32]), ALU.subtract).then_inc(arg_c_ready, 1)
                    dve.wait_ge(e_c_ready, t + 1)
                    misc.tick(dve.tensor_tensor(p_c[:], p_c[:], bcast(keep_c[:, t:t + 1, :], [P, NH, 32]), ALU.mult))
                    misc.wait(dve)
                    misc.tick(dve.tensor_reduce(sum_c[:], p_c[:], AX.X, ALU.add))
                    misc.wait(dve)
                    misc.tick(dve.tensor_scalar(sum_c[:], sum_c[:], 1e-30, None, ALU.max))
                    misc.wait(dve)
                    misc.tick(dve.reciprocal(sum_c[:], sum_c[:]))
                    misc.wait(dve)
                    if t == 0:
                        dve.wait_ge(sig_n_ready, 1)
                    misc.tick(dve.tensor_tensor(sum_c[:], sum_c[:], sig_n[:, t, :, 0], ALU.mult))
                    misc.wait(dve)
                    dve.tensor_tensor(p_c[:], p_c[:], bcast(sum_c[:].unsqueeze(2), [P, NH, 32]), ALU.mult).then_inc(p_c_ready, 1)
                    if t:
                        take_oc(t - 1)
                take_oc(TT - 1)

                def scores_max(s):
                    t = STEPS[s][0]
                    for br, name in enumerate(("ss", "sw")):
                        n = P * len(blocks_of(t)[br])
                        src = job_result(dve, (name, s))
                        ins = dve.tensor_reduce(n_max[:, s, br:br + 1], src[:, 0:n], AX.X, ALU.max, negate=True)
                    ins.then_inc(n_max_ready, 1)

                scores_max(0)
                for s, (t, g, hh) in enumerate(STEPS):
                    if s % (2 * FILL) == 0:
                        mixer_low(("ga", s // (2 * FILL)))
                    if s + 1 < len(STEPS):
                        scores_max(s + 1)
                    n = P * len(blocks_of(t)[0])
                    src = job_result(dve, ("ts", s))
                    job_read(dve.tensor_copy(pt_s[s % 2][:, 0:n], src[:, 0:n]), ("ts", s))
                    if hh == 0 and s:
                        group_output(s - HG)
                group_output(len(STEPS) - HG)
                dve.sem_inc(o_acc_ready, 1)
                for n in range(4):
                    mixer_low(("gb", n))
                for fc in range(4):
                    src = job_result(dve, ("oT", fc))
                    dve.wait_ge(o_hi_ready, fc + 1)
                    job_read(dve.tensor_tensor(o_lo[:, fc, :], src, o_hi[:, fc, :].bitcast(F32), ALU.subtract), ("oT", fc))
                dve.wait_ge(o_hi_ready, 5)
                dve.tensor_tensor(hm_lo[:], hm[:], hm_hi[:].bitcast(F32), ALU.subtract).then_inc(hm_lo_ready, 1)
                for j in range(2):
                    mixer_low(("um", j))
                    for n in range(4):
                        cch = 4 * j + n
                        src = job_result(dve, ("ym", cch))
                        job_read(dve.tensor_tensor(sig_a[:, cch, :], sig_a[:, cch, :], src, ALU.mult), ("ym", cch))
                    mixer_low(("un", j))
                    for n in range(4):
                        cch = 4 * j + n
                        src = job_result(dve, ("yn", cch))
                        if cch >= 2:
                            dve.wait_ge(u_ready, DC + DC + cch - 1)
                        job_read(dve.tensor_tensor(wt[n % 2][:], sig_b[:, cch, :], src, ALU.mult), ("yn", cch))
                        taken(dve, ("yn", cch))
                        dve.tensor_tensor(wt[n % 2][:], wt[n % 2][:], sig_a[:, cch, :], ALU.add).then_inc(merged, 1)
                        dve.wait_ge(u_hi_ready, 2 * DC + cch + 1)
                        dve.tensor_tensor(u_lo[:, cch, :], wt[n % 2][:], u_hi[:, cch, :].bitcast(F32), ALU.subtract).then_inc(u_ready, 1)
                for n in range(4):
                    mixer_low(("wo", n))

            def group_output(s0):
                t, g, _ = STEPS[s0]
                for s in range(s0, s0 + HG):
                    taken(dve, ("ss", s))
                    taken(dve, ("sw", s))
                misc.tick(dve.reciprocal(w_sw[:], sums[:, s0:s0 + HG, :]))
                misc.wait(dve)
                misc.tick(dve.tensor_tensor(w_sw[:], w_sw[:], sig_n[:, t, g * HG:(g + 1) * HG, 1:3], ALU.mult))
                misc.wait(dve)
                src = job_result(dve, ("o_nsa", t, g)).rearrange("p (h b e) -> p h b e", h=HG, b=2)
                ins = dve.tensor_tensor(o_tmp[:], src, bcast(w_sw[:].unsqueeze(3), [P, HG, 2, ND]), ALU.mult)
                job_read(ins, ("o_nsa", t, g))
                taken(dve, ("o_nsa", t, g))
                acc = o_acc[:, t, g * HG * ND:(g + 1) * HG * ND].rearrange("p (h e) -> p h e", h=HG)
                if g == 0:
                    taken(dve, ("oc", t))
                for br in range(2):
                    misc.tick(dve.tensor_tensor(acc, acc, o_tmp[:, :, br, :], ALU.add))
                    misc.wait(dve)

            src = job_result(dve, ("cols", 1))
            job_read(dve.tensor_copy(col1[:], src[:, 0:120]), ("cols", 1))
            src = job_result(dve, ("cols", 2))
            job_read(dve.tensor_copy(col2[:], src[:, 0:81]), ("cols", 2))
            dve.wait_ge(silu_c_ready, 1)
            for j in range(DC):
                dve.wait_ge(ada_first_landed[j], 16)
                if j:
                    misc.wait(dve)
                    ins = dve.scalar_tensor_tensor(ada_acc0[:], ada_w[:, j, :], silu_c[:, j:j + 1], ada_acc0[:], ALU.mult, ALU.add)
                else:
                    ins = dve.tensor_scalar(ada_acc0[:], ada_w[:, 0, :], silu_c[:, 0:1], None, ALU.mult)
                misc.tick(ins) if j < DC - 1 else ins.then_inc(ada_summed, 1)
            src = job_result(dve, ("ada0",))
            taken(dve, ("cols", 1))
            ins = dve.tensor_tensor(ada[:, 0:2 * ADA_FIRST], src[:, 0:2 * ADA_FIRST], col1[:, 0:2 * ADA_FIRST], ALU.add)
            job_read(ins, ("ada0",))
            taken(dve, ("ada0",))
            gains(0)
            split_low(("g0", 0))
            inverse_rms(("pre", 0))
            modulate(0)
            ffn_up(0)
            ffn_down(0, ("t0",))
            taken(dve, ("ada", 5), 1)
            gains_post(0, 0.5)
            gains(1)
            inverse_rms(("post", 0))
            update_h(0, y_ffn)
            inverse_rms(("pre", 1))
            modulate(1)
            mixer()
            taken(dve, ("ada", "m", 1))
            gains_post(1, 1.0)
            gains(2)
            inverse_rms(("post", 1))
            update_h(1, y_mix)
            inverse_rms(("pre", 2))
            modulate(2)
            ffn_up(1)
            ffn_down(1, None)
            gains_post(2, 0.5)
            inverse_rms(("post", 2))
            update_h(2, y_ffn)

        @block.tensor
        def _(pe):
            def three_passes(ps, pairs):
                total = len(pairs)
                for n, (wh, wl, ah, al) in enumerate(pairs):
                    pe.matmul(ps, wh, ah, start=(n == 0), stop=False)
                    pe.matmul(ps, wh, al, start=False, stop=False)
                    ins = pe.matmul(ps, wl, ah, start=False, stop=(n == total - 1))
                return ins

            def unit_ready(name, i=0):
                n, slot = w_number(name, i)
                pe.wait_ge(lo_ready, n)
                return w_hi[slot], w_lo[slot]

            def k_pairs(unit, j, kn, ahi, alo, k0=0, first=True, width=COLS):
                wh, wl = unit
                return [(wh[:, k * width + j * P:k * width + (j + 1) * P], wl[:, k * width + j * P:k * width + (j + 1) * P],
                         ahi[:, k0 + k, :], alo[:, k0 + k, :]) for k in range(kn)]

            def sum_squares(s):
                ps = job_start(pe, ("pre", s))
                for cch in range(DC):
                    pe.wait_ge(sq_ready, s * DC + cch + 1)
                    ins = pe.matmul(ps, ones[:], sq[cch % 2][:], start=(cch == 0), stop=(cch == DC - 1))
                    if cch < DC - 1:
                        ins.then_inc(sq_used, 1)
                job_end(ins, ("pre", s))

            def ada_columns(name, i, number):
                ps = job_start(pe, name, i)
                pe.wait_ge(ada_summed, number + 2)
                for j in range(2):
                    ins = pe.matmul(ps[:, j:j + 1], ada_acc[:, j * P:(j + 1) * P], ones[:, 0:1], start=True, stop=True)
                job_end(ins, name)

            def ffn_up(f):
                pe.wait_ge(u_ready, (3 * f + 1) * DC)
                with pe.Fori(0, UP_ITERS) as i:
                    n0, slot = w_number(("g0", f))
                    pe.wait_ge(lo_ready, n0 + 2 * i)
                    for j in range(2):
                        ps = job_start(pe, ("g", f, j), i)
                        ins = three_passes(ps, k_pairs((w_hi[slot], w_lo[slot]), j, DC, u_hi, u_lo))
                        job_end(ins, ("g", f, j))
                    if f == 0:
                        ada_columns(("ada", "a"), i, 2 * i)
                    unit = unit_ready(("up", f), i)
                    for j in range(2):
                        ps = job_start(pe, ("u", f, j), i)
                        ins = three_passes(ps, k_pairs(unit, j, DC, u_hi, u_lo))
                        job_end(ins, ("u", f, j))
                    if f == 0:
                        ada_columns(("ada", "b"), i, 2 * i + 1)

            def ffn_down(f):
                pe.wait_ge(mid_ready, (f + 1) * FC)
                base_n, _ = w_number(("gate", f))
                base_n += 2 * (UP_ITERS - 1)
                with pe.Fori(0, 2) as i:
                    for n in range(6):
                        pe.wait_ge(lo_ready, base_n + 6 * i + n)
                        slot = (base_n + n - 1) % 2
                        k0, k1 = DOWN_K[n % 3], DOWN_K[n % 3 + 1]
                        for j in range(2):
                            name = ("y", f, n // 3 * 2 + j)
                            if n % 3 == 0:
                                ps = job_start(pe, name, i)
                            else:
                                ps = PS[:, plan.jobs[name][0], :]
                            for k in range(k1 - k0):
                                wh, wl = (w[slot][:, k * COLS + j * P:k * COLS + (j + 1) * P] for w in (w_hi, w_lo))
                                f_at = k0 + k
                                pe.matmul(ps, wh, mid_hi[:, f_at, :], start=(f_at == 0), stop=False)
                                pe.matmul(ps, wh, mid_lo[:, f_at, :], start=False, stop=False)
                                ins = pe.matmul(ps, wl, mid_hi[:, f_at, :], start=False, stop=(f_at == FC - 1))
                            if n % 3 == 2:
                                job_end(ins, name)
                        if n % 3 < 2:
                            ins.then_inc(w_used, 1)
                        if f == 0 and n in (2, 5):
                            ada_columns(("ada", n), i, 2 * UP_ITERS + 2 * i + n // 3)

            def post_sum(s):
                ps = job_start(pe, ("post", s))
                pe.wait_ge(ysum_ready, (s + 1) * DC)
                job_end(pe.matmul(ps, ones[:], rs[:], start=True, stop=True), ("post", s))

            def mixer():
                def unit(name):
                    return unit_ready(name)

                def last_of(ins, name):
                    if unit_end[name] is None:
                        ins.then_inc(w_used, 1)

                def feature_unit(name, jobs, act_hi=u_hi, act_lo=u_lo, kn=DC, width=COLS):
                    w = unit(name)
                    for j, job in enumerate(jobs):
                        feature_chunk(w, j, job, act_hi, act_lo, kn, width)

                def feature_chunk(w, j, job, act_hi=u_hi, act_lo=u_lo, kn=DC, width=COLS):
                    ps = job_start(pe, job)
                    job_end(three_passes(ps, k_pairs(w, j, kn, act_hi, act_lo, width=width)), job)

                def token_unit(name, jobs, n):
                    wh, wl = unit(name)
                    per = TT // len(jobs)
                    for b, job in enumerate(jobs):
                        ps = job_start(pe, job)
                        for i in range(per):
                            t = b * per + i
                            pairs = [(u_hi[:, k, t * P:(t + 1) * P], u_lo[:, k, t * P:(t + 1) * P],
                                      wh[:, k * n:(k + 1) * n], wl[:, k * n:(k + 1) * n]) for k in range(DC)]
                            ins = three_passes(ps[:, i * n:(i + 1) * n], pairs)
                        job_end(ins, job)

                pe.wait_ge(u_ready, 2 * DC)
                pe.wait_ge(mixer_consts, 1)
                token_unit(("t0",), [("t0", 0), ("t0", 1)], 160)
                token_unit(("t1",), [("t1",)], P)
                for n in range(2):
                    token_unit(("v", n), [("v", n, 0), ("v", n, 1)], COLS)
                taken(pe, ("t0", 0))
                taken(pe, ("t0", 1))
                for a in range(2):
                    ps = job_start(pe, ("ifT", a))
                    for t in range(TT):
                        ins = pe.transpose(ps[0:MH, t * P:(t + 1) * P], g_tok[:, t, a * MH:(a + 1) * MH], ident[:])
                    job_end(ins, ("ifT", a))
                for n in range(4):
                    feature_unit(("qk", n), [("qk", 2 * n), ("qk", 2 * n + 1)])
                for n in range(2):
                    ada_columns(("ada", "m", n), 0, 26 + n)
                ps = job_start(pe, ("colT",))
                pe.wait_ge(m_ready, 1)
                pe.wait_ge(em_ready, 1)
                for a, row in enumerate((row_i, row_t)):
                    for t in range(TT):
                        at_ = (a * TT + t) * MH
                        ins = pe.transpose(ps[:, at_:at_ + MH], row[:, t * P:(t + 1) * P], ident[0:MH, 0:MH])
                job_end(ins, ("colT",))
                for n in range(2):
                    feature_unit(("o", n), [("o", 2 * n), ("o", 2 * n + 1)])

                def head_scores(hd):
                    ps = job_start(pe, ("negM", hd))
                    job_end(pe.matmul(ps, pick[:, hd, :], row_m[:], start=True, stop=True), ("negM", hd))
                    pe.wait_ge(qk_ready, MH + hd + 1)
                    for j in range(TT):
                        ps = job_start(pe, ("S", hd, j))
                        job_end(pe.matmul(ps[:, 0:T - j * P], qkc[:, MH + hd, j * P:(j + 1) * P], qkc[:, hd, j * P:T],
                                          start=True, stop=True), ("S", hd, j))

                def head_values(hd):
                    for b in range(2):
                        ps = job_start(pe, ("num", hd, b))
                        for i in range(2):
                            t = 2 * b + i
                            for j in range(t + 1):
                                taken(pe, ("S", hd, j))
                                ins = pe.matmul(ps[:, i * (MD + 1):(i + 1) * (MD + 1)], p_m[:, j, (t - j) * P:(t - j + 1) * P],
                                                v_aug[:, j, hd, :], start=(j == 0), stop=(j == t))
                        job_end(ins, ("num", hd, b))

                taken(pe, ("v", 1, 1))
                head_scores(0)
                for hd, name in enumerate([("kcvc",), ("kk",), ("qn", 0), ("qn", 1)]):
                    feature_unit(name, [name + ("a",), name + ("b",)])
                    head_values(hd)
                    if hd < MH - 1:
                        head_scores(hd + 1)

                def hidden(kv, a):
                    w = unit(("c1", kv, a))
                    if a == 0:
                        pe.wait_ge(blk_lo_ready, kv + 1)
                    for half in range(2):
                        job = ("hid", kv, half)
                        ps = job_start(pe, job) if a == 0 else PS[:, plan.jobs[job][0], :]
                        for k in range(DC):
                            wh, wl = (x_[:, k * COLS + half * P:k * COLS + (half + 1) * P] for x_ in w)
                            bh, bl = (x_[:, a * DC + k, :, :].rearrange("p g n -> p (g n)") for x_ in (blk_hi, blk_lo))
                            pe.matmul(ps[:, 0:64], wh, bh, start=(a == 0 and k == 0), stop=False)
                            pe.matmul(ps[:, 0:64], wh, bl, start=False, stop=False)
                            ins = pe.matmul(ps[:, 0:64], wl, bh, start=False, stop=(a == 1 and k == DC - 1))
                        if a == 1:
                            job_end(ins, job)
                    last_of(ins, ("c1", kv, a))

                hidden(0, 0)
                for hd in range(MH):
                    ps = job_start(pe, ("hT", hd))
                    pe.wait_ge(hm_normed, hd + 1)
                    for t in range(TT):
                        ins = pe.transpose(ps[:, t * P:(t + 1) * P], hm[:, hd, t * P:(t + 1) * P], ident[:])
                    job_end(ins, ("hT", hd))
                hidden(0, 1)
                hidden(1, 0)
                hidden(1, 1)
                ps = job_start(pe, ("kcmp",))
                for half in range(2):
                    taken(pe, ("hid", 0, half))
                    taken(pe, ("hid", 1, half))
                for g in range(NG):
                    for half in range(2):
                        ins = pe.matmul(ps[g * ND:(g + 1) * ND, 0:32], w2[:, 0, half, :], hid[:, 0, half, g * 32:(g + 1) * 32],
                                        start=(half == 0), stop=(half == 1))
                job_end(ins, ("kcmp",))
                ps = job_start(pe, ("vcmp",))
                pe.wait_ge(hid_rep_ready, 1)
                for g in range(NG):
                    for half in range(2):
                        ins = pe.matmul(ps[:, g * ND:(g + 1) * ND], hid_rep[:, half, g, :, :].rearrange("p h n -> p (h n)"),
                                        w2[:, 1, half, :], start=(half == 0), stop=(half == 1))
                job_end(ins, ("vcmp",))
                taken(pe, ("kcmp",))
                taken(pe, ("qn", 1, "b"))
                taken(pe, ("kk", "b"))

                def cmp_scores(t):
                    for g in range(NG):
                        rows = slice(g * ND, (g + 1) * ND)
                        ps = job_start(pe, ("sc", t, g))
                        for hh in range(HG):
                            ins = pe.matmul(ps[:, hh * 32:(hh + 1) * 32], qn[rows, hh, t * P:(t + 1) * P], k_cmp[rows, :],
                                            start=True, stop=True)
                        job_end(ins, ("sc", t, g))

                cmp_scores(0)
                for t in range(TT):
                    if t + 1 < TT:
                        cmp_scores(t + 1)
                    ps = job_start(pe, ("pcT", t))
                    pe.wait_ge(p_c_ready, t + 1)
                    for g in range(NG):
                        ins = pe.transpose(ps[:, g * P:(g + 1) * P], p_c[:, 4 * g:4 * g + 4, :].rearrange("p h n -> p (h n)"), ident[:])
                    job_end(ins, ("pcT", t))
                    ps = job_start(pe, ("oc", t))
                    taken(pe, ("pcT", t))
                    pe.wait_ge(v_bd_ready, 1)
                    for g in range(NG):
                        ins = pe.matmul(ps[:, g * COLS:(g + 1) * COLS], pt_c[:, g, :], v_bd[:, g, :, :].rearrange("p h e -> p (h e)"),
                                        start=True, stop=True)
                    job_end(ins, ("oc", t))

                def nsa_scores(s):
                    t, g, hh = STEPS[s]
                    rows = slice(g * ND, (g + 1) * ND)
                    for br, name in enumerate(("ss", "sw")):
                        blocks = blocks_of(t)[br]
                        n = P * len(blocks)
                        ps = job_start(pe, (name, s))
                        pe.matmul(ps[:, 0:n], qn[rows, hh, t * P:(t + 1) * P], ksw[rows, br, blocks[0] * P:(t + 1) * P],
                                  start=True, stop=False)
                        if br == 1 and t - blocks[0] == WINDOW // P:
                            pe.matmul(ps[:, 0:P], ident_b[:], left_b[:], start=False, stop=False)
                        job_end(pe.matmul(ps[:, n - P:n], ident_b[:], diag_b[:], start=False, stop=True), (name, s))

                def nsa_transposes(s):
                    t = STEPS[s][0]
                    for br, (name, score, p) in enumerate((("ts", "ss", p_s), ("tw", "sw", p_w))):
                        ps = job_start(pe, (name, s))
                        taken(pe, (score, s))
                        for j in range(len(blocks_of(t)[br])):
                            ins = pe.transpose(ps[:, j * P:(j + 1) * P], p[s % 2][:, j * P:(j + 1) * P], ident[:])
                        job_end(ins, (name, s))

                def nsa_values(s):
                    t, g, hh = STEPS[s]
                    job = ("o_nsa", t, g)
                    ps = job_start(pe, job) if hh == 0 else PS[:, plan.jobs[job][0], :]
                    for br, (name, pt) in enumerate((("ts", pt_s), ("tw", pt_w))):
                        taken(pe, (name, s))
                        blocks = blocks_of(t)[br]
                        at_ = (2 * hh + br) * ND
                        for n, j in enumerate(blocks):
                            ins = pe.matmul(ps[:, at_:at_ + ND], pt[s % 2][:, n * P:(n + 1) * P], vsw[:, j, br, g * ND:(g + 1) * ND],
                                            start=(n == 0), stop=(n == len(blocks) - 1))
                    if hh == HG - 1:
                        job_end(ins, job)

                pe.wait_ge(mixer_consts, 1)
                nsa_scores(0)
                for s in range(len(STEPS)):
                    if s + 1 < len(STEPS):
                        nsa_scores(s + 1)
                    if s % FILL == 0:
                        name = ("ga", s // (2 * FILL))
                        gate_unit = unit(name)
                        feature_chunk(gate_unit, s // FILL % 2, ("ga", s // FILL))
                    nsa_transposes(s)
                    if s:
                        nsa_values(s - 1)
                nsa_values(len(STEPS) - 1)
                for n in range(4):
                    feature_unit(("gb", n), [("gb", 2 * n), ("gb", 2 * n + 1)])
                pe.wait_ge(o_acc_ready, 1)
                for fc in range(4):
                    ps = job_start(pe, ("oT", fc))
                    for t in range(TT):
                        ins = pe.transpose(ps[:, t * P:(t + 1) * P], o_acc[:, t, fc * P:(fc + 1) * P], ident[:])
                    job_end(ins, ("oT", fc))
                pe.wait_ge(hm_lo_ready, 1)
                for fc in range(4):
                    taken(pe, ("oT", fc))
                for j in range(2):
                    feature_unit(("um", j), [("ym", 4 * j + n) for n in range(4)], hm_hi, hm_lo, 4, T)
                    feature_unit(("un", j), [("yn", 4 * j + n) for n in range(4)], o_hi, o_lo, 4, T)
                pe.wait_ge(u_ready, 3 * DC)
                for n in range(4):
                    feature_unit(("wo", n), [("y1", 2 * n), ("y1", 2 * n + 1)])

            pe.wait_ge(consts_ready, 1)
            pe.wait_ge(rows_landed, 16 * 9)
            ps = job_start(pe, ("cols", 1))
            job_end(pe.transpose(ps[:, 0:120], rows1[:], ident[0:120, 0:120]), ("cols", 1))
            ps = job_start(pe, ("cols", 2))
            job_end(pe.transpose(ps[:, 0:81], rows2[:], ident[0:81, 0:81]), ("cols", 2))
            pe.wait_ge(x_landed, 16)
            for cch in range(DC):
                ps = job_start(pe, ("x", cch))
                for t in range(TT):
                    ins = pe.transpose(ps[:, t * P:(t + 1) * P], x_tok[:, t, cch * P:(cch + 1) * P], ident[:])
                job_end(ins, ("x", cch))
            sum_squares(0)
            ps = job_start(pe, ("ada0",))
            pe.wait_ge(ada_summed, 1)
            for j in range(2 * ADA_FIRST):
                ins = pe.matmul(ps[:, j:j + 1], chunk(ada_acc0, j), ones[:, 0:1], start=True, stop=True)
            job_end(ins, ("ada0",))
            ffn_up(0)
            ffn_down(0)
            post_sum(0)
            sum_squares(1)
            mixer()
            post_sum(1)
            sum_squares(2)
            ffn_up(1)
            ffn_down(1)
            post_sum(2)
            for cch in range(DC):
                pe.wait_ge(h_ready, 2 * DC + cch + 1)
                ps = job_start(pe, ("out", cch))
                for t in range(TT):
                    ins = pe.transpose(ps[:, t * P:(t + 1) * P], h[:, cch, t * P:(t + 1) * P], ident[:])
                job_end(ins, ("out", cch))


_INS = ['x', 'c', 'w_ada', 'b_ada', 'norm_gains', 'ffn_wg', 'ffn_wu', 'ffn_wd', 'w_in', 'mlstm_conv_w', 'mlstm_conv_b', 'mlstm_gate_b', 'mlstm_head_gain', 'cmp_pe', 'cmp_w1', 'cmp_b1', 'cmp_w2', 'cmp_b2', 'w_up_mlstm', 'w_up_nsa', 'w_out']
_OUTS = [((1, 512, 1024), 'float32')]


def kernel(**inputs):
    import numpy as _np
    import concourse.bacc as _bacc
    from concourse import mybir as _mybir
    from concourse.bass_utils import run_bass_kernel_spmd as _run

    nc = _bacc.Bacc("TRN2", target_bir_lowering=False, num_devices=1)
    arrays, args = {}, []
    for name in _INS:
        a = _np.ascontiguousarray(inputs[name])
        if a.dtype.kind in "iu":
            a = a.astype(_np.int64)
        arrays[f"in_{name}_dram"] = a
        args.append(nc.dram_tensor(f"in_{name}_dram", a.shape, _mybir.dt.from_np(a.dtype), kind="ExternalInput").ap())
    for i, (shape, dtype) in enumerate(_OUTS):
        dt = _mybir.dt.from_np(_np.dtype(dtype))
        args.append(nc.dram_tensor(f"out_{i}_dram", shape, dt, kind="ExternalOutput").ap())
    build_layer(nc, *args)
    r = _run(nc, [arrays], core_ids=[0])
    got = tuple(r.results[0][f"out_{i}_dram"] for i in range(len(_OUTS)))
    return got[0]
```

```python
import concourse.bass as bass
from concourse import mybir
from contextlib import ExitStack

F32 = mybir.dt.float32
F32R = mybir.dt.float32r
BF16 = mybir.dt.bfloat16
ALU = mybir.AluOpType
ACT = mybir.ActivationFunctionType
AX = mybir.AxisListType

P = 128
T = 512
TT = T // P
D = 1024
DC = D // P
FF = 2816
FC = FF // P
COLS = 256
UP_ITERS = FF // COLS
DOWN_UNITS = 3
DOWN_K = (0, 8, 16, FC)
EPS_SUM = 1e-6 * D
ROOT_D = float(D) ** 0.5
NEG = -1.0e30
ADA_FIRST = 8

MH, MD = 4, 128
NH, ND, NG, HG = 8, 64, 2, 4
NCMP = 31
CB = 32
WINDOW = 256
GATE_N = 3 * NH
OFF_Q, OFF_K, OFF_V, OFF_O, OFF_IF = 0, 512, 1024, 1536, 2048
OFF_QN = 2056
OFF_KC, OFF_VC, OFF_KS, OFF_VS, OFF_KW, OFF_VW = (2568 + 128 * j for j in range(6))
OFF_GN, OFF_GA, OFF_GB = 3336, 3360, 4384


class Count:

    def __init__(self, sem):
        self.sem, self.n, self.off, self.mark = sem, 0, 0, 0

    def tick(self, ins):
        ins.then_inc(self.sem, 1)
        self.n += 1
        return self.n

    def wait(self, eng, n=None):
        eng.wait_ge(self.sem, (self.n if n is None else n) + self.off)

    def begin(self, i, stride):
        self.mark, self.off, self.stride = self.n, i * stride, stride

    def end(self, iters):
        assert self.n - self.mark == self.stride, (self.n, self.mark)
        self.n, self.off = self.mark + self.stride * iters, 0


class Plan:

    def __init__(self):
        self.bank_count = [0] * 8
        self.jobs = {}
        self.landed_count = [0, 0]
        self.raw_count = 0
        self.raws = {}
        self.weight_count = 0
        self.weights = {}

    def job(self, name, bank):
        assert name not in self.jobs, name
        self.jobs[name] = (bank, self.bank_count[bank], 0)
        self.bank_count[bank] += 1

    def loop_jobs(self, iters, body):
        before = list(self.bank_count)
        for name, bank in body:
            self.job(name, bank)
        step = [a - b for a, b in zip(self.bank_count, before)]
        for name, bank in body:
            self.jobs[name] = self.jobs[name][:2] + (step[bank],)
        self.bank_count = [b + s * iters for b, s in zip(before, step)]

    def unit(self, name, dmas=1):
        slot = self.raw_count % 2
        self.landed_count[slot] += 16 * dmas
        self.raws[name] = (slot, self.landed_count[slot], 0)
        self.raw_count += 1
        if name[0] != "ada":
            self.weights[name] = (self.weight_count, 0)
            self.weight_count += 1

    def loop_units(self, iters, body):
        before, w0, r0 = list(self.landed_count), self.weight_count, self.raw_count
        for name in body:
            self.unit(name)
        step = [a - b for a, b in zip(self.landed_count, before)]
        wstep = self.weight_count - w0
        assert (self.raw_count - r0) % 2 == 0 and wstep % 2 == 0
        for name in body:
            slot, value, _ = self.raws[name]
            self.raws[name] = (slot, value, step[slot])
            if name in self.weights:
                self.weights[name] = (self.weights[name][0], wstep)
        self.landed_count = [b + s * iters for b, s in zip(before, step)]
        self.weight_count = w0 + wstep * iters
        self.raw_count = r0 + (self.raw_count - r0) * iters


def build_layer(nc, x, c, w_ada, b_ada, norm_gains, ffn_wg, ffn_wu, ffn_wd, w_in, mlstm_conv_w, mlstm_conv_b,
                mlstm_gate_b, mlstm_head_gain, cmp_pe, cmp_w1, cmp_b1, cmp_w2, cmp_b2, w_up_mlstm, w_up_nsa,
                w_out, out):
    with ExitStack() as ctx:
        base = nc.sbuf_base + (-nc.sbuf_base) % 32
        at = [base]

        def sem(name):
            return ctx.enter_context(nc.semaphore(name))

        def place(name, shape, dt, offset=None):
            size = mybir.dt.size(dt)
            for n in shape[1:]:
                size *= n
            size += -size % 32
            if offset is None:
                offset = at[0]
                at[0] += size
            return nc.alloc_sbuf_tensor_at(name, shape, dt, offset=offset), offset + size

        h, _ = place("h", [P, DC, T], F32)
        u_at = at[0]
        u_hi, _ = place("u_hi", [P, DC, T], F32R)
        u_lo_at = at[0]
        u_lo, _ = place("u_lo", [P, DC, T], F32R)
        raw = [place(f"raw{s}", [P, DC * COLS], F32)[0] for s in range(2)]
        w_hi = [place(f"w_hi{s}", [P, DC * COLS], F32R)[0] for s in range(2)]
        w_lo = [place(f"w_lo{s}", [P, DC * COLS], F32R)[0] for s in range(2)]
        ident, _ = place("ident", [P, P], F32)
        ones, _ = place("ones", [P, P], F32)
        col1, _ = place("col1", [P, 120], F32)
        col2, _ = place("col2", [P, 81], F32)
        ada, _ = place("ada", [P, 9 * DC], F32)
        eps_col, _ = place("eps_col", [P, 1], F32)
        silu_c, _ = place("silu_c", [P, DC], F32)
        gain_a, _ = place("gain_a", [P, DC], F32)
        gain_g, _ = place("gain_g", [P, DC], F32)
        sq_at = at[0]
        sq = [place(f"sq{s}", [P, T], F32)[0] for s in range(2)]
        wt_at = at[0]
        wt = [place(f"wt{s}", [P, T], F32)[0] for s in range(2)]
        rs_at = at[0]
        rs, _ = place("rs", [P, T], F32)
        root_t, _ = place("root_t", [P, TT], F32)
        inv_t, _ = place("inv_t", [P, TT], F32)
        warm, _ = place("warm", [P, 1], F32)
        region = at[0]

        mid_hi, e = place("mid_hi", [P, FC, T], F32R, region)
        mid_lo, e = place("mid_lo", [P, FC, T], F32R, e)
        ada_acc, e = place("ada_acc", [P, 2, COLS], F32, e)
        ffn_end = e
        y_ffn, _ = place("y_ffn", [P, DC, T], F32, u_lo_at)
        ada_w, e = place("ada_w", [P, DC, ADA_FIRST * COLS], F32, region)
        x_tok, e = place("x_tok", [P, TT, D], F32, e)
        ada_acc0, e = place("ada_acc0", [P, ADA_FIRST * COLS], F32, e)
        c_col, e = place("c_col", [P, DC], F32, e)
        rows1, e = place("rows1", [120, P], F32, e)
        rows2, e = place("rows2", [81, P], F32, e)
        first_end = e
        out_tok, _ = place("out_tok", [P, TT, D], F32, region)

        qkc, e = place("qkc", [P, 2 * MH, T], F32, region)
        sig_o, e = place("sig_o", [P, MH, T], F32, e)
        v_aug, e = place("v_aug", [P, TT, MH, MD + 1], F32, e)
        p_m, e = place("p_m", [P, TT, T], F32, e)
        o_acc, a = place("o_acc", [P, TT, NH * ND], F32, region)
        p_s, a = zip(*[place(f"p_s{n}", [P, T], F32, a + 2048 * n) for n in range(2)])
        p_w, a = zip(*[place(f"p_w{n}", [P, 384], F32, a[1] + 1536 * n) for n in range(2)])
        pt_s, a = zip(*[place(f"pt_s{n}", [P, T], F32, a[1] + 2048 * n) for n in range(2)])
        pt_w, a = zip(*[place(f"pt_w{n}", [P, 384], F32, a[1] + 1536 * n) for n in range(2)])
        sig_b, a = place("sig_b", [P, DC, T], F32, a[1])
        assert a <= e
        hm_hi, a = place("hm_hi", [P, MH, T], F32R, region)
        hm_lo, a = place("hm_lo", [P, MH, T], F32R, a)
        hm, e = place("hm", [P, MH, T], F32, e)
        qn_at = e
        qn, e = place("qn", [P, 4, T], F32, e)
        ksw, e = place("ksw", [P, 2, T], F32, e)
        vsw, e = place("vsw", [P, TT, 2, P], F32, e)
        o_hi, a = place("o_hi", [P, 4, T], F32R, qn_at)
        o_lo, a = place("o_lo", [P, 4, T], F32R, a)
        assert a <= e
        sig_a_at = e
        sig_a, e = place("sig_a", [P, DC, T], F32, e)
        y_mix, _ = place("y_mix", [P, DC, T], F32, sig_a_at)
        late_at = e
        kv_2, a = place("kv_2", [P, 2, NG, T // 2], F32, sig_a_at)
        blk, a = place("blk", [P, 16, NG, 32], F32, a)
        blk_hi, a = place("blk_hi", [P, 16, NG, 32], F32R, a)
        kv_t, _ = place("kv_t", [P, 2, 2, T // 2], F32, a)
        blk_lo, a = place("blk_lo", [P, 16, NG, 32], F32R, a)
        assert a <= late_at
        row_i, a = place("row_i", [MH, T], F32, late_at)
        row_f, a = place("row_f", [MH, T], F32, a)
        row_t, a = place("row_t", [MH, T], F32, a)
        row_z, a = place("row_z", [MH, T], F32, a)
        row_s, late = place("row_s", [MH, T], F32, a)
        row_m, _ = place("row_m", [MH, T], F32, rs_at)
        v_bd, a = place("v_bd", [P, NG, HG, ND], F32, late_at)
        p_c, a = place("p_c", [P, NH, 32], F32, a)
        pt_c, a = place("pt_c", [P, NG, P], F32, a)
        hid_rep, a = place("hid_rep", [P, 2, NG, HG, 32], F32, a)
        o_tmp, a = place("o_tmp", [P, HG, 2, ND], F32, a)
        v_tmp, a = place("v_tmp", [P, NG, ND], F32, a)
        hid, a = place("hid", [P, 2, 2, 64], F32, a)
        assert a <= late
        w2, late = place("w2", [P, 2, 2, ND], F32, late)
        k_cmp, late = place("k_cmp", [P, 32], F32, late)
        b2_row, late = place("b2_row", [P, ND], F32, late)
        mask_row, late = place("mask_row", [P, T], F32, late)
        add_c, late = place("add_c", [P, TT, 32], F32, late)
        keep_c, late = place("keep_c", [P, TT, 32], F32, late)
        bd, late = place("bd", [P, HG], F32, late)
        ident_b, late = place("ident_b", [P, P], BF16, late)
        diag_b, late = place("diag_b", [P, P], BF16, late)
        left_b, late = place("left_b", [P, P], BF16, late)
        pick, late = place("pick", [MH, MH, P], F32, late)
        g_bias, late = place("g_bias", [MH, 2], F32, late)
        g_tok, late = place("g_tok", [P, TT, 32], F32, late)
        sig_n, late = place("sig_n", [P, TT, NH, 3], F32, late)
        cols, late = place("cols", [P, 2, TT, MH], F32, late)
        den, late = place("den", [P, MH, TT], F32, late)
        ssm, late = place("ssm", [P, MH, TT], F32, late)
        max_c, late = place("max_c", [P, NH], F32, late)
        sum_c, late = place("sum_c", [P, NH], F32, late)
        n_max, late = place("n_max", [P, 32, 2], F32, late)
        sums, late = place("sums", [P, 32, 2], F32, late)
        w_sw, late = place("w_sw", [P, HG, 2], F32, late)
        eps_m, late = place("eps_m", [P, 1], F32, late)

        PS = ctx.enter_context(nc.psum_tensor("PS", [P, 8, 512], F32))

        bank_full = [sem(f"bank_full{b}") for b in range(8)]
        bank_free = [sem(f"bank_free{b}") for b in range(8)]
        raw_landed = [sem(f"raw_landed{s}") for s in range(2)]
        hi_ready = sem("hi_ready")
        lo_ready = sem("lo_ready")
        w_used = sem("w_used")
        ada_summed = sem("ada_summed")
        consts_ready = sem("consts_ready")
        rows_landed = sem("rows_landed")
        c_landed = sem("c_landed")
        x_landed = sem("x_landed")
        ada_first_landed = [sem(f"ada_first_landed{j}") for j in range(DC)]
        silu_c_ready = sem("silu_c_ready")
        h_ready = [sem("h_even_ready"), sem("h_odd_ready")]
        sq_ready = sem("sq_ready")
        sq_used = sem("sq_used")
        w_scaled = sem("w_scaled")
        u_hi_ready = sem("u_hi_ready")
        u_ready = sem("u_ready")
        mid_hi_ready = sem("mid_hi_ready")
        mid_ready = sem("mid_ready")
        ysum_ready = sem("ysum_ready")
        ysum_used = sem("ysum_used")
        delta_ready = sem("delta_ready")
        diag_ready = sem("diag_ready")
        stored = sem("stored")
        small_landed = sem("small_landed")
        mixer_consts = sem("mixer_consts")
        soft_ready = sem("soft_ready")
        conv_first = sem("conv_first")
        qk_ready = sem("qk_ready")
        m_ready = sem("m_ready")
        em_ready = sem("em_ready")
        arg_ready = sem("arg_ready")
        e_ready = sem("e_ready")
        kv_moved = sem("kv_moved")
        hm_ready = sem("hm_ready")
        gates_ready = sem("gates_ready")
        ssm_root = sem("ssm_root")
        blk_ready = sem("blk_ready")
        blk_hi_ready = sem("blk_hi_ready")
        blk_lo_ready = sem("blk_lo_ready")
        hm_normed = sem("hm_normed")
        hid_rep_ready = sem("hid_rep_ready")
        v_bd_ready = sem("v_bd_ready")
        arg_c_ready = sem("arg_c_ready")
        e_c_ready = sem("e_c_ready")
        p_c_ready = sem("p_c_ready")
        sig_n_ready = sem("sig_n_ready")
        n_max_ready = sem("n_max_ready")
        o_hi_ready = sem("o_hi_ready")
        o_acc_ready = sem("o_acc_ready")
        hm_lo_ready = sem("hm_lo_ready")
        merged = sem("merged")
        dve_step = sem("dve_step")
        act_step = sem("act_step")
        pool_step = sem("pool_step")

        plan = Plan()

        def plan_norm(kind, s):
            plan.job((kind, s), 6)
            plan.job(("r", kind, s), 7)

        plan.job(("cols", 1), 0)
        plan.job(("cols", 2), 1)
        for cch in range(DC):
            plan.job(("x", cch), 2 + cch % 4)
        plan_norm("pre", 0)
        plan.job(("ada0",), 0)

        def has_ada(f, n):
            return n == 2 or (f == 0 and n == 5)

        def ada_number(f, it, n):
            return 2 * UP_ITERS + (2 * it + n // 3 if f == 0 else 4 + it)

        def plan_ffn_up(f):
            plan.unit(("g0", f))
            plan.loop_units(UP_ITERS, [("up", f), ("ada", "a"), ("gate", f), ("ada", "b")] if f == 0
                            else [("up", f), ("gate", f)])
            plan.loop_jobs(UP_ITERS, [(("g", f, 0), 0), (("g", f, 1), 1), (("u", f, 0), 2), (("u", f, 1), 3)]
                           + ([(("ada", "ab"), 7)] if f == 0 else []))

        def plan_ffn_down(f, following):
            for it in range(2):
                for n in range(6):
                    if (it, n) != (0, 0):
                        plan.unit(("d", f, it, n))
                    if has_ada(f, n):
                        plan.unit(("ada", f, it, n))
            for name, dmas in following:
                plan.unit(name, dmas)
            plan.loop_jobs(2, [(("y", f, n), n) for n in range(4)]
                           + [(("ada", f, n), 7) for n in (2, 5) if has_ada(f, n)])

        unit_end = {}

        def plan_unit(name, dmas, jobs, ends=True):
            plan.unit(name, dmas)
            for job, bank in jobs:
                plan.job(job, bank)
            unit_end[name] = jobs[-1][0] if ends else None

        GATES = [("ga", n) for n in range(4)] + [("gb", n) for n in range(4)]
        MIX = ([("qk", 0), ("t0",), ("t1",), ("v", 0), ("v", 1)] + [("qk", n) for n in range(1, 4)]
               + [("kcvc",), ("o", 0), ("o", 1), ("kk",), ("c1", 0, 0), ("c1", 0, 1), ("qn", 0), ("c1", 1, 0), ("c1", 1, 1),
                  ("qn", 1)] + GATES + [("um", 0), ("un", 0), ("um", 1), ("un", 1)] + [("wo", n) for n in range(4)])
        STEPS = [(t, g, hh) for t in range(TT) for g in range(NG) for hh in range(HG)]
        NSA_CHUNKS = 2 * len(GATES) - TT - 2
        chunk_at = {}
        for n in range(NSA_CHUNKS):
            chunk_at[n * len(STEPS) // NSA_CHUNKS] = TT + n

        def gate_job(cch):
            return GATES[cch // 2][0:1] + (cch % DC,)

        def plan_head(hd):
            plan.job(("negM", hd), 4)
            for j in range(TT):
                plan.job(("S", hd, j), j)

        def plan_values(hd):
            plan.job(("num", hd, 0), 6)
            plan.job(("num", hd, 1), 5)

        def plan_mixer():
            plan_unit(("qk", 0), 1, [(("qk", 0), 2), (("qk", 1), 3)])
            plan_unit(("t0",), 3, [(("t0", 0), 0), (("t0", 1), 1)])
            plan_unit(("t1",), 1, [(("t1",), 4)])
            plan_unit(("v", 0), 1, [(("v", 0, 0), 5), (("v", 0, 1), 6)])
            plan_unit(("v", 1), 1, [(("v", 1, 0), 2), (("v", 1, 1), 3)])
            plan.job(("ifT", 0), 0)
            plan.job(("ifT", 1), 1)
            for n in range(1, 4):
                plan_unit(("qk", n), 1, [(("qk", 2 * n), 2 + 2 * n % 4), (("qk", 2 * n + 1), 2 + (2 * n + 1) % 4)])
            plan_unit(("kcvc",), 1, [(("kcvc", "a"), 4), (("kcvc", "b"), 7)])
            plan_unit(("o", 0), 1, [(("o", 0), 5), (("o", 1), 6)])
            plan.job(("colT",), 0)
            plan_head(0)
            plan_unit(("o", 1), 1, [(("o", 2), 7), (("o", 3), 5)])
            plan_values(0)
            plan_head(1)
            plan_unit(("kk",), 2, [(("kk", "a"), 7), (("kk", "b"), 5)])
            plan_values(1)
            plan_head(2)
            plan_unit(("c1", 0, 0), 1, [(("hid", 0), 7)], ends=False)
            plan.unit(("c1", 0, 1))
            unit_end[("c1", 0, 1)] = ("hid", 0)
            plan_values(2)
            plan_head(3)
            plan_unit(("qn", 0), 4, [(("qn", 0, "a"), 7), (("qn", 0, "b"), 5)])
            plan_values(3)
            plan_unit(("c1", 1, 0), 1, [(("hid", 1), 7)], ends=False)
            plan.unit(("c1", 1, 1))
            unit_end[("c1", 1, 1)] = ("hid", 1)
            plan.job(("kcmp",), 4)
            plan_unit(("qn", 1), 4, [(("qn", 1, "a"), 7), (("qn", 1, "b"), 5)])
            for hd in range(MH):
                plan.job(("hT", hd), hd)
            plan.job(("vcmp",), 6)
            for t in range(TT):
                plan.job(("sc", t, 0), 2 * (t % 2))
                plan.job(("sc", t, 1), 2 * (t % 2) + 1)
                plan.job(("pcT", t), 4 + t % 2)
                plan.job(("oc", t), 6)
            for s, (t, g, hh) in enumerate(STEPS):
                plan.job(("ss", s), 2 * (s % 2))
                plan.job(("sw", s), 2 * (s % 2) + 1)
                plan.job(("ts", s), 4)
                plan.job(("tw", s), 5)
                if hh == 0:
                    plan.job(("o_nsa", t, g), 6)
            for n, name in enumerate(GATES):
                plan_unit(name, 1, [(gate_job(2 * n), 7), (gate_job(2 * n + 1), 7 if n < len(GATES) - 1 else 6)])
            for fc in range(4):
                plan.job(("oT", fc), fc)
            for j in range(2):
                plan_unit(("um", j), 1, [(("ym", 4 * j + n), n) for n in range(4)])
                plan_unit(("un", j), 1, [(("yn", 4 * j + n), 4 + n) for n in range(4)])
            for n in range(4):
                plan_unit(("wo", n), 1, [(("y1", 2 * n), 2 * (n % 2)), (("y1", 2 * n + 1), 2 * (n % 2) + 1)])
            plan_norm("post", 1)

        plan_ffn_up(0)
        plan_ffn_down(0, [])
        plan_norm("post", 0)
        plan_norm("pre", 1)
        plan_mixer()
        plan_norm("pre", 2)
        plan_ffn_up(1)
        plan_ffn_down(1, [])
        plan_norm("post", 2)
        for cch in range(DC):
            plan.job(("out", cch), 2 + cch % 4)
        assert [n for n in plan.weights if n in MIX] == MIX

        def after(name):
            n = MIX.index(name) + 1
            return MIX[n] if n < len(MIX) else ("g0", 1)

        def blocks_of(t):
            return range(0, t + 1), range(max(0, t - WINDOW // P), t + 1)

        def job_start(eng, name, i=0):
            bank, k, step = plan.jobs[name]
            eng.wait_ge(bank_free[bank], k + 1 + i * step)
            return PS[:, bank, :]

        def job_end(ins, name):
            ins.then_inc(bank_full[plan.jobs[name][0]], 1)

        def job_result(eng, name, i=0):
            bank, k, step = plan.jobs[name]
            eng.wait_ge(bank_full[bank], k + 1 + i * step)
            return PS[:, bank, :]

        def job_read(ins, name):
            ins.then_inc(bank_free[plan.jobs[name][0]], 1)

        job_done = job_result
        mixer_used = 2

        def taken(eng, name, i=0, before=0):
            bank, k, step = plan.jobs[name]
            eng.wait_ge(bank_free[bank], k + 2 - before + i * step)

        def unit_landed(eng, name, i=0):
            slot, value, step = plan.raws[name]
            eng.wait_ge(raw_landed[slot], value + i * step)
            return raw[slot]

        def w_number(name, i=0):
            n, step = plan.weights[name]
            return n + 1 + i * step, n % 2

        def h_updated(eng, adds, cch):
            eng.wait_ge(h_ready[cch % 2], adds * DC // 2 + cch // 2 + 1)

        def bcast(ap, shape):
            return ap.broadcast_to(shape)

        def chunk(t, j):
            return t[:, j * P:(j + 1) * P]

        block = ctx.enter_context(nc.Block())

        dve_misc = sem("dve_misc")
        @block.sync
        def _(sp):
            sp.dma_start(c_col[:], c.rearrange("b (p j) -> p (b j)", j=DC)).then_inc(c_landed, 16)
            sp.dma_start(x_tok[:], x[0].rearrange("(t p) d -> p t d", p=P)).then_inc(x_landed, 16)
            sp.dma_start(rows1[0:72, :], b_ada.rearrange("l (r n) -> (l r) n", n=P)).then_inc(rows_landed, 16)
            sp.dma_start(rows1[72:120, :], norm_gains.rearrange("l g (r n) -> (l g r) n", n=P)).then_inc(rows_landed, 16)
            sp.dma_start(rows2[0:32, :], mlstm_conv_w.rearrange("l w o (r n) -> (l w o r) n", n=P)).then_inc(rows_landed, 16)
            sp.dma_start(rows2[32:40, :], mlstm_conv_b.rearrange("l (r n) -> (l r) n", n=P)).then_inc(rows_landed, 16)
            sp.dma_start(rows2[40:44, :], mlstm_head_gain.rearrange("l (r n) -> (l r) n", n=P)).then_inc(rows_landed, 16)
            sp.dma_start(rows2[44:48, :], cmp_b1.rearrange("l k (r n) -> (l k r) n", n=P)).then_inc(rows_landed, 16)
            sp.dma_start(rows2[48:80, :], cmp_pe.rearrange("l k (r a) n -> (l k r) (a n)", a=2)).then_inc(rows_landed, 16)
            sp.dma_start(rows2[80:81, 0:ND], cmp_b2[:, 0, :]).then_inc(rows_landed, 16)
            sp.dma_start(rows2[80:81, ND:P], cmp_b2[:, 0, :]).then_inc(rows_landed, 16)
            ada_rows = w_ada[0].rearrange("(p j) n -> p j n", j=DC)

            def load_first_ada(j):
                sp.dma_start(ada_w[:, j, :], ada_rows[:, j, 0:ADA_FIRST * COLS]).then_inc(ada_first_landed[j], 16)

            for j in range(DC // 2):
                load_first_ada(j)

            last = {0: None, 1: None}

            def slot_empty(name):
                slot = plan.raws[name][0]
                if last[slot] is not None:
                    sp.wait_ge(*last[slot])
                return slot

            def load(name, pieces):
                slot = slot_empty(name)
                for dst, src in pieces:
                    sp.dma_start(raw[slot][:, dst[0]:dst[1]].rearrange("p (k n) -> p k n", n=dst[2]), src).then_inc(raw_landed[slot], 16)
                if name[0] == "ada":
                    ada_seen[0] += 1
                    last[slot] = (ada_summed, ada_seen[0])
                else:
                    last[slot] = (lo_ready, w_number(name)[0])

            ada_seen = [1]

            def rows_of(w, r0, r1, c0, cn):
                return w[r0 * P:r1 * P, bass.ds(c0, cn)].rearrange("(k p) n -> p k n", p=P)

            def dense(kn, n):
                return (0, kn * n, n)

            def ada_src(a):
                return ada_rows[:, :, bass.ds(a * COLS, COLS)]

            def load_ffn_up(f):
                load(("g0", f), [(dense(DC, COLS), rows_of(ffn_wg[0, f], 0, DC, 0, COLS))])
                if f == 0:
                    for j in range(DC // 2, DC):
                        load_first_ada(j)
                wslot = plan.raws[("up", f)][0]
                gslot = plan.raws[("gate", f)][0]
                g_n = w_number(("g0", f))[0]

                def raw3(slot):
                    return raw[slot][:].rearrange("p (k n) -> p k n", n=COLS)

                def iteration(i, last_one):
                    sp.wait_ge(lo_ready, g_n + 2 * i - f)
                    sp.dma_start(raw3(wslot), rows_of(ffn_wu[0, f], 0, DC, i * COLS, COLS)).then_inc(raw_landed[wslot], 16)
                    if f == 0:
                        aslot = plan.raws[("ada", "a")][0]
                        sp.wait_ge(ada_summed, 2 * i + 1)
                        sp.dma_start(raw3(aslot), ada_src(ADA_FIRST + 2 * i)).then_inc(raw_landed[aslot], 16)
                        sp.wait_ge(lo_ready, g_n + 1 + 2 * i)
                    else:
                        sp.wait_ge(lo_ready, g_n + 2 * i)
                    src = rows_of(ffn_wd[0, f], DOWN_K[0], DOWN_K[1], 0, COLS) if last_one else \
                        rows_of(ffn_wg[0, f], 0, DC, i * COLS + COLS, COLS)
                    sp.dma_start(raw3(gslot), src).then_inc(raw_landed[gslot], 16)
                    if f == 0:
                        sp.wait_ge(ada_summed, 2 * i + 2)
                        sp.dma_start(raw3(aslot), ada_src(ADA_FIRST + 1 + 2 * i)).then_inc(raw_landed[aslot], 16)

                with sp.Fori(0, UP_ITERS - 1) as i:
                    iteration(i, False)
                iteration(UP_ITERS - 1, True)
                n_last = g_n + 2 * UP_ITERS
                if f == 0:
                    ada_seen[0] = 1 + 2 * UP_ITERS
                    last[gslot] = (lo_ready, n_last)
                    last[1 - gslot] = (ada_summed, ada_seen[0])
                else:
                    last[gslot] = (lo_ready, n_last)
                    last[1 - gslot] = (lo_ready, n_last - 1)

            def load_ffn_down(f):
                for it in range(2):
                    for n in range(6):
                        if (it, n) != (0, 0):
                            k0, k1 = DOWN_K[n % 3], DOWN_K[n % 3 + 1]
                            c0 = (2 * it + n // 3) * COLS
                            load(("d", f, it, n), [(dense(k1 - k0, COLS), rows_of(ffn_wd[0, f], k0, k1, c0, COLS))])
                        if has_ada(f, n):
                            load(("ada", f, it, n), [(dense(DC, COLS), ada_src(ADA_FIRST + ada_number(f, it, n)))])

            def load_mixer():
                w3 = w_in[0].rearrange("(k p) n -> p k n", p=P)

                def columns(c0, cn):
                    return w3[:, :, c0:c0 + cn]

                def load_parts(name, n, parts):
                    slot = slot_empty(name)
                    for view, src in parts(raw[slot]):
                        sp.dma_start(view, src).then_inc(raw_landed[slot], 16)
                    last[slot] = (lo_ready, w_number(name)[0])

                def t0_parts(slot):
                    s3 = slot[:, 0:DC * 160].rearrange("p (k n) -> p k n", n=160)
                    return [(s3[:, :, 0:8], columns(OFF_IF, 8)), (s3[:, :, 8:32], columns(OFF_GN, GATE_N)),
                            (s3[:, :, 32:160], columns(OFF_VS, P))]

                def kk_parts(slot):
                    s3 = slot[:].rearrange("p (k n) -> p k n", n=COLS)
                    return [(s3[:, :, 0:P], columns(OFF_KS, P)), (s3[:, :, P:COLS], columns(OFF_KW, P))]

                def qn_parts(n):
                    def parts(slot):
                        s3 = slot[:].rearrange("p (k n) -> p k n", n=COLS)
                        return [(s3[:, :, (2 * cc + g) * ND:(2 * cc + g + 1) * ND],
                                 columns(OFF_QN + (g * HG + 2 * n + cc) * ND, ND)) for cc in range(2) for g in range(NG)]
                    return parts

                load(("qk", 0), [(dense(DC, COLS), columns(OFF_Q, COLS))])
                load_parts(("t0",), 160, t0_parts)
                load(("t1",), [(dense(DC, P), columns(OFF_VW, P))])
                job_done(sp, ("y", 0, 3), 1)
                for kv in range(2):
                    sp.dma_start(w2[:, kv, :, :], cmp_w2[0, kv].rearrange("(h p) e -> p h e", p=P)).then_inc(small_landed, 16)
                sp.dma_start(b2_row[:], cmp_b2[0, 1:2, :].broadcast_to([P, ND])).then_inc(small_landed, 16)
                for a in range(2):
                    sp.dma_start(g_bias[:, a:a + 1], mlstm_gate_b[0, a * MH:(a + 1) * MH].rearrange("(p o) -> p o", o=1)).then_inc(small_landed, 16)
                for n in range(2):
                    load(("v", n), [(dense(DC, COLS), columns(OFF_V + n * COLS, COLS))])
                for n in range(1, 4):
                    load(("qk", n), [(dense(DC, COLS), columns(OFF_Q + n * COLS, COLS))])
                load(("kcvc",), [(dense(DC, COLS), columns(OFF_KC, COLS))])
                for n in range(2):
                    load(("o", n), [(dense(DC, COLS), columns(OFF_O + n * COLS, COLS))])
                load_parts(("kk",), COLS, kk_parts)
                for kv in range(2):
                    for a in range(2):
                        load(("c1", kv, a), [(dense(DC, COLS), rows_of(cmp_w1[0, kv], a * DC, (a + 1) * DC, 0, COLS))])
                    load_parts(("qn", kv), COLS, qn_parts(kv))
                for name, off in (("ga", OFF_GA), ("gb", OFF_GB)):
                    for n in range(4):
                        load((name, n), [(dense(DC, COLS), columns(off + n * COLS, COLS))])
                for j in range(2):
                    load(("um", j), [(dense(4, T), rows_of(w_up_mlstm[0], 0, 4, j * T, T))])
                    load(("un", j), [(dense(4, T), rows_of(w_up_nsa[0], 0, 4, j * T, T))])
                for n in range(4):
                    load(("wo", n), [(dense(DC, COLS), rows_of(w_out[0], 0, DC, n * COLS, COLS))])

            load_ffn_up(0)
            load_ffn_down(0)
            load_mixer()
            load_ffn_up(1)
            load_ffn_down(1)
            out3 = out[0].rearrange("(t p) d -> p t d", p=P)
            for cch in range(1, DC, 2):
                at_ = slice((cch - 1) * P, (cch + 1) * P)
                taken(sp, ("out", cch - 1))
                taken(sp, ("out", cch))
                sp.dma_start(out3[:, :, at_], out_tok[:, :, at_]).then_inc(stored, 16)
            sp.wait_ge(stored, 16 * DC // 2)

        @block.gpsimd
        def _(pool):
            step = Count(pool_step)
            step.tick(pool.memset(ident[:], 0.0))
            step.tick(pool.memset(ones[:], 1.0))
            step.tick(pool.memset(eps_col[:], EPS_SUM))
            step.wait(pool)
            for b in range(8):
                pool.sem_inc(bank_free[b], 1)
            pool.affine_select(out=ident[:], in_=ident[:], compare_op=ALU.not_equal, fill=1.0, base=0,
                               pattern=[[-1, P]], channel_multiplier=1).then_inc(consts_ready, 1)

            def sum_y_squares(sums, y_job):
                for cch in range(DC - 2):
                    n = sums * (DC - 2) + cch + 1
                    taken(pool, *y_job(cch))
                    if cch == 0:
                        ins = pool.tensor_copy(rs[:], sq[cch % 2][:])
                    else:
                        pool.wait_ge(ysum_ready, n - 1)
                        ins = pool.tensor_tensor(rs[:], rs[:], sq[cch % 2][:], ALU.add)
                    ins.then_inc(ysum_ready, 1)

            def add_to_h(adds):
                for cch in range(1, DC, 2):
                    pool.wait_ge(delta_ready, adds * DC + cch + 1)
                    pool.tensor_tensor(h[:, cch, :], h[:, cch, :], wt[1][:], ALU.add).then_inc(h_ready[1], 1)

            def ffn_y(f):
                return lambda cch: (("y", f, cch % 4), cch // 4)

            def mixer_constants():
                for dst, value in ((mask_row, 0.0), (add_c, 0.0), (keep_c, 1.0), (bd, 0.0), (diag_b, 0.0), (left_b, 0.0),
                                   (pick, 0.0), (row_z, 0.0), (blk, 0.0), (v_aug, 1.0), (eps_m, 1e-6)):
                    step.tick(pool.memset(dst[:], value))
                step.wait(pool)
                step.tick(pool.affine_select(out=mask_row[:, 0:P], in_=mask_row[:, 0:P], compare_op=ALU.is_ge, fill=NEG,
                                             base=0, pattern=[[1, P]], channel_multiplier=-1))
                step.tick(pool.affine_select(out=diag_b[:], in_=diag_b[:], compare_op=ALU.is_ge, fill=NEG, base=0,
                                             pattern=[[-1, P]], channel_multiplier=1))
                step.tick(pool.affine_select(out=left_b[:], in_=left_b[:], compare_op=ALU.is_gt, fill=NEG, base=0,
                                             pattern=[[1, P]], channel_multiplier=-1))
                for dst, fill in ((add_c, NEG), (keep_c, 0.0)):
                    step.tick(pool.affine_select(out=dst[:], in_=dst[:], compare_op=ALU.is_ge, fill=fill, base=-(CB - 1),
                                                 pattern=[[P, TT], [-CB // 2, 32]], channel_multiplier=1))
                step.wait(pool)
                step.tick(pool.memset(add_c[:, :, 31:32], NEG))
                step.tick(pool.memset(keep_c[:, :, 31:32], 0.0))
                for n in range(HG):
                    step.wait(pool)
                    step.tick(pool.memset(bd[32 * n:32 * n + 32, n:n + 1], 1.0))
                step.wait(pool)
                step.tick(pool.affine_select(out=pick[:], in_=pick[:], compare_op=ALU.not_equal, fill=-1.0, base=0,
                                             pattern=[[-1, MH], [0, P]], channel_multiplier=1))
                step.tick(pool.tensor_copy(ident_b[:], ident[:]))
                step.wait(pool)
                pool.sem_inc(mixer_consts, 1)

            def compression_blocks():
                pool.wait_ge(kv_moved, 64)
                for kv in range(2):
                    if kv:
                        pool.wait_ge(blk_hi_ready, kv)
                    for a in range(2):
                        src = kv_2[:, kv, :, 8 * a:8 * a + 8 * NCMP].rearrange("p g (n l) -> p l g n", l=8)
                        pe_at = 48 + 16 * kv + 8 * a
                        pe = bcast(col2[:, pe_at:pe_at + 8].unsqueeze(2).unsqueeze(3), [P, 8, NG, NCMP])
                        step.tick(pool.tensor_tensor(blk[:, 8 * a:8 * a + 8, :, 0:NCMP], src, pe, ALU.add))
                    step.wait(pool)
                    pool.sem_inc(blk_ready, 1)
                    pool.wait_ge(blk_hi_ready, kv + 1)
                    if kv:
                        job_done(pool, ("hid", 0))
                    pool.tensor_tensor(blk_lo[:], blk[:], blk_hi[:].bitcast(F32), ALU.subtract).then_inc(blk_lo_ready, 1)
                    pool.wait_ge(blk_lo_ready, kv + 1)

            sum_y_squares(0, ffn_y(0))
            add_to_h(0)
            mixer_constants()
            compression_blocks()
            sum_y_squares(1, lambda cch: (("y1", cch),))
            add_to_h(1)
            sum_y_squares(2, ffn_y(1))
            add_to_h(2)

        @block.scalar
        def _(act):
            step = Count(act_step)

            def split_high(name, i=0, used=None, size=DC * COLS):
                n, slot = w_number(name, i)
                src = unit_landed(act, name, i)
                if used is not None:
                    act.wait_ge(w_used, used)
                act.activation(w_hi[slot][:, 0:size], src[:, 0:size], ACT.Copy).then_inc(hi_ready, 1)

            def pre_norm_squares(s):
                for cch in range(DC):
                    h_updated(act, s - 1, cch)
                    if cch >= 2:
                        act.wait_ge(sq_used, s * (DC - 1) + cch - 1)
                    act.activation(sq[cch % 2][:], h[:, cch, :], ACT.Square).then_inc(sq_ready, 1)

            def root(job):
                src = job_result(act, job)
                job_read(act.activation(root_t[:], src[:, 0:TT], ACT.Sqrt, bias=eps_col[:, 0:1]), job)

            def load_table(func):
                step.tick(act.activation(warm[:], eps_col[:], func))

            def modulate_high(s):
                shift = s * 3 * DC
                for cch in range(DC):
                    act.wait_ge(w_scaled, s * DC + cch + 1)
                    act.activation(u_hi[:, cch, :], wt[cch % 2][:], ACT.Identity,
                                   bias=ada[:, shift + cch:shift + cch + 1]).then_inc(u_hi_ready, 1)

            def ffn_up(f):
                with act.Fori(0, UP_ITERS) as i:
                    act.activation(warm[:], eps_col[:], ACT.Silu)
                    split_high(("up", f), i)
                    for j in range(2):
                        src = job_result(act, ("g", f, j), i)
                        taken(act, ("u", f, j), i, before=1)
                        job_read(act.activation(sq[j][:], src, ACT.Silu), ("g", f, j))
                    split_high(("gate", f), i)
                    for j in range(2):
                        taken(act, ("u", f, j), i)
                        act.activation(mid_hi[:, bass.ds(2 * i + j, 1), :], wt[j][:].rearrange("p (a t) -> p a t", a=1),
                                       ACT.Copy).then_inc(mid_hi_ready, 1)

            def take_y(job, sums, cch, y):
                src = job_result(act, job[0], job[1])
                if cch == 0 and sums != 1:
                    act.wait_ge(mid_ready, (sums // 2 + 1) * FC)
                act.activation(y[:, cch, :], src, ACT.Copy)
                if cch >= 2:
                    act.wait_ge(ysum_ready, sums * (DC - 2) + cch - 1)
                job_read(act.activation(sq[cch % 2][:], src, ACT.Square), job[0])

            def ffn_down(f, sums, y, next_name):
                load_table(ACT.Sqrt)
                for it in range(2):
                    for n in range(6):
                        if (it, n) != (1, 5):
                            nxt = ("d", f, it, n + 1) if n < 5 else ("d", f, 1, 0)
                            kk = (n + 1) % 3
                            used = None if n % 3 == 0 else f * 8 + mixer_used * f + it * 4 + n - n // 3
                            split_high(nxt, 0, used, (DOWN_K[kk + 1] - DOWN_K[kk]) * COLS)
                        elif next_name is not None:
                            split_high(next_name, used=8)
                        if n % 3 == 2:
                            for j in range(2):
                                name = ("y", f, n // 3 * 2 + j)
                                take_y((name, it), sums, (it * 2 + n // 3) * 2 + j, y)

            def split_after(name):
                n = MIX.index(name)
                if n:
                    before = MIX[n - 1]
                    if unit_end[before] is not None:
                        job_done(act, unit_end[before])
                        used = None
                    else:
                        used = 8 + 1 + before[1]
                else:
                    used = None
                size = 160 * DC if after(name) == ("t0",) else P * DC if after(name) == ("t1",) else DC * COLS
                split_high(after(name), 0, used=used, size=size)

            def copy_out(job, dst, scale=None):
                src = job_result(act, job)
                return job_read(act.activation(dst, src, ACT.Copy) if scale is None else
                                act.activation(dst, src, ACT.Copy, scale=scale), job)

            def conv_unit(n):
                split_after(("qk", n))
                for j in range(2):
                    cch = 2 * n + j
                    src = job_result(act, ("qk", cch))
                    act.activation(qkc[:, cch, :], src, ACT.Identity, bias=col2[:, 32 + cch:33 + cch],
                                   scale=col2[:, 24 + cch:25 + cch]).then_inc(conv_first, 1)
                for j in range(2):
                    cch = 2 * n + j
                    taken(act, ("qk", cch))
                    act.activation(qkc[:, cch, :], qkc[:, cch, :], ACT.Silu).then_inc(qk_ready, 1)

            def mixer():
                conv_unit(0)
                split_after(("t0",))
                split_after(("t1",))
                for n in range(2):
                    split_after(("v", n))
                    for b in range(2):
                        src = job_result(act, ("v", n, b))
                        if (n, b) == (0, 0):
                            act.wait_ge(mixer_consts, 1)
                        job_read(act.activation(v_aug[:, 2 * b:2 * b + 2, 2 * n:2 * n + 2, 0:MD],
                                                src.rearrange("p (t h e) -> p t h e", t=2, h=2), ACT.Copy), ("v", n, b))
                act.wait_ge(small_landed, 80)
                src = job_result(act, ("ifT", 0))
                job_read(act.activation(row_i[:], src[0:MH, :], ACT.Identity, bias=g_bias[:, 0:1]), ("ifT", 0))
                src = job_result(act, ("ifT", 1))
                job_read(act.activation(row_f[:], src[0:MH, :], ACT.Identity, bias=g_bias[:, 1:2]), ("ifT", 1))
                taken(act, ("ifT", 1))
                step.tick(act.activation(row_t[:], row_f[:], ACT.Abs))
                step.wait(act)
                step.tick(act.activation(row_t[:], row_t[:], ACT.Exp, scale=-1.0))
                step.wait(act)
                act.activation(row_t[:], row_t[:], ACT.Ln, bias=1.0).then_inc(soft_ready, 1)
                for n in range(1, 4):
                    conv_unit(n)
                split_after(("kcvc",))
                for j, ab in enumerate("ab"):
                    src = job_result(act, ("kcvc", ab))
                    job_read(act.activation(kv_t[:, j, :, :], src.rearrange("p (n par) -> p par n", par=2), ACT.Copy), ("kcvc", ab))
                taken(act, ("kcvc", "b"))
                for par in range(2):
                    for g in range(NG):
                        act.dma_start(kv_2[par * ND:(par + 1) * ND, :, g, :],
                                      kv_t[g * ND:(g + 1) * ND, :, par, :]).then_inc(kv_moved, 16)
                act.wait_ge(m_ready, 1)
                act.activation(row_t[:], row_t[:], ACT.Exp, scale=-1.0).then_inc(em_ready, 1)

                def o_gate(n):
                    for cch in (2 * n, 2 * n + 1):
                        src = job_result(act, ("o", cch))
                        job_read(act.activation(sig_o[:, cch, :], src, ACT.Sigmoid), ("o", cch))

                def head_exps(hd):
                    for j in range(TT):
                        act.wait_ge(arg_ready, hd * TT + j + 1)
                        act.activation(sq[j % 2][:, 0:T - j * P], sq[j % 2][:, 0:T - j * P], ACT.Exp,
                                       bias=cols[:, 0, j, hd:hd + 1]).then_inc(e_ready, 1)

                def head_squares(hd):
                    act.wait_ge(hm_ready, hd + 1)
                    step.wait(act)
                    for t in range(TT):
                        step.tick(act.activation(wt[0][:, t * P:(t + 1) * P], hm[:, hd, t * P:(t + 1) * P], ACT.Square,
                                                 accum_out=ssm[:, hd, t:t + 1]))

                def take_queries(n):
                    for j, ab in enumerate("ab"):
                        copy_out(("qn", n, ab), qn[:, 2 * n + j, :], scale=ND ** -0.5)

                def blocks_high(kv):
                    act.wait_ge(blk_ready, kv + 1)
                    if kv:
                        job_done(act, ("hid", 0))
                    act.activation(blk_hi[:], blk[:], ACT.Copy).then_inc(blk_hi_ready, 1)

                def hidden_silu(kv):
                    src = job_result(act, ("hid", kv))
                    for half in range(2):
                        b1 = 44 + 2 * kv + half
                        ins = act.activation(hid[:, kv, half, :], src[:, half * 64:(half + 1) * 64], ACT.Silu,
                                             bias=col2[:, b1:b1 + 1])
                    job_read(ins, ("hid", kv))

                split_after(("o", 0))
                o_gate(0)
                split_after(("o", 1))
                head_exps(0)
                blocks_high(0)
                split_after(("kk",))
                o_gate(1)
                head_exps(1)
                split_after(("c1", 0, 0))
                for j, ab in enumerate("ab"):
                    copy_out(("kk", ab), ksw[:, j, :])
                head_squares(0)
                head_exps(2)
                split_after(("c1", 0, 1))
                split_after(("qn", 0))
                hidden_silu(0)
                head_squares(1)
                head_exps(3)
                blocks_high(1)
                split_after(("c1", 1, 0))
                take_queries(0)
                head_squares(2)
                split_after(("c1", 1, 1))
                head_squares(3)
                step.wait(act)
                act.activation(ssm[:], ssm[:], ACT.Sqrt, bias=eps_m[:, 0:1], scale=1.0 / MD).then_inc(ssm_root, 1)
                split_after(("qn", 1))
                hidden_silu(1)
                src = job_result(act, ("kcmp",))
                job_read(act.activation(k_cmp[:], src[:, 0:32], ACT.Identity, bias=col2[:, 80:81]), ("kcmp",))
                taken(act, ("t0", 0))
                taken(act, ("t0", 1))
                act.activation(sig_n[:], g_tok[:, :, 8:32].rearrange("p t (h b) -> p t h b", b=3), ACT.Sigmoid).then_inc(sig_n_ready, 1)
                take_queries(1)

                def take_gate(cch):
                    copy_out(gate_job(cch), (sig_a if cch < DC else sig_b)[:, cch % DC, :])

                for t in range(TT):
                    if t % 2 == 0:
                        split_after(GATES[t // 2])
                    act.wait_ge(arg_c_ready, t + 1)
                    act.activation(p_c[:], p_c[:], ACT.Exp).then_inc(e_c_ready, 1)
                    if t == 0:
                        for hd in range(MH):
                            taken(act, ("hT", hd))
                    take_gate(t)
                    src = job_result(act, ("pcT", t))
                    if t:
                        job_done(act, ("oc", t - 1))
                    job_read(act.activation(pt_c[:].rearrange("p g t -> p (g t)"), src[:, 0:NG * P], ACT.Copy), ("pcT", t))
                for s, (t, g, hh) in enumerate(STEPS):
                    cch = chunk_at.get(s)
                    if cch is not None and cch % 2 == 0:
                        split_after(GATES[cch // 2])
                    for br, (name, p) in enumerate((("ss", p_s), ("sw", p_w))):
                        n = P * len(blocks_of(t)[br])
                        act.wait_ge(n_max_ready, s + 1)
                        src = job_result(act, (name, s))
                        if s >= 2:
                            job_done(act, ("ts" if br == 0 else "tw", s - 2))
                        job_read(act.activation(p[s % 2][:, 0:n], src[:, 0:n], ACT.Exp, bias=n_max[:, s, br:br + 1],
                                                accum_out=sums[:, s, br:br + 1]), (name, s))
                    if cch is not None:
                        take_gate(cch)
                    n = P * len(blocks_of(t)[1])
                    src = job_result(act, ("tw", s))
                    job_read(act.activation(pt_w[s % 2][:, 0:n], src[:, 0:n], ACT.Copy), ("tw", s))
                split_after(GATES[-1])
                for fc in range(4):
                    src = job_result(act, ("oT", fc))
                    act.activation(o_hi[:, fc, :], src, ACT.Copy).then_inc(o_hi_ready, 1)
                act.activation(hm_hi[:], hm[:], ACT.Copy).then_inc(o_hi_ready, 1)
                taken(act, gate_job(DC - 1))
                act.activation(sig_a[:], sig_a[:], ACT.Sigmoid).then_inc(gates_ready, 1)
                take_gate(2 * DC - 2)
                take_gate(2 * DC - 1)
                taken(act, gate_job(2 * DC - 1))
                act.activation(sig_b[:], sig_b[:], ACT.Sigmoid).then_inc(gates_ready, 1)
                load_table(ACT.Sqrt)
                for j in range(2):
                    split_after(("um", j))
                    split_after(("un", j))
                    for n in range(4):
                        act.wait_ge(merged, 4 * j + n + 1)
                        act.activation(u_hi[:, 4 * j + n, :], wt[n % 2][:], ACT.Copy).then_inc(u_hi_ready, 1)
                for n in range(4):
                    split_after(("wo", n))
                    for j in range(2):
                        take_y((("y1", 2 * n + j), 0), 1, 2 * n + j, y_mix)

            act.wait_ge(c_landed, 16)
            act.activation(silu_c[:], c_col[:], ACT.Silu).then_inc(silu_c_ready, 1)
            act.wait_ge(consts_ready, 1)
            load_table(ACT.Sqrt)
            for cch in range(DC):
                job_read(act.activation(h[:, cch, :], job_result(act, ("x", cch)), ACT.Copy), ("x", cch))
            for cch in range(DC):
                taken(act, ("x", cch))
                if cch >= 2:
                    act.wait_ge(sq_used, cch - 1)
                act.activation(sq[cch % 2][:], h[:, cch, :], ACT.Square).then_inc(sq_ready, 1)
            root(("pre", 0))
            split_high(("g0", 0))
            modulate_high(0)
            ffn_up(0)
            ffn_down(0, 0, y_ffn, ("qk", 0))
            root(("post", 0))
            pre_norm_squares(1)
            root(("pre", 1))
            modulate_high(1)
            mixer()
            root(("post", 1))
            pre_norm_squares(2)
            root(("pre", 2))
            modulate_high(2)
            ffn_up(1)
            ffn_down(1, 2, y_ffn, None)
            root(("post", 2))
            for cch in range(DC):
                src = job_result(act, ("out", cch))
                job_read(act.activation(out_tok[:, :, cch * P:(cch + 1) * P], src.rearrange("p (t n) -> p t n", t=TT),
                                        ACT.Copy), ("out", cch))

        @block.vector
        def _(dve):
            step = Count(dve_step)

            def split_low(name, i=0, size=DC * COLS):
                n, slot = w_number(name, i)
                dve.wait_ge(hi_ready, n)
                dve.tensor_tensor(w_lo[slot][:, 0:size], raw[plan.raws[name][0]][:, 0:size],
                                  w_hi[slot][:, 0:size].bitcast(F32), ALU.subtract).then_inc(lo_ready, 1)

            def sum_ada(name, i, number, half=0):
                acc = ada_acc[:, half, :]
                src = unit_landed(dve, name, i)
                for j in range(DC):
                    part = src[:, j * COLS:(j + 1) * COLS]
                    if j:
                        dve.wait_ge(dve_step, (DC - 1) * number + j)
                        ins = dve.scalar_tensor_tensor(acc, part, silu_c[:, j:j + 1], acc, ALU.mult, ALU.add)
                    else:
                        ins = dve.tensor_scalar(acc, part, silu_c[:, 0:1], None, ALU.mult)
                    ins.then_inc(dve_step if j < DC - 1 else ada_summed, 1)

            def take_ada(name, i, number, units=1):
                src = job_result(dve, name, i)
                at_ = bass.ds(2 * (number + ADA_FIRST), 2 * units)
                job_read(dve.tensor_tensor(ada[:, at_], src[:, 0:2 * units], col1[:, at_], ALU.add), name)

            def inverse_rms(job):
                taken(dve, job)
                misc.tick(dve.reciprocal(inv_t[:], root_t[:]))
                misc.wait(dve)
                dve.tensor_tensor(rs[:].rearrange("p (t n) -> p t n", t=TT), bcast(ident[:].unsqueeze(1), [P, TT, P]),
                                  bcast(inv_t[:].unsqueeze(2), [P, TT, P]), ALU.mult).then_inc(diag_ready, 1)

            misc = Count(dve_misc)

            def gains(s):
                shift, scale, gate = (ada[:, (3 * s + j) * DC:(3 * s + j + 1) * DC] for j in range(3))
                pre = col1[:, 72 + 2 * s * DC:72 + (2 * s + 1) * DC]
                misc.tick(dve.scalar_tensor_tensor(gain_a[:], scale, 1.0, pre, ALU.add, ALU.mult))
                misc.wait(dve)
                misc.tick(dve.tensor_scalar(gain_a[:], gain_a[:], ROOT_D, None, ALU.mult))
                misc.wait(dve)

            def gains_post(s, weight):
                gate = ada[:, (3 * s + 2) * DC:(3 * s + 3) * DC]
                post = col1[:, 72 + (2 * s + 1) * DC:72 + (2 * s + 2) * DC]
                misc.tick(dve.scalar_tensor_tensor(gain_g[:], gate, weight * ROOT_D, post, ALU.mult, ALU.mult))
                misc.wait(dve)

            def modulate(s):
                shift = s * 3 * DC
                r = job_result(dve, ("r", "pre", s))

                base = (0, DC, 3 * DC)[s]

                def low(cch):
                    dve.wait_ge(u_hi_ready, base + cch + 1)
                    dve.scalar_tensor_tensor(u_lo[:, cch, :], wt[cch % 2][:], ada[:, shift + cch:shift + cch + 1],
                                             u_hi[:, cch, :].bitcast(F32), ALU.add, ALU.subtract).then_inc(u_ready, 1)
                for cch in range(DC):
                    if cch >= 2:
                        low(cch - 2)
                        dve.wait_ge(u_ready, base + cch - 1)
                    dve.scalar_tensor_tensor(wt[cch % 2][:], h[:, cch, :], gain_a[:, cch:cch + 1], r,
                                             ALU.mult, ALU.mult).then_inc(w_scaled, 1)
                low(DC - 2)
                low(DC - 1)
                dve.wait_ge(w_scaled, (s + 1) * DC)
                dve.sem_inc(bank_free[plan.jobs[("r", "pre", s)][0]], 1)

            def ffn_up(f):
                with dve.Fori(0, UP_ITERS) as i:
                    split_low(("up", f), i)
                    if f == 0:
                        sum_ada(("ada", "a"), i, 2 * i, 0)
                    split_low(("gate", f), i)
                    if f == 0:
                        sum_ada(("ada", "b"), i, 2 * i + 1, 1)
                    for j in range(2):
                        taken(dve, ("g", f, j), i)
                        src = job_result(dve, ("u", f, j), i)
                        job_read(dve.tensor_tensor(wt[j][:], src, sq[j][:], ALU.mult), ("u", f, j))
                    if f == 0:
                        take_ada(("ada", "ab"), i, 2 * i, 2)
                    for j in range(2):
                        dve.wait_ge(mid_hi_ready, (i + f * UP_ITERS) * 2 + j + 1)
                        at_ = bass.ds(2 * i + j, 1)
                        dve.tensor_tensor(mid_lo[:, at_, :], wt[j][:].rearrange("p (a t) -> p a t", a=1),
                                          mid_hi[:, at_, :].bitcast(F32), ALU.subtract).then_inc(mid_ready, 1)

            def ffn_down(f, next_name):
                for it in range(2):
                    for n in range(6):
                        if n == 3:
                            take_ada(("ada", f, 2), it, ada_number(f, it, 2))
                        if (it, n) != (1, 5):
                            nxt = ("d", f, it, n + 1) if n < 5 else ("d", f, 1, 0)
                            kk = (n + 1) % 3
                            split_low(nxt, 0, (DOWN_K[kk + 1] - DOWN_K[kk]) * COLS)
                        elif next_name is not None:
                            split_low(next_name, 0)
                        if has_ada(f, n + 1):
                            sum_ada(("ada", f, it, n + 1), 0, ada_number(f, it, n + 1))
                    if f == 0:
                        take_ada(("ada", f, 5), it, ada_number(f, it, 5))

            def update_h(post, y):
                r = job_result(dve, ("r", "post", post))
                for cch in range(DC):
                    if cch >= 2:
                        h_updated(dve, post, cch - 2)
                    dve.scalar_tensor_tensor(wt[cch % 2][:], y[:, cch, :], gain_g[:, cch:cch + 1], r,
                                             ALU.mult, ALU.mult).then_inc(delta_ready, 1)
                    if cch % 2:
                        dve.wait_ge(delta_ready, post * DC + cch)
                        dve.tensor_tensor(h[:, cch - 1, :], h[:, cch - 1, :], wt[0][:], ALU.add).then_inc(h_ready[0], 1)
                dve.wait_ge(delta_ready, (post + 1) * DC)
                dve.sem_inc(bank_free[plan.jobs[("r", "post", post)][0]], 1)

            def mixer_low(name):
                nxt = after(name)
                size = 160 * DC if nxt == ("t0",) else P * DC if nxt == ("t1",) else DC * COLS
                split_low(nxt, 0, size=size)

            def conv_taps(n):
                mixer_low(("qk", n))
                for tap in (2, 1, 0):
                    for j in range(2):
                        cch = 2 * n + j
                        dve.wait_ge(conv_first, cch + 1)
                        if tap < 2:
                            misc.wait(dve, misc.n - 1 if tap == 1 or j == 0 else misc.n)
                        src = PS[:, plan.jobs[("qk", cch)][0], :]
                        lag = 3 - tap
                        w = 8 * tap + cch
                        ins = dve.scalar_tensor_tensor(qkc[:, cch, lag:T], src[:, 0:T - lag], col2[:, w:w + 1],
                                                       qkc[:, cch, lag:T], ALU.mult, ALU.add)
                        if tap:
                            misc.tick(ins)
                        else:
                            job_read(ins, ("qk", cch))

            def mixer():
                conv_taps(0)
                mixer_low(("t0",))
                for b in range(2):
                    src = job_result(dve, ("t0", b))[:, 0:320].rearrange("p (t n) -> p t n", t=2)
                    dve.wait_ge(mixer_consts, 1)
                    misc.tick(dve.tensor_copy(g_tok[:, 2 * b:2 * b + 2, :], src[:, :, 0:32]))
                    job_read(dve.tensor_copy(vsw[:, 2 * b:2 * b + 2, 0, :], src[:, :, 32:160]), ("t0", b))
                mixer_low(("t1",))
                src = job_result(dve, ("t1",)).rearrange("p (t n) -> p t n", t=TT)
                job_read(dve.tensor_copy(vsw[:, :, 1, :], src), ("t1",))
                for n in range(2):
                    mixer_low(("v", n))
                dve.wait_ge(soft_ready, 1)
                misc.tick(dve.scalar_tensor_tensor(row_f[:], row_f[:], 0.0, row_t[:], ALU.min, ALU.subtract))
                misc.wait(dve)
                misc.tick(dve.tensor_tensor_scan(row_s[:], row_f[:], row_z[:], 0.0, ALU.add, ALU.add))
                misc.wait(dve)
                misc.tick(dve.tensor_tensor(row_i[:], row_i[:], row_s[:], ALU.subtract))
                misc.wait(dve)
                misc.tick(dve.tensor_tensor_scan(row_m[:], row_i[:], row_i[:], 0.0, ALU.max, ALU.max))
                misc.wait(dve)
                dve.tensor_tensor(row_t[:], row_s[:], row_m[:], ALU.add).then_inc(m_ready, 1)
                for n in range(1, 4):
                    conv_taps(n)
                def head_weights(hd):
                    neg = job_result(dve, ("negM", hd))
                    for j in range(TT + 1):
                        if j < TT:
                            n = T - j * P
                            if j >= 2:
                                taken(dve, ("S", hd, j - 2))
                            elif hd:
                                taken(dve, ("S", hd - 1, j + 2))
                            ins = dve.tensor_tensor(sq[j % 2][:, 0:n], neg[:, j * P:T], mask_row[:, 0:n], ALU.add)
                            ins.then_inc(arg_ready, 1)
                        if j:
                            i, n = j - 1, T - (j - 1) * P
                            src = job_result(dve, ("S", hd, i))
                            dve.wait_ge(e_ready, hd * TT + j)
                            job_read(dve.scalar_tensor_tensor(p_m[:, i, 0:n], src[:, 0:n], MD ** -0.5, sq[i % 2][:, 0:n],
                                                              ALU.mult, ALU.mult), ("S", hd, i))
                    dve.wait_ge(arg_ready, hd * TT + TT)
                    dve.sem_inc(bank_free[plan.jobs[("negM", hd)][0]], 1)

                def head_output(hd):
                    for b in range(2):
                        num = job_result(dve, ("num", hd, b))[:, 0:2 * (MD + 1)].rearrange("p (t e) -> p t e", t=2)
                        misc.tick(dve.tensor_copy(den[:, hd, 2 * b:2 * b + 2], num[:, :, MD]))
                    misc.wait(dve)
                    misc.tick(dve.scalar_tensor_tensor(max_c[:, 0:TT], den[:, hd, :], -1.0, cols[:, 1, :, hd], ALU.mult, ALU.max))
                    misc.wait(dve)
                    misc.tick(dve.tensor_tensor(den[:, hd, :], den[:, hd, :], max_c[:, 0:TT], ALU.max))
                    misc.wait(dve)
                    misc.tick(dve.reciprocal(den[:, hd, :], den[:, hd, :]))
                    misc.wait(dve)
                    h3 = hm[:, hd, :].rearrange("p (t e) -> p t e", t=TT)
                    for b in range(2):
                        num = job_result(dve, ("num", hd, b))[:, 0:2 * (MD + 1)].rearrange("p (t e) -> p t e", t=2)
                        job_read(dve.tensor_tensor(h3[:, 2 * b:2 * b + 2, :], num[:, :, 0:MD],
                                                   bcast(den[:, hd, 2 * b:2 * b + 2].unsqueeze(2), [P, 2, MD]), ALU.mult), ("num", hd, b))
                        taken(dve, ("num", hd, b))
                    dve.sem_inc(hm_ready, 1)

                mixer_low(("kcvc",))
                mixer_low(("o", 0))
                src = job_result(dve, ("colT",))
                job_read(dve.tensor_copy(cols[:].rearrange("p a t h -> p (a t h)"), src[:, 0:2 * TT * MH]), ("colT",))
                mixer_low(("o", 1))
                head_weights(0)
                mixer_low(("kk",))
                head_output(0)
                head_weights(1)
                mixer_low(("c1", 0, 0))
                head_output(1)
                head_weights(2)
                mixer_low(("c1", 0, 1))
                mixer_low(("qn", 0))
                head_output(2)
                head_weights(3)
                mixer_low(("c1", 1, 0))
                head_output(3)
                mixer_low(("c1", 1, 1))
                dve.wait_ge(ssm_root, 1)
                misc.tick(dve.reciprocal(ssm[:], ssm[:]))
                misc.wait(dve)
                for hd in range(MH):
                    h3 = hm[:, hd, :].rearrange("p (t e) -> p t e", t=TT)
                    dve.tensor_tensor(h3, h3, bcast(ssm[:, hd, :].unsqueeze(2), [P, TT, MD]), ALU.mult).then_inc(hm_normed, 1)
                mixer_low(("qn", 1))
                taken(dve, ("hid", 1))
                for g in range(NG):
                    src = hid[:, 1, :, g * 32:(g + 1) * 32].unsqueeze(2)
                    misc.tick(dve.tensor_copy(hid_rep[:, :, g, :, :], bcast(src, [P, 2, HG, 32])))
                misc.wait(dve)
                dve.sem_inc(hid_rep_ready, 1)
                for hd in range(MH):
                    src = job_result(dve, ("hT", hd))
                    job_read(dve.scalar_tensor_tensor(hm[:, hd, :], src, col2[:, 40 + hd:41 + hd], sig_o[:, hd, :],
                                                      ALU.mult, ALU.mult), ("hT", hd))
                src = job_result(dve, ("vcmp",))[:, 0:NG * ND].rearrange("p (g e) -> p g e", g=NG)
                job_read(dve.tensor_tensor(v_tmp[:], src, bcast(b2_row[:].unsqueeze(1), [P, NG, ND]), ALU.add), ("vcmp",))
                taken(dve, ("vcmp",))
                for n in range(HG):
                    misc.tick(dve.tensor_scalar(v_bd[:, :, n, :], v_tmp[:], bd[:, n:n + 1], None, ALU.mult))
                misc.wait(dve)
                dve.sem_inc(v_bd_ready, 1)
                def take_oc(t):
                    src = job_result(dve, ("oc", t))
                    job_read(dve.tensor_copy(o_acc[:, t, :], src), ("oc", t))

                for t in range(TT):
                    if t % 2 == 0:
                        mixer_low(GATES[t // 2])
                    for g in range(NG):
                        src = job_result(dve, ("sc", t, g))[:, 0:P].rearrange("p (h n) -> p h n", n=32)
                        if t and g == 0:
                            job_done(dve, ("pcT", t - 1))
                        job_read(dve.tensor_tensor(p_c[:, 4 * g:4 * g + 4, :], src, bcast(add_c[:, t:t + 1, :], [P, HG, 32]), ALU.add), ("sc", t, g))
                        taken(dve, ("sc", t, g))
                    misc.tick(dve.tensor_reduce(max_c[:], p_c[:], AX.X, ALU.max))
                    misc.wait(dve)
                    dve.tensor_tensor(p_c[:], p_c[:], bcast(max_c[:].unsqueeze(2), [P, NH, 32]), ALU.subtract).then_inc(arg_c_ready, 1)
                    dve.wait_ge(e_c_ready, t + 1)
                    misc.tick(dve.tensor_tensor(p_c[:], p_c[:], bcast(keep_c[:, t:t + 1, :], [P, NH, 32]), ALU.mult))
                    misc.wait(dve)
                    misc.tick(dve.tensor_reduce(sum_c[:], p_c[:], AX.X, ALU.add))
                    misc.wait(dve)
                    misc.tick(dve.tensor_scalar(sum_c[:], sum_c[:], 1e-30, None, ALU.max))
                    misc.wait(dve)
                    misc.tick(dve.reciprocal(sum_c[:], sum_c[:]))
                    misc.wait(dve)
                    if t == 0:
                        dve.wait_ge(sig_n_ready, 1)
                    misc.tick(dve.tensor_tensor(sum_c[:], sum_c[:], sig_n[:, t, :, 0], ALU.mult))
                    misc.wait(dve)
                    dve.tensor_tensor(p_c[:], p_c[:], bcast(sum_c[:].unsqueeze(2), [P, NH, 32]), ALU.mult).then_inc(p_c_ready, 1)
                    if t:
                        take_oc(t - 1)
                take_oc(TT - 1)

                def scores_max(s):
                    t = STEPS[s][0]
                    for br, name in enumerate(("ss", "sw")):
                        n = P * len(blocks_of(t)[br])
                        src = job_result(dve, (name, s))
                        ins = dve.tensor_reduce(n_max[:, s, br:br + 1], src[:, 0:n], AX.X, ALU.max, negate=True)
                    ins.then_inc(n_max_ready, 1)

                scores_max(0)
                for s, (t, g, hh) in enumerate(STEPS):
                    if chunk_at.get(s, 1) % 2 == 0:
                        mixer_low(GATES[chunk_at[s] // 2])
                    if s + 1 < len(STEPS):
                        scores_max(s + 1)
                    n = P * len(blocks_of(t)[0])
                    src = job_result(dve, ("ts", s))
                    job_read(dve.tensor_copy(pt_s[s % 2][:, 0:n], src[:, 0:n]), ("ts", s))
                    if hh == 0 and s:
                        group_output(s - HG)
                group_output(len(STEPS) - HG)
                dve.sem_inc(o_acc_ready, 1)
                mixer_low(GATES[-1])
                for fc in range(4):
                    src = job_result(dve, ("oT", fc))
                    dve.wait_ge(o_hi_ready, fc + 1)
                    job_read(dve.tensor_tensor(o_lo[:, fc, :], src, o_hi[:, fc, :].bitcast(F32), ALU.subtract), ("oT", fc))
                dve.wait_ge(o_hi_ready, 5)
                dve.tensor_tensor(hm_lo[:], hm[:], hm_hi[:].bitcast(F32), ALU.subtract).then_inc(hm_lo_ready, 1)
                for j in range(2):
                    mixer_low(("um", j))
                    for n in range(4):
                        cch = 4 * j + n
                        src = job_result(dve, ("ym", cch))
                        if cch == 0:
                            dve.wait_ge(gates_ready, 2)
                        job_read(dve.tensor_tensor(sig_a[:, cch, :], sig_a[:, cch, :], src, ALU.mult), ("ym", cch))
                    mixer_low(("un", j))
                    for n in range(4):
                        cch = 4 * j + n
                        src = job_result(dve, ("yn", cch))
                        if cch >= 2:
                            dve.wait_ge(u_ready, DC + DC + cch - 1)
                        job_read(dve.tensor_tensor(wt[n % 2][:], sig_b[:, cch, :], src, ALU.mult), ("yn", cch))
                        taken(dve, ("yn", cch))
                        dve.tensor_tensor(wt[n % 2][:], wt[n % 2][:], sig_a[:, cch, :], ALU.add).then_inc(merged, 1)
                        dve.wait_ge(u_hi_ready, 2 * DC + cch + 1)
                        dve.tensor_tensor(u_lo[:, cch, :], wt[n % 2][:], u_hi[:, cch, :].bitcast(F32), ALU.subtract).then_inc(u_ready, 1)
                for n in range(4):
                    mixer_low(("wo", n))

            def group_output(s0):
                t, g, _ = STEPS[s0]
                for s in range(s0, s0 + HG):
                    taken(dve, ("ss", s))
                    taken(dve, ("sw", s))
                misc.tick(dve.reciprocal(w_sw[:], sums[:, s0:s0 + HG, :]))
                misc.wait(dve)
                misc.tick(dve.tensor_tensor(w_sw[:], w_sw[:], sig_n[:, t, g * HG:(g + 1) * HG, 1:3], ALU.mult))
                misc.wait(dve)
                src = job_result(dve, ("o_nsa", t, g)).rearrange("p (h b e) -> p h b e", h=HG, b=2)
                ins = dve.tensor_tensor(o_tmp[:], src, bcast(w_sw[:].unsqueeze(3), [P, HG, 2, ND]), ALU.mult)
                job_read(ins, ("o_nsa", t, g))
                taken(dve, ("o_nsa", t, g))
                acc = o_acc[:, t, g * HG * ND:(g + 1) * HG * ND].rearrange("p (h e) -> p h e", h=HG)
                if g == 0:
                    taken(dve, ("oc", t))
                for br in range(2):
                    misc.tick(dve.tensor_tensor(acc, acc, o_tmp[:, :, br, :], ALU.add))
                    misc.wait(dve)

            src = job_result(dve, ("cols", 1))
            job_read(dve.tensor_copy(col1[:], src[:, 0:120]), ("cols", 1))
            src = job_result(dve, ("cols", 2))
            job_read(dve.tensor_copy(col2[:], src[:, 0:81]), ("cols", 2))
            dve.wait_ge(silu_c_ready, 1)
            for j in range(DC):
                dve.wait_ge(ada_first_landed[j], 16)
                if j == DC - 2:
                    inverse_rms(("pre", 0))
                if j == DC - 1:
                    split_low(("g0", 0))
                if j:
                    misc.wait(dve)
                    ins = dve.scalar_tensor_tensor(ada_acc0[:], ada_w[:, j, :], silu_c[:, j:j + 1], ada_acc0[:], ALU.mult, ALU.add)
                else:
                    ins = dve.tensor_scalar(ada_acc0[:], ada_w[:, 0, :], silu_c[:, 0:1], None, ALU.mult)
                misc.tick(ins) if j < DC - 1 else ins.then_inc(ada_summed, 1)
            src = job_result(dve, ("ada0",))
            taken(dve, ("cols", 1))
            ins = dve.tensor_tensor(ada[:, 0:2 * ADA_FIRST], src[:, 0:2 * ADA_FIRST], col1[:, 0:2 * ADA_FIRST], ALU.add)
            job_read(ins, ("ada0",))
            taken(dve, ("ada0",))
            gains(0)
            modulate(0)
            ffn_up(0)
            ffn_down(0, ("qk", 0))
            taken(dve, ("ada", 0, 5), 1)
            gains_post(0, 0.5)
            gains(1)
            inverse_rms(("post", 0))
            update_h(0, y_ffn)
            inverse_rms(("pre", 1))
            modulate(1)
            mixer()
            gains_post(1, 1.0)
            gains(2)
            inverse_rms(("post", 1))
            update_h(1, y_mix)
            inverse_rms(("pre", 2))
            modulate(2)
            ffn_up(1)
            ffn_down(1, None)
            taken(dve, ("ada", 1, 2), 1)
            gains_post(2, 0.5)
            inverse_rms(("post", 2))
            update_h(2, y_ffn)

        @block.tensor
        def _(pe):
            def three_passes(ps, pairs):
                total = len(pairs)
                for n, (wh, wl, ah, al) in enumerate(pairs):
                    pe.matmul(ps, wh, ah, start=(n == 0), stop=False)
                    pe.matmul(ps, wh, al, start=False, stop=False)
                    ins = pe.matmul(ps, wl, ah, start=False, stop=(n == total - 1))
                return ins

            def unit_ready(name, i=0):
                n, slot = w_number(name, i)
                pe.wait_ge(lo_ready, n)
                return w_hi[slot], w_lo[slot]

            def k_pairs(unit, j, kn, ahi, alo, k0=0, first=True, width=COLS):
                wh, wl = unit
                return [(wh[:, k * width + j * P:k * width + (j + 1) * P], wl[:, k * width + j * P:k * width + (j + 1) * P],
                         ahi[:, k0 + k, :], alo[:, k0 + k, :]) for k in range(kn)]

            def token_sums(ps, squares, first, last):
                for t in range(TT):
                    ins = pe.matmul(ps[:, t:t + 1], chunk(squares, t), ones[:, 0:1], start=first and t == 0,
                                    stop=last and t == TT - 1)
                return ins

            def spread_inverse(kind, s):
                ps = job_start(pe, ("r", kind, s))
                pe.wait_ge(diag_ready, 2 * s + (kind == "post") + 1)
                job_end(pe.matmul(ps, ones[:], rs[:], start=True, stop=True), ("r", kind, s))

            def pre_norm(s):
                ps = job_start(pe, ("pre", s))
                for cch in range(DC):
                    pe.wait_ge(sq_ready, s * DC + cch + 1)
                    ins = token_sums(ps, sq[cch % 2], cch == 0, cch == DC - 1)
                    if cch < DC - 1:
                        ins.then_inc(sq_used, 1)
                job_end(ins, ("pre", s))
                spread_inverse("pre", s)

            def post_norm(s, y_job):
                ps = job_start(pe, ("post", s))
                pe.wait_ge(ysum_ready, (s + 1) * (DC - 2))
                token_sums(ps, rs, True, False)
                for cch in (DC - 2, DC - 1):
                    taken(pe, *y_job(cch))
                    ins = token_sums(ps, sq[cch % 2], False, cch == DC - 1)
                job_end(ins, ("post", s))
                spread_inverse("post", s)

            def ada_columns(name, i, number, units=1):
                ps = job_start(pe, name, i)
                pe.wait_ge(ada_summed, number + 1 + units)
                for u in range(units):
                    for j in range(2):
                        ins = pe.matmul(ps[:, 2 * u + j:2 * u + j + 1], ada_acc[:, u, j * P:(j + 1) * P], ones[:, 0:1],
                                        start=True, stop=True)
                job_end(ins, name)

            def chunks_as_they_come(unit, jobs, i, u_base):
                wh, wl = unit
                ps = [job_start(pe, job, i) for job in jobs]
                for k in range(DC):
                    pe.wait_ge(u_ready, u_base + k + 1)
                    for j, job in enumerate(jobs):
                        at_ = slice(k * COLS + j * P, k * COLS + (j + 1) * P)
                        pe.matmul(ps[j], wh[:, at_], u_hi[:, k, :], start=(k == 0), stop=False)
                        pe.matmul(ps[j], wh[:, at_], u_lo[:, k, :], start=False, stop=False)
                        ins = pe.matmul(ps[j], wl[:, at_], u_hi[:, k, :], start=False, stop=(k == DC - 1))
                        if k == DC - 1:
                            job_end(ins, job)

            def ffn_up(f):
                u_base = 3 * f * DC
                with pe.Fori(0, UP_ITERS) as i:
                    n0, slot = w_number(("g0", f))
                    pe.wait_ge(lo_ready, n0 + 2 * i)
                    chunks_as_they_come((w_hi[slot], w_lo[slot]), [("g", f, 0), ("g", f, 1)], i, u_base)
                    unit = unit_ready(("up", f), i)
                    for j in range(2):
                        ps = job_start(pe, ("u", f, j), i)
                        ins = three_passes(ps, k_pairs(unit, j, DC, u_hi, u_lo))
                        job_end(ins, ("u", f, j))
                    if f == 0:
                        ada_columns(("ada", "ab"), i, 2 * i, 2)

            def ffn_down(f):
                pe.wait_ge(mid_ready, (f + 1) * FC)
                base_n, _ = w_number(("gate", f))
                base_n += 2 * (UP_ITERS - 1)
                with pe.Fori(0, 2) as i:
                    for n in range(6):
                        pe.wait_ge(lo_ready, base_n + 6 * i + n)
                        slot = (base_n + n - 1) % 2
                        k0, k1 = DOWN_K[n % 3], DOWN_K[n % 3 + 1]
                        for j in range(2):
                            name = ("y", f, n // 3 * 2 + j)
                            if n % 3 == 0:
                                ps = job_start(pe, name, i)
                            else:
                                ps = PS[:, plan.jobs[name][0], :]
                            for k in range(k1 - k0):
                                wh, wl = (w[slot][:, k * COLS + j * P:k * COLS + (j + 1) * P] for w in (w_hi, w_lo))
                                f_at = k0 + k
                                pe.matmul(ps, wh, mid_hi[:, f_at, :], start=(f_at == 0), stop=False)
                                pe.matmul(ps, wh, mid_lo[:, f_at, :], start=False, stop=False)
                                ins = pe.matmul(ps, wl, mid_hi[:, f_at, :], start=False, stop=(f_at == FC - 1))
                            if n % 3 == 2:
                                job_end(ins, name)
                        if n % 3 < 2:
                            ins.then_inc(w_used, 1)
                        if has_ada(f, n):
                            ada_columns(("ada", f, n), i, ada_number(f, i, n))

            def mixer():
                def unit(name):
                    return unit_ready(name)

                def last_of(ins, name):
                    if unit_end[name] is None:
                        ins.then_inc(w_used, 1)

                def feature_unit(name, jobs, act_hi=u_hi, act_lo=u_lo, kn=DC, width=COLS):
                    w = unit(name)
                    for j, job in enumerate(jobs):
                        feature_chunk(w, j, job, act_hi, act_lo, kn, width)

                def feature_chunk(w, j, job, act_hi=u_hi, act_lo=u_lo, kn=DC, width=COLS):
                    ps = job_start(pe, job)
                    job_end(three_passes(ps, k_pairs(w, j, kn, act_hi, act_lo, width=width)), job)

                def token_unit(name, jobs, n):
                    wh, wl = unit(name)
                    per = TT // len(jobs)
                    for b, job in enumerate(jobs):
                        ps = job_start(pe, job)
                        for i in range(per):
                            t = b * per + i
                            pairs = [(u_hi[:, k, t * P:(t + 1) * P], u_lo[:, k, t * P:(t + 1) * P],
                                      wh[:, k * n:(k + 1) * n], wl[:, k * n:(k + 1) * n]) for k in range(DC)]
                            ins = three_passes(ps[:, i * n:(i + 1) * n], pairs)
                        job_end(ins, job)

                chunks_as_they_come(unit(("qk", 0)), [("qk", 0), ("qk", 1)], 0, DC)
                pe.wait_ge(mixer_consts, 1)
                token_unit(("t0",), [("t0", 0), ("t0", 1)], 160)
                token_unit(("t1",), [("t1",)], P)
                for n in range(2):
                    token_unit(("v", n), [("v", n, 0), ("v", n, 1)], COLS)
                taken(pe, ("t0", 0))
                taken(pe, ("t0", 1))
                for a in range(2):
                    ps = job_start(pe, ("ifT", a))
                    for t in range(TT):
                        ins = pe.transpose(ps[0:MH, t * P:(t + 1) * P], g_tok[:, t, a * MH:(a + 1) * MH], ident[:])
                    job_end(ins, ("ifT", a))
                for n in range(1, 4):
                    feature_unit(("qk", n), [("qk", 2 * n), ("qk", 2 * n + 1)])
                def column_gates():
                    ps = job_start(pe, ("colT",))
                    pe.wait_ge(m_ready, 1)
                    pe.wait_ge(em_ready, 1)
                    for a, row in enumerate((row_i, row_t)):
                        for t in range(TT):
                            at_ = (a * TT + t) * MH
                            ins = pe.transpose(ps[:, at_:at_ + MH], row[:, t * P:(t + 1) * P], ident[0:MH, 0:MH])
                    job_end(ins, ("colT",))

                def head_scores(hd):
                    ps = job_start(pe, ("negM", hd))
                    job_end(pe.matmul(ps, pick[:, hd, :], row_m[:], start=True, stop=True), ("negM", hd))
                    pe.wait_ge(qk_ready, MH + hd + 1)
                    for j in range(TT):
                        ps = job_start(pe, ("S", hd, j))
                        job_end(pe.matmul(ps[:, 0:T - j * P], qkc[:, MH + hd, j * P:(j + 1) * P], qkc[:, hd, j * P:T],
                                          start=True, stop=True), ("S", hd, j))

                def head_values(hd):
                    for b in range(2):
                        ps = job_start(pe, ("num", hd, b))
                        for i in range(2):
                            t = 2 * b + i
                            for j in range(t + 1):
                                taken(pe, ("S", hd, j))
                                ins = pe.matmul(ps[:, i * (MD + 1):(i + 1) * (MD + 1)], p_m[:, j, (t - j) * P:(t - j + 1) * P],
                                                v_aug[:, j, hd, :], start=(j == 0), stop=(j == t))
                        job_end(ins, ("num", hd, b))

                def hidden(kv, a):
                    w = unit(("c1", kv, a))
                    if a == 0:
                        pe.wait_ge(blk_lo_ready, kv + 1)
                    job = ("hid", kv)
                    ps = job_start(pe, job) if a == 0 else PS[:, plan.jobs[job][0], :]
                    for half in range(2):
                        dst = ps[:, half * 64:(half + 1) * 64]
                        for k in range(DC):
                            wh, wl = (x_[:, k * COLS + half * P:k * COLS + (half + 1) * P] for x_ in w)
                            bh, bl = (x_[:, a * DC + k, :, :].rearrange("p g n -> p (g n)") for x_ in (blk_hi, blk_lo))
                            pe.matmul(dst, wh, bh, start=(a == 0 and half == 0 and k == 0), stop=False)
                            pe.matmul(dst, wh, bl, start=False, stop=False)
                            ins = pe.matmul(dst, wl, bh, start=False, stop=(a == 1 and half == 1 and k == DC - 1))
                    if a == 1:
                        job_end(ins, job)
                    last_of(ins, ("c1", kv, a))

                feature_unit(("kcvc",), [("kcvc", "a"), ("kcvc", "b")])
                feature_unit(("o", 0), [("o", 0), ("o", 1)])
                column_gates()
                taken(pe, ("v", 1, 1))
                head_scores(0)
                feature_unit(("o", 1), [("o", 2), ("o", 3)])
                head_values(0)
                head_scores(1)
                feature_unit(("kk",), [("kk", "a"), ("kk", "b")])
                head_values(1)
                head_scores(2)
                hidden(0, 0)
                hidden(0, 1)
                head_values(2)
                head_scores(3)
                feature_unit(("qn", 0), [("qn", 0, "a"), ("qn", 0, "b")])
                head_values(3)
                hidden(1, 0)
                hidden(1, 1)
                ps = job_start(pe, ("kcmp",))
                taken(pe, ("hid", 0))
                for g in range(NG):
                    for half in range(2):
                        ins = pe.matmul(ps[g * ND:(g + 1) * ND, 0:32], w2[:, 0, half, :], hid[:, 0, half, g * 32:(g + 1) * 32],
                                        start=(half == 0), stop=(half == 1))
                job_end(ins, ("kcmp",))
                feature_unit(("qn", 1), [("qn", 1, "a"), ("qn", 1, "b")])
                for hd in range(MH):
                    ps = job_start(pe, ("hT", hd))
                    pe.wait_ge(hm_normed, hd + 1)
                    for t in range(TT):
                        ins = pe.transpose(ps[:, t * P:(t + 1) * P], hm[:, hd, t * P:(t + 1) * P], ident[:])
                    job_end(ins, ("hT", hd))
                ps = job_start(pe, ("vcmp",))
                pe.wait_ge(hid_rep_ready, 1)
                for g in range(NG):
                    for half in range(2):
                        ins = pe.matmul(ps[:, g * ND:(g + 1) * ND], hid_rep[:, half, g, :, :].rearrange("p h n -> p (h n)"),
                                        w2[:, 1, half, :], start=(half == 0), stop=(half == 1))
                job_end(ins, ("vcmp",))
                taken(pe, ("kcmp",))
                taken(pe, ("qn", 1, "b"))
                taken(pe, ("kk", "b"))

                def cmp_scores(t):
                    for g in range(NG):
                        rows = slice(g * ND, (g + 1) * ND)
                        ps = job_start(pe, ("sc", t, g))
                        for hh in range(HG):
                            ins = pe.matmul(ps[:, hh * 32:(hh + 1) * 32], qn[rows, hh, t * P:(t + 1) * P], k_cmp[rows, :],
                                            start=True, stop=True)
                        job_end(ins, ("sc", t, g))

                def gate_chunk(cch):
                    if cch % 2 == 0:
                        gate_parts[:] = unit(GATES[cch // 2])
                    feature_chunk(gate_parts, cch % 2, gate_job(cch))

                gate_parts = []
                cmp_scores(0)
                for t in range(TT):
                    if t + 1 < TT:
                        cmp_scores(t + 1)
                    gate_chunk(t)
                    ps = job_start(pe, ("pcT", t))
                    pe.wait_ge(p_c_ready, t + 1)
                    for g in range(NG):
                        ins = pe.transpose(ps[:, g * P:(g + 1) * P], p_c[:, 4 * g:4 * g + 4, :].rearrange("p h n -> p (h n)"), ident[:])
                    job_end(ins, ("pcT", t))
                    ps = job_start(pe, ("oc", t))
                    taken(pe, ("pcT", t))
                    pe.wait_ge(v_bd_ready, 1)
                    for g in range(NG):
                        ins = pe.matmul(ps[:, g * COLS:(g + 1) * COLS], pt_c[:, g, :], v_bd[:, g, :, :].rearrange("p h e -> p (h e)"),
                                        start=True, stop=True)
                    job_end(ins, ("oc", t))

                def nsa_scores(s):
                    t, g, hh = STEPS[s]
                    rows = slice(g * ND, (g + 1) * ND)
                    for br, name in enumerate(("ss", "sw")):
                        blocks = blocks_of(t)[br]
                        n = P * len(blocks)
                        ps = job_start(pe, (name, s))
                        pe.matmul(ps[:, 0:n], qn[rows, hh, t * P:(t + 1) * P], ksw[rows, br, blocks[0] * P:(t + 1) * P],
                                  start=True, stop=False)
                        if br == 1 and t - blocks[0] == WINDOW // P:
                            pe.matmul(ps[:, 0:P], ident_b[:], left_b[:], start=False, stop=False)
                        job_end(pe.matmul(ps[:, n - P:n], ident_b[:], diag_b[:], start=False, stop=True), (name, s))

                def nsa_transposes(s):
                    t = STEPS[s][0]
                    for br, (name, score, p) in enumerate((("ts", "ss", p_s), ("tw", "sw", p_w))):
                        ps = job_start(pe, (name, s))
                        taken(pe, (score, s))
                        for j in range(len(blocks_of(t)[br])):
                            ins = pe.transpose(ps[:, j * P:(j + 1) * P], p[s % 2][:, j * P:(j + 1) * P], ident[:])
                        job_end(ins, (name, s))

                def nsa_values(s):
                    t, g, hh = STEPS[s]
                    job = ("o_nsa", t, g)
                    ps = job_start(pe, job) if hh == 0 else PS[:, plan.jobs[job][0], :]
                    for br, (name, pt) in enumerate((("ts", pt_s), ("tw", pt_w))):
                        taken(pe, (name, s))
                        blocks = blocks_of(t)[br]
                        at_ = (2 * hh + br) * ND
                        for n, j in enumerate(blocks):
                            ins = pe.matmul(ps[:, at_:at_ + ND], pt[s % 2][:, n * P:(n + 1) * P], vsw[:, j, br, g * ND:(g + 1) * ND],
                                            start=(n == 0), stop=(n == len(blocks) - 1))
                    if hh == HG - 1:
                        job_end(ins, job)

                pe.wait_ge(mixer_consts, 1)
                nsa_scores(0)
                for s in range(len(STEPS)):
                    if s + 1 < len(STEPS):
                        nsa_scores(s + 1)
                    if s in chunk_at:
                        gate_chunk(chunk_at[s])
                    nsa_transposes(s)
                    if s:
                        nsa_values(s - 1)
                nsa_values(len(STEPS) - 1)
                pe.wait_ge(o_acc_ready, 1)
                for fc in range(4):
                    ps = job_start(pe, ("oT", fc))
                    for t in range(TT):
                        ins = pe.transpose(ps[:, t * P:(t + 1) * P], o_acc[:, t, fc * P:(fc + 1) * P], ident[:])
                    job_end(ins, ("oT", fc))
                gate_chunk(2 * DC - 2)
                gate_chunk(2 * DC - 1)
                pe.wait_ge(hm_lo_ready, 1)
                for fc in range(4):
                    taken(pe, ("oT", fc))
                for j in range(2):
                    feature_unit(("um", j), [("ym", 4 * j + n) for n in range(4)], hm_hi, hm_lo, 4, T)
                    feature_unit(("un", j), [("yn", 4 * j + n) for n in range(4)], o_hi, o_lo, 4, T)
                chunks_as_they_come(unit(("wo", 0)), [("y1", 0), ("y1", 1)], 0, 2 * DC)
                for n in range(1, 4):
                    feature_unit(("wo", n), [("y1", 2 * n), ("y1", 2 * n + 1)])

            pe.wait_ge(consts_ready, 1)
            pe.wait_ge(x_landed, 16)
            for cch in range(DC):
                ps = job_start(pe, ("x", cch))
                for t in range(TT):
                    ins = pe.transpose(ps[:, t * P:(t + 1) * P], x_tok[:, t, cch * P:(cch + 1) * P], ident[:])
                job_end(ins, ("x", cch))
            pe.wait_ge(rows_landed, 16 * 9)
            ps = job_start(pe, ("cols", 1))
            job_end(pe.transpose(ps[:, 0:120], rows1[:], ident[0:120, 0:120]), ("cols", 1))
            ps = job_start(pe, ("cols", 2))
            job_end(pe.transpose(ps[:, 0:81], rows2[:], ident[0:81, 0:81]), ("cols", 2))
            pre_norm(0)
            ps = job_start(pe, ("ada0",))
            pe.wait_ge(ada_summed, 1)
            for j in range(2 * ADA_FIRST):
                ins = pe.matmul(ps[:, j:j + 1], chunk(ada_acc0, j), ones[:, 0:1], start=True, stop=True)
            job_end(ins, ("ada0",))

            def ffn_y(f):
                return lambda cch: (("y", f, cch % 4), cch // 4)

            ffn_up(0)
            ffn_down(0)
            post_norm(0, ffn_y(0))
            pre_norm(1)
            mixer()
            post_norm(1, lambda cch: (("y1", cch),))
            pre_norm(2)
            ffn_up(1)
            ffn_down(1)
            post_norm(2, ffn_y(1))
            for cch in range(DC):
                h_updated(pe, 2, cch)
                ps = job_start(pe, ("out", cch))
                for t in range(TT):
                    ins = pe.transpose(ps[:, t * P:(t + 1) * P], h[:, cch, t * P:(t + 1) * P], ident[:])
                job_end(ins, ("out", cch))


_INS = ['x', 'c', 'w_ada', 'b_ada', 'norm_gains', 'ffn_wg', 'ffn_wu', 'ffn_wd', 'w_in', 'mlstm_conv_w', 'mlstm_conv_b', 'mlstm_gate_b', 'mlstm_head_gain', 'cmp_pe', 'cmp_w1', 'cmp_b1', 'cmp_w2', 'cmp_b2', 'w_up_mlstm', 'w_up_nsa', 'w_out']
_OUTS = [((1, 512, 1024), 'float32')]


def kernel(**inputs):
    import numpy as _np
    import concourse.bacc as _bacc
    from concourse import mybir as _mybir
    from concourse.bass_utils import run_bass_kernel_spmd as _run

    nc = _bacc.Bacc("TRN2", target_bir_lowering=False, num_devices=1)
    arrays, args = {}, []
    for name in _INS:
        a = _np.ascontiguousarray(inputs[name])
        if a.dtype.kind in "iu":
            a = a.astype(_np.int64)
        arrays[f"in_{name}_dram"] = a
        args.append(nc.dram_tensor(f"in_{name}_dram", a.shape, _mybir.dt.from_np(a.dtype), kind="ExternalInput").ap())
    for i, (shape, dtype) in enumerate(_OUTS):
        dt = _mybir.dt.from_np(_np.dtype(dtype))
        args.append(nc.dram_tensor(f"out_{i}_dram", shape, dt, kind="ExternalOutput").ap())
    build_layer(nc, *args)
    r = _run(nc, [arrays], core_ids=[0])
    got = tuple(r.results[0][f"out_{i}_dram"] for i in range(len(_OUTS)))
    return got[0]
```

```python
import concourse.bass as bass
from concourse import mybir
from contextlib import ExitStack

F32 = mybir.dt.float32
F32R = mybir.dt.float32r
BF16 = mybir.dt.bfloat16
ALU = mybir.AluOpType
ACT = mybir.ActivationFunctionType
AX = mybir.AxisListType

P = 128
T = 512
TT = T // P
D = 1024
DC = D // P
FF = 2816
FC = FF // P
COLS = 256
UP_ITERS = FF // COLS
DOWN_K = (0, 8, 16, FC)
EPS_SUM = 1e-6 * D
ROOT_D = float(D) ** 0.5
NEG = -1.0e30
ADA_FIRST = 8
SHIFT_A = slice(0, D // 2)
SHIFT_B = slice(D // 2, D * 3 // 4)
SHIFT_C = slice(D * 3 // 4, D)
SCALE = slice(D, 2 * D)

MH, MD = 4, 128
NH, ND, NG, HG = 8, 64, 2, 4
NCMP = 31
CB = 32
WINDOW = 256
GATE_N = 3 * NH
GATE_ROWS = 96
OFF_Q, OFF_K, OFF_V, OFF_O, OFF_IF = 0, 512, 1024, 1536, 2048
OFF_QN = 2056
OFF_KC, OFF_VC, OFF_KS, OFF_VS, OFF_KW, OFF_VW = (2568 + 128 * j for j in range(6))
OFF_GN, OFF_GA, OFF_GB = 3336, 3360, 4384


class Count:

    def __init__(self, sem):
        self.sem, self.n = sem, 0

    def tick(self, ins):
        ins.then_inc(self.sem, 1)
        self.n += 1
        return self.n

    def wait(self, eng, n=None):
        eng.wait_ge(self.sem, self.n if n is None else n)


class Plan:

    def __init__(self):
        self.bank_count = [0] * 8
        self.jobs = {}
        self.landed_count = [0, 0]
        self.raw_count = 0
        self.raws = {}
        self.weight_count = 0
        self.weights = {}

    def job(self, name, bank):
        assert name not in self.jobs, name
        self.jobs[name] = (bank, self.bank_count[bank], 0)
        self.bank_count[bank] += 1

    def loop_jobs(self, iters, body):
        before = list(self.bank_count)
        for name, bank in body:
            self.job(name, bank)
        step = [a - b for a, b in zip(self.bank_count, before)]
        for name, bank in body:
            self.jobs[name] = self.jobs[name][:2] + (step[bank],)
        self.bank_count = [b + s * iters for b, s in zip(before, step)]

    def unit(self, name, dmas=1):
        slot = self.raw_count % 2
        self.landed_count[slot] += 16 * dmas
        self.raws[name] = (slot, self.landed_count[slot], 0)
        self.raw_count += 1
        if name[0] != "ada":
            self.weights[name] = (self.weight_count, 0)
            self.weight_count += 1

    def loop_units(self, iters, body):
        before, w0, r0 = list(self.landed_count), self.weight_count, self.raw_count
        for name in body:
            self.unit(name)
        step = [a - b for a, b in zip(self.landed_count, before)]
        wstep = self.weight_count - w0
        assert (self.raw_count - r0) % 2 == 0 and wstep % 2 == 0
        for name in body:
            slot, value, _ = self.raws[name]
            self.raws[name] = (slot, value, step[slot])
            if name in self.weights:
                self.weights[name] = (self.weights[name][0], wstep)
        self.landed_count = [b + s * iters for b, s in zip(before, step)]
        self.weight_count = w0 + wstep * iters
        self.raw_count = r0 + (self.raw_count - r0) * iters


def build_layer(nc, x, c, w_ada, b_ada, norm_gains, ffn_wg, ffn_wu, ffn_wd, w_in, mlstm_conv_w, mlstm_conv_b,
                mlstm_gate_b, mlstm_head_gain, cmp_pe, cmp_w1, cmp_b1, cmp_w2, cmp_b2, w_up_mlstm, w_up_nsa,
                w_out, out):
    with ExitStack() as ctx:
        base = nc.sbuf_base + (-nc.sbuf_base) % 32
        at = [base]

        def sem(name):
            return ctx.enter_context(nc.semaphore(name))

        def place(name, shape, dt, offset=None):
            size = mybir.dt.size(dt)
            for n in shape[1:]:
                size *= n
            size += -size % 32
            if offset is None:
                offset = at[0]
                at[0] += size
            return nc.alloc_sbuf_tensor_at(name, shape, dt, offset=offset), offset + size

        h, _ = place("h", [P, DC, T], F32)
        u_at = at[0]
        u_hi, _ = place("u_hi", [P, DC, T], F32R)
        u_lo_at = at[0]
        u_lo, _ = place("u_lo", [P, DC, T], F32R)
        raw = [place(f"raw{s}", [P, DC * COLS], F32)[0] for s in range(2)]
        w_hi = [place(f"w_hi{s}", [P, DC * COLS], F32R)[0] for s in range(2)]
        w_lo = [place(f"w_lo{s}", [P, DC * COLS], F32R)[0] for s in range(2)]
        ident, _ = place("ident", [P, P], F32)
        ones, _ = place("ones", [P, P], F32)
        col1, _ = place("col1", [P, 120], F32)
        col2, _ = place("col2", [P, 81], F32)
        ada, _ = place("ada", [P, 9 * DC], F32)
        eps_col, _ = place("eps_col", [P, 1], F32)
        silu_c, _ = place("silu_c", [P, DC], F32)
        gain_a, _ = place("gain_a", [P, DC], F32)
        gain_g, _ = place("gain_g", [P, DC], F32)
        sq_at = at[0]
        sq = [place(f"sq{s}", [P, T], F32)[0] for s in range(2)]
        wt_at = at[0]
        wt = [place(f"wt{s}", [P, T], F32)[0] for s in range(2)]
        rs_at = at[0]
        rs, _ = place("rs", [P, T], F32)
        root_t, _ = place("root_t", [P, TT], F32)
        inv_t, _ = place("inv_t", [P, TT], F32)
        warm, _ = place("warm", [P, 1], F32)
        region = at[0]

        mid_hi, e = place("mid_hi", [P, FC, T], F32R, region)
        mid_lo, e = place("mid_lo", [P, FC, T], F32R, e)
        ada_acc, e = place("ada_acc", [P, 2, COLS], F32, e)
        ffn_end = e
        y_ffn, _ = place("y_ffn", [P, DC, T], F32, u_lo_at)
        ada_w, e = place("ada_w", [P, DC, ADA_FIRST * COLS], F32, region)
        x_tok, e = place("x_tok", [P, TT, D], F32, e)
        ada_acc0, e = place("ada_acc0", [P, ADA_FIRST * COLS], F32, e)
        c_col, e = place("c_col", [P, DC], F32, e)
        rows1, e = place("rows1", [120, P], F32, e)
        rows2, e = place("rows2", [81, P], F32, e)
        first_end = e
        out_tok, _ = place("out_tok", [P, TT, D], F32, region)

        qkc, e = place("qkc", [P, 2 * MH, T], F32, region)
        sig_o, e = place("sig_o", [P, MH, T], F32, e)
        v_aug, e = place("v_aug", [P, TT, MH, MD + 1], F32, e)
        p_m, e = place("p_m", [P, TT, T], F32, e)
        o_acc, a = place("o_acc", [P, TT, NH * ND], F32, region)
        p_s, a = zip(*[place(f"p_s{n}", [P, T], F32, a + 2048 * n) for n in range(2)])
        p_w, a = zip(*[place(f"p_w{n}", [P, 384], F32, a[1] + 1536 * n) for n in range(2)])
        pt_s, a = zip(*[place(f"pt_s{n}", [P, T], F32, a[1] + 2048 * n) for n in range(2)])
        pt_w, a = zip(*[place(f"pt_w{n}", [P, 384], F32, a[1] + 1536 * n) for n in range(2)])
        sig_b, a = place("sig_b", [P, DC, T], F32, a[1])
        assert a <= e
        hm_hi, a = place("hm_hi", [P, MH, T], F32R, region)
        hm_lo, a = place("hm_lo", [P, MH, T], F32R, a)
        hm, e = place("hm", [P, MH, T], F32, e)
        qn_at = e
        qn, e = place("qn", [P, 4, T], F32, e)
        ksw, e = place("ksw", [P, 2, T], F32, e)
        vsw, e = place("vsw", [P, TT, 2, P], F32, e)
        o_hi, a = place("o_hi", [P, 4, T], F32R, qn_at)
        o_lo, a = place("o_lo", [P, 4, T], F32R, a)
        assert a <= e
        sig_a_at = e
        sig_a, e = place("sig_a", [P, DC, T], F32, e)
        y_mix, _ = place("y_mix", [P, DC, T], F32, sig_a_at)
        late_at = e
        kv_2, a = place("kv_2", [P, 2, NG, T // 2], F32, sig_a_at)
        blk, a = place("blk", [P, 16, NG, 32], F32, a)
        blk_hi, a = place("blk_hi", [P, 16, NG, 32], F32R, a)
        kv_t, _ = place("kv_t", [P, 2, 2, T // 2], F32, a)
        blk_lo, a = place("blk_lo", [P, 16, NG, 32], F32R, a)
        assert a <= late_at
        row_i, a = place("row_i", [MH, T], F32, late_at)
        row_f, a = place("row_f", [MH, T], F32, a)
        row_t, a = place("row_t", [MH, T], F32, a)
        row_z, a = place("row_z", [MH, T], F32, a)
        row_s, late = place("row_s", [MH, T], F32, a)
        row_m, _ = place("row_m", [MH, T], F32, rs_at)
        v_bd, a = place("v_bd", [P, NG, HG, ND], F32, late_at)
        p_c, a = place("p_c", [P, NH, 32], F32, a)
        p_cmp = [p_c[:], sq[0][:, 0:NH * 32].rearrange("p (h n) -> p h n", n=32)]
        pt_c, a = place("pt_c", [P, NG, P], F32, a)
        hid_rep, a = place("hid_rep", [P, 2, NG, HG, 32], F32, a)
        o_tmp, a = place("o_tmp", [P, HG, 2, ND], F32, a)
        v_tmp, a = place("v_tmp", [P, NG, ND], F32, a)
        hid, a = place("hid", [P, 2, 2, 64], F32, a)
        hid_t = wt[1][0:64, :].rearrange("p (kv n) -> p kv n", kv=2)
        assert a <= late
        w2, late = place("w2", [P, 2, 2, ND], F32, late)
        k_cmp, late = place("k_cmp", [P, NG, 32], F32, late)
        b2_row, late = place("b2_row", [P, ND], F32, late)
        mask_row, late = place("mask_row", [P, T], F32, late)
        add_c, late = place("add_c", [P, TT, 32], F32, late)
        keep_c, late = place("keep_c", [P, TT, 32], F32, late)
        bd, late = place("bd", [P, HG], F32, late)
        ident_b, late = place("ident_b", [P, P], BF16, late)
        diag_b, late = place("diag_b", [P, P], BF16, late)
        left_b, late = place("left_b", [P, P], BF16, late)
        pick, late = place("pick", [MH, MH, P], F32, late)
        g_bias, late = place("g_bias", [MH, 2], F32, late)
        g_tok, late = place("g_tok", [P, TT, GATE_N], F32, late)
        g_rows = wt[0][64:64 + GATE_N, :]
        sig_n, late = place("sig_n", [P, TT, NH, 3], F32, late)
        cols, late = place("cols", [P, 2, TT, MH], F32, late)
        den, late = place("den", [P, MH, TT], F32, late)
        ssm, late = place("ssm", [P, MH, TT], F32, late)
        max_c, late = place("max_c", [P, NH], F32, late)
        sum_c, late = place("sum_c", [P, NH], F32, late)
        n_max, late = place("n_max", [P, 32, 2], F32, late)
        sums, late = place("sums", [P, 32, 2], F32, late)
        w_sw, late = place("w_sw", [P, HG, 2], F32, late)
        eps_m, late = place("eps_m", [P, 1], F32, late)

        PS = ctx.enter_context(nc.psum_tensor("PS", [P, 8, 512], F32))

        bank_full = [sem(f"bank_full{b}") for b in range(8)]
        bank_free = [sem(f"bank_free{b}") for b in range(8)]
        raw_landed = [sem(f"raw_landed{s}") for s in range(2)]
        hi_ready = sem("hi_ready")
        lo_ready = sem("lo_ready")
        w_used = sem("w_used")
        ada_summed = sem("ada_summed")
        consts_ready = sem("consts_ready")
        rows_landed = sem("rows_landed")
        c_landed = sem("c_landed")
        x_landed = sem("x_landed")
        scale_landed = [sem(f"scale_landed{j}") for j in range(DC)]
        shift_landed = [[sem(f"shift_{part}_landed{n}") for n in range(2)] for part in "ab"]
        first_summed = sem("first_summed")
        shift_c_scaled = sem("shift_c_scaled")
        shift_c_summed = sem("shift_c_summed")
        silu_c_ready = sem("silu_c_ready")
        h_ready = [sem("h_even_ready"), sem("h_odd_ready")]
        sq_ready = sem("sq_ready")
        sq_used = sem("sq_used")
        w_scaled = sem("w_scaled")
        u_hi_ready = sem("u_hi_ready")
        u_ready = sem("u_ready")
        mid_hi_ready = sem("mid_hi_ready")
        mid_ready = sem("mid_ready")
        ysq_ready = sem("ysq_ready")
        ysum_ready = sem("ysum_ready")
        delta_ready = sem("delta_ready")
        tile_sums_ready = sem("tile_sums_ready")
        root_ready = sem("root_ready")
        inv_ready = sem("inv_ready")
        stored = sem("stored")
        small_landed = sem("small_landed")
        mixer_consts = sem("mixer_consts")
        soft_ready = sem("soft_ready")
        conv_first = sem("conv_first")
        qk_ready = sem("qk_ready")
        m_ready = sem("m_ready")
        em_ready = sem("em_ready")
        arg_ready = sem("arg_ready")
        e_ready = sem("e_ready")
        kv_moved = sem("kv_moved")
        hm_ready = sem("hm_ready")
        sig_o_ready = sem("sig_o_ready")
        gates_ready = sem("gates_ready")
        ssm_root = sem("ssm_root")
        blk_ready = sem("blk_ready")
        blk_hi_ready = sem("blk_hi_ready")
        blk_lo_ready = sem("blk_lo_ready")
        hm_normed = sem("hm_normed")
        hid_rep_ready = sem("hid_rep_ready")
        v_bd_ready = sem("v_bd_ready")
        arg_c_ready = sem("arg_c_ready")
        e_c_ready = sem("e_c_ready")
        p_c_ready = sem("p_c_ready")
        sig_n_ready = sem("sig_n_ready")
        n_max_ready = sem("n_max_ready")
        o_hi_ready = sem("o_hi_ready")
        o_acc_ready = sem("o_acc_ready")
        hm_lo_ready = sem("hm_lo_ready")
        merged = sem("merged")
        dve_step = sem("dve_step")
        act_step = sem("act_step")
        pool_step = sem("pool_step")

        plan = Plan()

        def plan_norm(kind, s):
            plan.job((kind, s), 6)
            plan.job(("r", kind, s), 7)

        plan.job(("cols", 1), 0)
        plan.job(("cols", 2), 1)
        for cch in range(DC):
            plan.job(("x", cch), 2 + cch % 4)
        plan_norm("pre", 0)
        for part, bank in (("scale", 0), ("a", 1), ("bc", 5)):
            plan.job(("ada0", part), bank)

        def has_ada(f, n):
            return n == 2 or (f == 0 and n == 5)

        def ada_number(f, it, n):
            return 2 * UP_ITERS + (2 * it + n // 3 if f == 0 else 4 + it)

        def plan_ffn_up(f):
            plan.unit(("g0", f))
            plan.loop_units(UP_ITERS, [("up", f), ("ada", "a"), ("gate", f), ("ada", "b")] if f == 0
                            else [("up", f), ("gate", f)])
            plan.loop_jobs(UP_ITERS, [(("g", f, 0), 0), (("g", f, 1), 1), (("u", f, 0), 2), (("u", f, 1), 3)]
                           + ([(("ada", "ab"), 7)] if f == 0 else []))

        def plan_ffn_down(f, following):
            for it in range(2):
                for n in range(6):
                    if (it, n) != (0, 0):
                        plan.unit(("d", f, it, n))
                    if has_ada(f, n):
                        plan.unit(("ada", f, it, n))
            for name, dmas in following:
                plan.unit(name, dmas)
            plan.loop_jobs(2, [(("y", f, n), n) for n in range(4)]
                           + [(("ada", f, n), 7) for n in (2, 5) if has_ada(f, n)])

        unit_end = {}

        def plan_unit(name, dmas, jobs, ends=True):
            plan.unit(name, dmas)
            for job, bank in jobs:
                plan.job(job, bank)
            unit_end[name] = jobs[-1][0] if ends else None

        GATES = [("ga", n) for n in range(4)] + [("gb", n) for n in range(4)]
        MIX = ([("qk", 0), ("vsw",), ("gt",), ("v", 0), ("v", 1)] + [("qk", n) for n in range(1, 4)]
               + [("kcvc",), ("o", 0), ("o", 1), ("kk",), ("qn", 0), ("c1", 0, 0), ("c1", 0, 1), ("qn", 1), ("c1", 1, 0),
                  ("c1", 1, 1)] + GATES + [("um", 0), ("un", 0), ("um", 1), ("un", 1)] + [("wo", n) for n in range(4)])
        STEPS = [(t, g, hh) for t in range(TT) for g in range(NG) for hh in range(HG)]
        NSA_CHUNKS = 2 * len(GATES) - TT - 2
        chunk_at = {}
        for n in range(NSA_CHUNKS):
            chunk_at[n * len(STEPS) // NSA_CHUNKS] = TT + n

        def gate_job(cch):
            return GATES[cch // 2][0:1] + (cch % DC,)

        def plan_head(hd):
            plan.job(("negM", hd), 4)
            for j in range(TT):
                plan.job(("S", hd, j), j)

        def plan_values(hd):
            plan.job(("num", hd, 0), 6)
            plan.job(("num", hd, 1), 5)

        def plan_mixer():
            plan_unit(("qk", 0), 1, [(("qk", 0), 2), (("qk", 1), 3)])
            plan_unit(("vsw",), 2, [(("vsw", 0), 0), (("vsw", 1), 1)])
            plan_unit(("gt",), 3, [(("gt",), 4)])
            plan_unit(("v", 0), 1, [(("v", 0, 0), 5), (("v", 0, 1), 6)])
            plan.job(("gT",), 0)
            plan_unit(("v", 1), 1, [(("v", 1, 0), 2), (("v", 1, 1), 3)])
            for n in range(1, 4):
                bank = 2 + 2 * n % 6
                plan_unit(("qk", n), 1, [(("qk", 2 * n), bank), (("qk", 2 * n + 1), bank + 1)])
            plan_unit(("kcvc",), 1, [(("kcvc", "a"), 4), (("kcvc", "b"), 5)])
            plan_unit(("o", 0), 1, [(("o", 0), 6), (("o", 1), 7)])
            plan.job(("colT",), 0)
            plan_head(0)
            plan_unit(("o", 1), 1, [(("o", 2), 7), (("o", 3), 4)])
            plan_values(0)
            plan_head(1)
            plan_unit(("kk",), 2, [(("kk", "a"), 7), (("kk", "b"), 4)])
            plan_values(1)
            plan_head(2)
            plan_unit(("qn", 0), 4, [(("qn", 0, "a"), 7), (("qn", 0, "b"), 4)])
            plan_values(2)
            plan_head(3)
            plan_unit(("c1", 0, 0), 1, [(("hid", 0), 7)], ends=False)
            plan.unit(("c1", 0, 1))
            unit_end[("c1", 0, 1)] = ("hid", 0)
            plan_values(3)
            plan.job(("hidT", 0), 7)
            plan_unit(("qn", 1), 4, [(("qn", 1, "a"), 0), (("qn", 1, "b"), 1)])
            plan.job(("kcmp",), 4)
            for hd in range(MH):
                plan.job(("hT", hd), (hd + 2) % 4)
            plan_unit(("c1", 1, 0), 1, [(("hid", 1), 7)], ends=False)
            plan.unit(("c1", 1, 1))
            unit_end[("c1", 1, 1)] = ("hid", 1)
            plan.job(("hidT", 1), 6)
            plan.job(("vcmp",), 5)
            for t in range(TT):
                plan.job(("sc", t), t % 2)
                plan.job(("pcT", t), 4 + t % 2)
                plan.job(("oc", t), 6)
            for s, (t, g, hh) in enumerate(STEPS):
                plan.job(("ss", s), 2 * (s % 2))
                plan.job(("sw", s), 2 * (s % 2) + 1)
                plan.job(("ts", s), 4)
                plan.job(("tw", s), 5)
                if hh == 0:
                    plan.job(("o_nsa", t, g), 6)
            for n, name in enumerate(GATES):
                plan_unit(name, 1, [(gate_job(2 * n), 7), (gate_job(2 * n + 1), 7 if n < len(GATES) - 1 else 6)])
            for fc in range(4):
                plan.job(("oT", fc), fc)
            for j in range(2):
                plan_unit(("um", j), 1, [(("ym", 4 * j + n), n) for n in range(4)])
                plan_unit(("un", j), 1, [(("yn", 4 * j + n), 4 + n) for n in range(4)])
            for n in range(4):
                plan_unit(("wo", n), 1, [(("y1", 2 * n), 2 * (n % 2)), (("y1", 2 * n + 1), 2 * (n % 2) + 1)])
            plan_norm("post", 1)

        plan_ffn_up(0)
        plan_ffn_down(0, [])
        plan_norm("post", 0)
        plan_norm("pre", 1)
        plan_mixer()
        plan_norm("pre", 2)
        plan_ffn_up(1)
        plan_ffn_down(1, [])
        plan_norm("post", 2)
        for cch in range(DC):
            plan.job(("out", cch), 2 + cch % 4)
        assert [n for n in plan.weights if n in MIX] == MIX

        def after(name):
            n = MIX.index(name) + 1
            return MIX[n] if n < len(MIX) else ("g0", 1)

        def blocks_of(t):
            return range(0, t + 1), range(max(0, t - WINDOW // P), t + 1)

        def job_start(eng, name, i=0):
            bank, k, step = plan.jobs[name]
            eng.wait_ge(bank_free[bank], k + 1 + i * step)
            return PS[:, bank, :]

        def job_end(ins, name):
            ins.then_inc(bank_full[plan.jobs[name][0]], 1)

        def job_result(eng, name, i=0):
            bank, k, step = plan.jobs[name]
            eng.wait_ge(bank_full[bank], k + 1 + i * step)
            return PS[:, bank, :]

        def job_read(ins, name):
            ins.then_inc(bank_free[plan.jobs[name][0]], 1)

        job_done = job_result
        mixer_used = 2

        def taken(eng, name, i=0, before=0):
            bank, k, step = plan.jobs[name]
            eng.wait_ge(bank_free[bank], k + 2 - before + i * step)

        def unit_landed(eng, name, i=0):
            slot, value, step = plan.raws[name]
            eng.wait_ge(raw_landed[slot], value + i * step)
            return raw[slot]

        def w_number(name, i=0):
            n, step = plan.weights[name]
            return n + 1 + i * step, n % 2

        def y_job(s, cch):
            return (("y1", cch),) if s == 1 else (("y", s // 2, cch % 4), cch // 4)

        def h_updated(eng, adds, cch):
            eng.wait_ge(h_ready[cch % 2], adds * DC // 2 + cch // 2 + 1)

        def bcast(ap, shape):
            return ap.broadcast_to(shape)

        def chunk(t, j):
            return t[:, j * P:(j + 1) * P]

        block = ctx.enter_context(nc.Block())

        dve_misc = sem("dve_misc")
        @block.sync
        def _(sp):
            sp.dma_start(c_col[:], c.rearrange("b (p j) -> p (b j)", j=DC)).then_inc(c_landed, 16)
            sp.dma_start(x_tok[:], x[0].rearrange("(t p) d -> p t d", p=P)).then_inc(x_landed, 16)
            sp.dma_start(rows1[0:72, :], b_ada.rearrange("l (r n) -> (l r) n", n=P)).then_inc(rows_landed, 16)
            sp.dma_start(rows1[72:120, :], norm_gains.rearrange("l g (r n) -> (l g r) n", n=P)).then_inc(rows_landed, 16)
            sp.dma_start(rows2[0:32, :], mlstm_conv_w.rearrange("l w o (r n) -> (l w o r) n", n=P)).then_inc(rows_landed, 16)
            sp.dma_start(rows2[32:40, :], mlstm_conv_b.rearrange("l (r n) -> (l r) n", n=P)).then_inc(rows_landed, 16)
            sp.dma_start(rows2[40:44, :], mlstm_head_gain.rearrange("l (r n) -> (l r) n", n=P)).then_inc(rows_landed, 16)
            sp.dma_start(rows2[44:48, :], cmp_b1.rearrange("l k (r n) -> (l k r) n", n=P)).then_inc(rows_landed, 16)
            sp.dma_start(rows2[48:80, :], cmp_pe.rearrange("l k (r a) n -> (l k r) (a n)", a=2)).then_inc(rows_landed, 16)
            sp.dma_start(rows2[80:81, 0:ND], cmp_b2[:, 0, :]).then_inc(rows_landed, 16)
            sp.dma_start(rows2[80:81, ND:P], cmp_b2[:, 0, :]).then_inc(rows_landed, 16)
            ada_rows = w_ada[0].rearrange("(p j) n -> p j n", j=DC)

            for j in range(DC):
                sp.dma_start(ada_w[:, j, SCALE], ada_rows[:, j, SCALE]).then_inc(scale_landed[j], 16)

            def load_shift(part, cols):
                for n in range(2):
                    rows = slice(n * DC // 2, (n + 1) * DC // 2)
                    sp.dma_start(ada_w[:, rows, cols], ada_rows[:, rows, cols]).then_inc(shift_landed[part][n], 16)

            load_shift(0, SHIFT_A)

            last = {0: None, 1: None}

            def slot_empty(name):
                slot = plan.raws[name][0]
                if last[slot] is not None:
                    sp.wait_ge(*last[slot])
                return slot

            def load(name, pieces):
                slot = slot_empty(name)
                for dst, src in pieces:
                    sp.dma_start(raw[slot][:, dst[0]:dst[1]].rearrange("p (k n) -> p k n", n=dst[2]), src).then_inc(raw_landed[slot], 16)
                if name[0] == "ada":
                    ada_seen[0] += 1
                    last[slot] = (ada_summed, ada_seen[0])
                else:
                    last[slot] = (lo_ready, w_number(name)[0])

            ada_seen = [1]

            def rows_of(w, r0, r1, c0, cn):
                return w[r0 * P:r1 * P, bass.ds(c0, cn)].rearrange("(k p) n -> p k n", p=P)

            def dense(kn, n):
                return (0, kn * n, n)

            def ada_src(a):
                return ada_rows[:, :, bass.ds(a * COLS, COLS)]

            def load_ffn_up(f):
                load(("g0", f), [(dense(DC, COLS), rows_of(ffn_wg[0, f], 0, DC, 0, COLS))])
                if f == 0:
                    load_shift(1, slice(SHIFT_B.start, SHIFT_C.stop))
                wslot = plan.raws[("up", f)][0]
                gslot = plan.raws[("gate", f)][0]
                g_n = w_number(("g0", f))[0]

                def raw3(slot):
                    return raw[slot][:].rearrange("p (k n) -> p k n", n=COLS)

                def iteration(i, last_one):
                    sp.wait_ge(lo_ready, g_n + 2 * i - f)
                    sp.dma_start(raw3(wslot), rows_of(ffn_wu[0, f], 0, DC, i * COLS, COLS)).then_inc(raw_landed[wslot], 16)
                    if f == 0:
                        aslot = plan.raws[("ada", "a")][0]
                        sp.wait_ge(ada_summed, 2 * i + 1)
                        sp.dma_start(raw3(aslot), ada_src(ADA_FIRST + 2 * i)).then_inc(raw_landed[aslot], 16)
                        sp.wait_ge(lo_ready, g_n + 1 + 2 * i)
                    else:
                        sp.wait_ge(lo_ready, g_n + 2 * i)
                    src = rows_of(ffn_wd[0, f], DOWN_K[0], DOWN_K[1], 0, COLS) if last_one else \
                        rows_of(ffn_wg[0, f], 0, DC, i * COLS + COLS, COLS)
                    sp.dma_start(raw3(gslot), src).then_inc(raw_landed[gslot], 16)
                    if f == 0:
                        sp.wait_ge(ada_summed, 2 * i + 2)
                        sp.dma_start(raw3(aslot), ada_src(ADA_FIRST + 1 + 2 * i)).then_inc(raw_landed[aslot], 16)

                with sp.Fori(0, UP_ITERS - 1) as i:
                    iteration(i, False)
                iteration(UP_ITERS - 1, True)
                n_last = g_n + 2 * UP_ITERS
                if f == 0:
                    ada_seen[0] = 1 + 2 * UP_ITERS
                    last[gslot] = (lo_ready, n_last)
                    last[1 - gslot] = (ada_summed, ada_seen[0])
                else:
                    last[gslot] = (lo_ready, n_last)
                    last[1 - gslot] = (lo_ready, n_last - 1)

            def load_ffn_down(f):
                for it in range(2):
                    for n in range(6):
                        if (it, n) != (0, 0):
                            k0, k1 = DOWN_K[n % 3], DOWN_K[n % 3 + 1]
                            c0 = (2 * it + n // 3) * COLS
                            load(("d", f, it, n), [(dense(k1 - k0, COLS), rows_of(ffn_wd[0, f], k0, k1, c0, COLS))])
                        if has_ada(f, n):
                            load(("ada", f, it, n), [(dense(DC, COLS), ada_src(ADA_FIRST + ada_number(f, it, n)))])

            def load_mixer():
                w3 = w_in[0].rearrange("(k p) n -> p k n", p=P)

                def columns(c0, cn):
                    return w3[:, :, c0:c0 + cn]

                def load_parts(name, n, parts):
                    slot = slot_empty(name)
                    for view, src in parts(raw[slot]):
                        sp.dma_start(view, src).then_inc(raw_landed[slot], 16)
                    last[slot] = (lo_ready, w_number(name)[0])

                def vsw_parts(slot):
                    s3 = slot[:].rearrange("p (k n) -> p k n", n=COLS)
                    return [(s3[:, :, 0:P], columns(OFF_VS, P)), (s3[:, :, P:COLS], columns(OFF_VW, P))]

                def gate_parts(slot):
                    s3 = slot[:, 0:DC * GATE_ROWS].rearrange("p (k n) -> p k n", n=GATE_ROWS)
                    return [(s3[:, :, 32 * n:32 * n + 32], columns(off, 32)) for n, off in enumerate((OFF_IF, OFF_IF + MH, OFF_GN))]

                def kk_parts(slot):
                    s3 = slot[:].rearrange("p (k n) -> p k n", n=COLS)
                    return [(s3[:, :, 0:P], columns(OFF_KS, P)), (s3[:, :, P:COLS], columns(OFF_KW, P))]

                def qn_parts(n):
                    def parts(slot):
                        s3 = slot[:].rearrange("p (k n) -> p k n", n=COLS)
                        return [(s3[:, :, (2 * cc + g) * ND:(2 * cc + g + 1) * ND],
                                 columns(OFF_QN + (g * HG + 2 * n + cc) * ND, ND)) for cc in range(2) for g in range(NG)]
                    return parts

                load(("qk", 0), [(dense(DC, COLS), columns(OFF_Q, COLS))])
                load_parts(("vsw",), COLS, vsw_parts)
                load_parts(("gt",), GATE_ROWS, gate_parts)
                job_done(sp, ("y", 0, 3), 1)
                for kv in range(2):
                    sp.dma_start(w2[:, kv, :, :], cmp_w2[0, kv].rearrange("(h p) e -> p h e", p=P)).then_inc(small_landed, 16)
                sp.dma_start(b2_row[:], cmp_b2[0, 1:2, :].broadcast_to([P, ND])).then_inc(small_landed, 16)
                for a in range(2):
                    sp.dma_start(g_bias[:, a:a + 1], mlstm_gate_b[0, a * MH:(a + 1) * MH].rearrange("(p o) -> p o", o=1)).then_inc(small_landed, 16)
                for n in range(2):
                    load(("v", n), [(dense(DC, COLS), columns(OFF_V + n * COLS, COLS))])
                for n in range(1, 4):
                    load(("qk", n), [(dense(DC, COLS), columns(OFF_Q + n * COLS, COLS))])
                load(("kcvc",), [(dense(DC, COLS), columns(OFF_KC, COLS))])
                for n in range(2):
                    load(("o", n), [(dense(DC, COLS), columns(OFF_O + n * COLS, COLS))])
                load_parts(("kk",), COLS, kk_parts)
                for kv in range(2):
                    load_parts(("qn", kv), COLS, qn_parts(kv))
                    for a in range(2):
                        load(("c1", kv, a), [(dense(DC, COLS), rows_of(cmp_w1[0, kv], a * DC, (a + 1) * DC, 0, COLS))])
                for name, off in (("ga", OFF_GA), ("gb", OFF_GB)):
                    for n in range(4):
                        load((name, n), [(dense(DC, COLS), columns(off + n * COLS, COLS))])
                for j in range(2):
                    load(("um", j), [(dense(4, T), rows_of(w_up_mlstm[0], 0, 4, j * T, T))])
                    load(("un", j), [(dense(4, T), rows_of(w_up_nsa[0], 0, 4, j * T, T))])
                for n in range(4):
                    load(("wo", n), [(dense(DC, COLS), rows_of(w_out[0], 0, DC, n * COLS, COLS))])

            load_ffn_up(0)
            load_ffn_down(0)
            load_mixer()
            load_ffn_up(1)
            load_ffn_down(1)
            out3 = out[0].rearrange("(t p) d -> p t d", p=P)
            for cch in range(1, DC, 2):
                at_ = slice((cch - 1) * P, (cch + 1) * P)
                taken(sp, ("out", cch - 1))
                taken(sp, ("out", cch))
                sp.dma_start(out3[:, :, at_], out_tok[:, :, at_]).then_inc(stored, 16)
            sp.wait_ge(stored, 16 * DC // 2)

        @block.gpsimd
        def _(pool):
            step = Count(pool_step)
            step.tick(pool.memset(ident[:], 0.0))
            step.tick(pool.memset(ones[:], 1.0))
            step.tick(pool.memset(eps_col[:], EPS_SUM))
            step.wait(pool)
            for b in range(8):
                pool.sem_inc(bank_free[b], 1)
            pool.affine_select(out=ident[:], in_=ident[:], compare_op=ALU.not_equal, fill=1.0, base=0,
                               pattern=[[-1, P]], channel_multiplier=1).then_inc(consts_ready, 1)

            def sum_y_squares(sums):
                for cch in range(DC - 2):
                    n = sums * (DC - 2) + cch + 1
                    pool.wait_ge(ysq_ready, sums * DC + cch + 1)
                    if cch == 0:
                        ins = pool.tensor_copy(rs[:], sq[cch % 2][:])
                    else:
                        pool.wait_ge(ysum_ready, n - 1)
                        ins = pool.tensor_tensor(rs[:], rs[:], sq[cch % 2][:], ALU.add)
                    ins.then_inc(ysum_ready, 1)

            def add_to_h(adds):
                for cch in range(1, DC, 2):
                    pool.wait_ge(delta_ready, adds * DC + cch + 1)
                    pool.tensor_tensor(h[:, cch, :], h[:, cch, :], wt[1][:], ALU.add).then_inc(h_ready[1], 1)

            def mixer_constants():
                for dst, value in ((mask_row, 0.0), (add_c, 0.0), (keep_c, 1.0), (bd, 0.0), (diag_b, 0.0), (left_b, 0.0),
                                   (pick, 0.0), (row_z, 0.0), (blk, 0.0), (v_aug, 1.0), (eps_m, 1e-6), (k_cmp, 0.0)):
                    step.tick(pool.memset(dst[:], value))
                step.wait(pool)
                step.tick(pool.affine_select(out=mask_row[:, 0:P], in_=mask_row[:, 0:P], compare_op=ALU.is_ge, fill=NEG,
                                             base=0, pattern=[[1, P]], channel_multiplier=-1))
                step.tick(pool.affine_select(out=diag_b[:], in_=diag_b[:], compare_op=ALU.is_ge, fill=NEG, base=0,
                                             pattern=[[-1, P]], channel_multiplier=1))
                step.tick(pool.affine_select(out=left_b[:], in_=left_b[:], compare_op=ALU.is_gt, fill=NEG, base=0,
                                             pattern=[[1, P]], channel_multiplier=-1))
                for dst, fill in ((add_c, NEG), (keep_c, 0.0)):
                    step.tick(pool.affine_select(out=dst[:], in_=dst[:], compare_op=ALU.is_ge, fill=fill, base=-(CB - 1),
                                                 pattern=[[P, TT], [-CB // 2, 32]], channel_multiplier=1))
                step.wait(pool)
                step.tick(pool.memset(add_c[:, :, 31:32], NEG))
                step.tick(pool.memset(keep_c[:, :, 31:32], 0.0))
                for n in range(HG):
                    step.wait(pool)
                    step.tick(pool.memset(bd[32 * n:32 * n + 32, n:n + 1], 1.0))
                step.wait(pool)
                step.tick(pool.affine_select(out=pick[:], in_=pick[:], compare_op=ALU.not_equal, fill=-1.0, base=0,
                                             pattern=[[-1, MH], [0, P]], channel_multiplier=1))
                step.tick(pool.tensor_copy(ident_b[:], ident[:]))
                step.wait(pool)
                pool.sem_inc(mixer_consts, 1)

            def compression_blocks():
                pool.wait_ge(kv_moved, 64)
                for kv in range(2):
                    if kv:
                        pool.wait_ge(blk_hi_ready, kv)
                    for a in range(2):
                        src = kv_2[:, kv, :, 8 * a:8 * a + 8 * NCMP].rearrange("p g (n l) -> p l g n", l=8)
                        pe_at = 48 + 16 * kv + 8 * a
                        pe = bcast(col2[:, pe_at:pe_at + 8].unsqueeze(2).unsqueeze(3), [P, 8, NG, NCMP])
                        step.tick(pool.tensor_tensor(blk[:, 8 * a:8 * a + 8, :, 0:NCMP], src, pe, ALU.add))
                    step.wait(pool)
                    pool.sem_inc(blk_ready, 1)
                    pool.wait_ge(blk_hi_ready, kv + 1)
                    if kv:
                        job_done(pool, ("hid", 0))
                    pool.tensor_tensor(blk_lo[:], blk[:], blk_hi[:].bitcast(F32), ALU.subtract).then_inc(blk_lo_ready, 1)
                    pool.wait_ge(blk_lo_ready, kv + 1)

            for j in range(1, DC):
                pool.wait_ge(shift_c_scaled, j + 1)
                first = ada_w[:, 0, SHIFT_C] if j == 1 else ada_acc0[:, SHIFT_C]
                if j > 1:
                    step.wait(pool)
                ins = pool.tensor_tensor(ada_acc0[:, SHIFT_C], first, ada_w[:, j, SHIFT_C], ALU.add)
                step.tick(ins) if j < DC - 1 else ins.then_inc(shift_c_summed, 1)
            sum_y_squares(0)
            add_to_h(0)
            mixer_constants()
            compression_blocks()
            sum_y_squares(1)
            add_to_h(1)
            sum_y_squares(2)
            add_to_h(2)

        @block.scalar
        def _(act):
            step = Count(act_step)

            def split_high(name, i=0, used=None, size=DC * COLS):
                n, slot = w_number(name, i)
                src = unit_landed(act, name, i)
                if used is not None:
                    act.wait_ge(w_used, used)
                act.activation(w_hi[slot][:, 0:size], src[:, 0:size], ACT.Copy).then_inc(hi_ready, 1)

            def pre_norm_squares(s):
                for cch in range(DC):
                    h_updated(act, s - 1, cch)
                    if cch >= 2:
                        act.wait_ge(sq_used, s * (DC - 1) + cch - 1)
                    act.activation(sq[cch % 2][:], h[:, cch, :], ACT.Square).then_inc(sq_ready, 1)

            def root(job):
                if job[0] == "pre":
                    act.wait_ge(tile_sums_ready, job[1] + 1)
                    act.activation(root_t[:], inv_t[:], ACT.Sqrt, bias=eps_col[:, 0:1]).then_inc(root_ready, 1)
                else:
                    src = job_result(act, job)
                    job_read(act.activation(root_t[:], src[:, 0:TT], ACT.Sqrt, bias=eps_col[:, 0:1]), job)

            def load_table(func):
                step.tick(act.activation(warm[:], eps_col[:], func))

            def shift_c_products(half):
                act.wait_ge(shift_landed[1][half], 16)
                if half == 0:
                    act.wait_ge(silu_c_ready, 1)
                for j in range(half * DC // 2, (half + 1) * DC // 2):
                    act.activation(ada_w[:, j, SHIFT_C], ada_w[:, j, SHIFT_C], ACT.Identity,
                                   scale=silu_c[:, j:j + 1]).then_inc(shift_c_scaled, 1)

            def modulate_high(s):
                shift = s * 3 * DC
                for cch in range(DC):
                    if cch == {0: 4, 2: 6}.get(s):
                        split_high(("up", s // 2))
                    if s == 0 and cch % 4 == 0:
                        taken(act, ("ada0", "a" if cch == 0 else "bc"))
                    if s == 0 and cch == 2:
                        shift_c_products(1)
                    act.wait_ge(w_scaled, s * DC + cch + 1)
                    act.activation(u_hi[:, cch, :], wt[cch % 2][:], ACT.Identity,
                                   bias=ada[:, shift + cch:shift + cch + 1]).then_inc(u_hi_ready, 1)

            def ffn_up(f):
                def iteration(i, up_is_split=False):
                    act.activation(warm[:], eps_col[:], ACT.Silu)
                    if not up_is_split:
                        split_high(("up", f), i)
                    for j in range(2):
                        src = job_result(act, ("g", f, j), i)
                        taken(act, ("u", f, j), i, before=1)
                        job_read(act.activation(sq[j][:], src, ACT.Silu), ("g", f, j))
                    split_high(("gate", f), i)
                    for j in range(2):
                        taken(act, ("u", f, j), i)
                        act.activation(mid_hi[:, bass.ds(2 * i + j, 1), :], wt[j][:].rearrange("p (a t) -> p a t", a=1),
                                       ACT.Copy).then_inc(mid_hi_ready, 1)

                iteration(0, up_is_split=True)
                with act.Fori(1, UP_ITERS) as i:
                    iteration(i)

            def take_y(job, sums, cch, y):
                src = job_result(act, job[0], job[1])
                if cch == 0 and sums != 1:
                    act.wait_ge(mid_ready, (sums // 2 + 1) * FC)
                if cch >= 2:
                    act.wait_ge(ysum_ready, sums * (DC - 2) + cch - 1)
                act.activation(sq[cch % 2][:], src, ACT.Square).then_inc(ysq_ready, 1)
                job_read(act.activation(y[:, cch, :], src, ACT.Copy), job[0])

            def ffn_down(f, sums, y, next_name):
                load_table(ACT.Sqrt)
                for it in range(2):
                    for n in range(6):
                        if (it, n) != (1, 5):
                            nxt = ("d", f, it, n + 1) if n < 5 else ("d", f, 1, 0)
                            kk = (n + 1) % 3
                            used = None if n % 3 == 0 else f * 8 + mixer_used * f + it * 4 + n - n // 3
                            split_high(nxt, 0, used, (DOWN_K[kk + 1] - DOWN_K[kk]) * COLS)
                        elif next_name is not None:
                            split_high(next_name, used=8)
                        if n % 3 == 2:
                            for j in range(2):
                                name = ("y", f, n // 3 * 2 + j)
                                take_y((name, it), sums, (it * 2 + n // 3) * 2 + j, y)

            def split_after(name):
                n = MIX.index(name)
                if n:
                    before = MIX[n - 1]
                    if unit_end[before] is not None:
                        job_done(act, unit_end[before])
                        used = None
                    else:
                        used = 8 + 1 + before[1]
                else:
                    used = None
                size = GATE_ROWS * DC if after(name) == ("gt",) else DC * COLS
                split_high(after(name), 0, used=used, size=size)

            def copy_out(job, dst, scale=None):
                src = job_result(act, job)
                return job_read(act.activation(dst, src, ACT.Copy) if scale is None else
                                act.activation(dst, src, ACT.Copy, scale=scale), job)

            def conv_unit(n):
                if n != 1:
                    split_after(("qk", n))
                for j in range(2):
                    cch = 2 * n + j
                    src = job_result(act, ("qk", cch))
                    act.activation(qkc[:, cch, :], src, ACT.Identity, bias=col2[:, 32 + cch:33 + cch],
                                   scale=col2[:, 24 + cch:25 + cch]).then_inc(conv_first, 1)
                for j in range(2):
                    cch = 2 * n + j
                    taken(act, ("qk", cch))
                    act.activation(qkc[:, cch, :], qkc[:, cch, :], ACT.Silu).then_inc(qk_ready, 1)

            def mixer():
                conv_unit(0)
                split_after(("vsw",))
                split_after(("gt",))
                act.wait_ge(small_landed, 80)
                src = job_result(act, ("gt",))
                act.activation(row_i[:], src[0:MH, :], ACT.Identity, bias=g_bias[:, 0:1])
                act.activation(g_rows, src[64:64 + GATE_N, :], ACT.Copy)
                job_read(act.activation(row_f[:], src[32:32 + MH, :], ACT.Identity, bias=g_bias[:, 1:2]), ("gt",))
                for n in range(2):
                    split_after(("v", n))
                    for b in range(2):
                        src = job_result(act, ("v", n, b))
                        if (n, b) == (0, 0):
                            act.wait_ge(mixer_consts, 1)
                        job_read(act.activation(v_aug[:, 2 * b:2 * b + 2, 2 * n:2 * n + 2, 0:MD],
                                                src.rearrange("p (t h e) -> p t h e", t=2, h=2), ACT.Copy), ("v", n, b))
                split_after(("qk", 1))
                taken(act, ("gt",))
                step.tick(act.activation(row_t[:], row_f[:], ACT.Abs))
                step.wait(act)
                step.tick(act.activation(row_t[:], row_t[:], ACT.Exp, scale=-1.0))
                step.wait(act)
                act.activation(row_t[:], row_t[:], ACT.Ln, bias=1.0).then_inc(soft_ready, 1)
                for n in range(1, 4):
                    conv_unit(n)
                split_after(("kcvc",))
                for j, ab in enumerate("ab"):
                    src = job_result(act, ("kcvc", ab))
                    job_read(act.activation(kv_t[:, j, :, :], src.rearrange("p (n par) -> p par n", par=2), ACT.Copy), ("kcvc", ab))
                taken(act, ("kcvc", "b"))
                for par in range(2):
                    for g in range(NG):
                        act.dma_start(kv_2[par * ND:(par + 1) * ND, :, g, :],
                                      kv_t[g * ND:(g + 1) * ND, :, par, :]).then_inc(kv_moved, 16)
                act.wait_ge(m_ready, 1)
                act.activation(row_t[:], row_t[:], ACT.Exp, scale=-1.0).then_inc(em_ready, 1)

                def o_gate(n):
                    for cch in (2 * n, 2 * n + 1):
                        copy_out(("o", cch), sig_o[:, cch, :])

                def head_exps(hd):
                    for j in range(TT):
                        act.wait_ge(arg_ready, hd * TT + j + 1)
                        act.activation(sq[j % 2][:, 0:T - j * P], sq[j % 2][:, 0:T - j * P], ACT.Exp,
                                       bias=cols[:, 0, j, hd:hd + 1]).then_inc(e_ready, 1)

                def head_squares(hd):
                    act.wait_ge(hm_ready, hd + 1)
                    step.wait(act)
                    for t in range(TT):
                        step.tick(act.activation(wt[0][:, t * P:(t + 1) * P], hm[:, hd, t * P:(t + 1) * P], ACT.Square,
                                                 accum_out=ssm[:, hd, t:t + 1]))

                def take_queries(n):
                    for j, ab in enumerate("ab"):
                        copy_out(("qn", n, ab), qn[:, 2 * n + j, :], scale=ND ** -0.5)

                def blocks_high(kv):
                    act.wait_ge(blk_ready, kv + 1)
                    if kv:
                        job_done(act, ("hid", 0))
                    act.activation(blk_hi[:], blk[:], ACT.Copy).then_inc(blk_hi_ready, 1)

                def hidden_out(kv):
                    src = job_result(act, ("hid", kv))
                    job_read(act.activation(hid_t[:, kv, :], src[0:64, 0:COLS], ACT.Copy), ("hid", kv))

                def hidden_silu(kv):
                    src = job_result(act, ("hidT", kv))
                    for half in range(2):
                        b1 = 44 + 2 * kv + half
                        ins = act.activation(hid[:, kv, half, :], src[:, half * 64:(half + 1) * 64], ACT.Silu,
                                             bias=col2[:, b1:b1 + 1])
                    job_read(ins, ("hidT", kv))

                split_after(("o", 0))
                o_gate(0)
                split_after(("o", 1))
                head_exps(0)
                blocks_high(0)
                o_gate(1)
                split_after(("kk",))
                head_exps(1)
                for j, ab in enumerate("ab"):
                    copy_out(("kk", ab), ksw[:, j, :])
                head_squares(0)
                split_after(("qn", 0))
                head_exps(2)
                take_queries(0)
                split_after(("c1", 0, 0))
                head_squares(1)
                head_exps(3)
                split_after(("c1", 0, 1))
                hidden_out(0)
                head_squares(2)
                hidden_silu(0)
                split_after(("qn", 1))
                head_squares(3)
                step.wait(act)
                act.activation(ssm[:], ssm[:], ACT.Sqrt, bias=eps_m[:, 0:1], scale=1.0 / MD).then_inc(ssm_root, 1)
                blocks_high(1)
                for cch in range(MH):
                    taken(act, ("o", cch))
                taken(act, ("gT",))
                act.activation(sig_o[:], sig_o[:], ACT.Sigmoid).then_inc(sig_o_ready, 1)
                act.activation(sig_n[:], g_tok[:].rearrange("p t (h b) -> p t h b", b=3), ACT.Sigmoid).then_inc(sig_n_ready, 1)
                take_queries(1)
                split_after(("c1", 1, 0))
                src = job_result(act, ("kcmp",))
                for g in range(NG):
                    rows = slice(g * ND, (g + 1) * ND)
                    ins = act.activation(k_cmp[rows, g, :], src[rows, 0:32], ACT.Identity, bias=col2[rows, 80:81])
                job_read(ins, ("kcmp",))
                split_after(("c1", 1, 1))
                hidden_out(1)
                hidden_silu(1)

                def take_gate(cch):
                    copy_out(gate_job(cch), (sig_a if cch < DC else sig_b)[:, cch % DC, :])

                for t in range(TT):
                    act.wait_ge(arg_c_ready, t + 1)
                    act.activation(p_cmp[t % 2], p_cmp[t % 2], ACT.Exp).then_inc(e_c_ready, 1)
                    if t % 2 == 0:
                        split_after(GATES[t // 2])
                    if t == 0:
                        for hd in range(MH):
                            taken(act, ("hT", hd))
                    take_gate(t)
                    src = job_result(act, ("pcT", t))
                    if t:
                        job_done(act, ("oc", t - 1))
                    job_read(act.activation(pt_c[:].rearrange("p g t -> p (g t)"), src[:, 0:NG * P], ACT.Copy), ("pcT", t))
                for s, (t, g, hh) in enumerate(STEPS):
                    cch = chunk_at.get(s)
                    if cch is not None and cch % 2 == 0:
                        split_after(GATES[cch // 2])
                    for br, (name, p) in enumerate((("ss", p_s), ("sw", p_w))):
                        n = P * len(blocks_of(t)[br])
                        act.wait_ge(n_max_ready, s + 1)
                        src = job_result(act, (name, s))
                        if s >= 2:
                            job_done(act, ("ts" if br == 0 else "tw", s - 2))
                        job_read(act.activation(p[s % 2][:, 0:n], src[:, 0:n], ACT.Exp, bias=n_max[:, s, br:br + 1],
                                                accum_out=sums[:, s, br:br + 1]), (name, s))
                    if cch is not None:
                        take_gate(cch)
                    n = P * len(blocks_of(t)[1])
                    src = job_result(act, ("tw", s))
                    job_read(act.activation(pt_w[s % 2][:, 0:n], src[:, 0:n], ACT.Copy), ("tw", s))
                split_after(GATES[-1])
                take_gate(2 * DC - 2)
                for fc in range(4):
                    src = job_result(act, ("oT", fc))
                    act.activation(o_hi[:, fc, :], src, ACT.Copy).then_inc(o_hi_ready, 1)
                act.activation(hm_hi[:], hm[:], ACT.Copy).then_inc(o_hi_ready, 1)
                taken(act, gate_job(DC - 1))
                act.activation(sig_a[:], sig_a[:], ACT.Sigmoid).then_inc(gates_ready, 1)
                take_gate(2 * DC - 1)
                split_after(("um", 0))
                taken(act, gate_job(2 * DC - 1))
                act.activation(sig_b[:], sig_b[:], ACT.Sigmoid).then_inc(gates_ready, 1)
                load_table(ACT.Sqrt)
                for j in range(2):
                    if j:
                        split_after(("um", j))
                    split_after(("un", j))
                    for n in range(4):
                        act.wait_ge(merged, 4 * j + n + 1)
                        act.activation(u_hi[:, 4 * j + n, :], wt[n % 2][:], ACT.Copy).then_inc(u_hi_ready, 1)
                for n in range(4):
                    split_after(("wo", n))
                    for j in range(2):
                        take_y((("y1", 2 * n + j), 0), 1, 2 * n + j, y_mix)

            act.wait_ge(c_landed, 16)
            act.activation(silu_c[:], c_col[:], ACT.Silu).then_inc(silu_c_ready, 1)
            act.wait_ge(consts_ready, 1)
            load_table(ACT.Sqrt)
            for cch in range(DC):
                job_read(act.activation(h[:, cch, :], job_result(act, ("x", cch)), ACT.Copy), ("x", cch))
            for cch in range(DC):
                taken(act, ("x", cch))
                if cch >= 2:
                    act.wait_ge(sq_used, cch - 1)
                act.activation(sq[cch % 2][:], h[:, cch, :], ACT.Square).then_inc(sq_ready, 1)
            root(("pre", 0))
            split_high(("g0", 0))
            shift_c_products(0)
            modulate_high(0)
            ffn_up(0)
            ffn_down(0, 0, y_ffn, ("qk", 0))
            root(("post", 0))
            pre_norm_squares(1)
            root(("pre", 1))
            modulate_high(1)
            mixer()
            root(("post", 1))
            pre_norm_squares(2)
            root(("pre", 2))
            modulate_high(2)
            ffn_up(1)
            ffn_down(1, 2, y_ffn, None)
            root(("post", 2))
            for cch in range(DC):
                src = job_result(act, ("out", cch))
                job_read(act.activation(out_tok[:, :, cch * P:(cch + 1) * P], src.rearrange("p (t n) -> p t n", t=TT),
                                        ACT.Copy), ("out", cch))

        @block.vector
        def _(dve):
            step = Count(dve_step)

            def split_low(name, i=0, size=DC * COLS):
                n, slot = w_number(name, i)
                dve.wait_ge(hi_ready, n)
                dve.tensor_tensor(w_lo[slot][:, 0:size], raw[plan.raws[name][0]][:, 0:size],
                                  w_hi[slot][:, 0:size].bitcast(F32), ALU.subtract).then_inc(lo_ready, 1)

            def sum_ada(name, i, number, half=0):
                acc = ada_acc[:, half, :]
                src = unit_landed(dve, name, i)
                for j in range(DC):
                    part = src[:, j * COLS:(j + 1) * COLS]
                    if j:
                        dve.wait_ge(dve_step, (DC - 1) * number + j)
                        ins = dve.scalar_tensor_tensor(acc, part, silu_c[:, j:j + 1], acc, ALU.mult, ALU.add)
                    else:
                        ins = dve.tensor_scalar(acc, part, silu_c[:, 0:1], None, ALU.mult)
                    ins.then_inc(dve_step if j < DC - 1 else ada_summed, 1)

            def take_ada(name, i, number, units=1):
                src = job_result(dve, name, i)
                at_ = bass.ds(2 * (number + ADA_FIRST), 2 * units)
                job_read(dve.tensor_tensor(ada[:, at_], src[:, 0:2 * units], col1[:, at_], ALU.add), name)

            def inverse_rms(job):
                if job[0] == "pre":
                    src = job_result(dve, job)
                    job_read(dve.tensor_tensor(rs[:].rearrange("p (t n) -> p t n", t=TT), src.rearrange("p (t n) -> p t n", t=TT),
                                               bcast(ident[:].unsqueeze(1), [P, TT, P]), ALU.mult), job)
                    taken(dve, job)
                    dve.tensor_reduce(inv_t[:], rs[:].rearrange("p (t n) -> p t n", t=TT), AX.X, ALU.add).then_inc(tile_sums_ready, 1)
                    dve.wait_ge(root_ready, job[1] + 1)
                else:
                    taken(dve, job)
                dve.reciprocal(inv_t[:], root_t[:]).then_inc(inv_ready, 1)

            misc = Count(dve_misc)

            def gains(s):
                shift, scale, gate = (ada[:, (3 * s + j) * DC:(3 * s + j + 1) * DC] for j in range(3))
                pre = col1[:, 72 + 2 * s * DC:72 + (2 * s + 1) * DC]
                misc.tick(dve.scalar_tensor_tensor(gain_a[:], scale, 1.0, pre, ALU.add, ALU.mult))
                misc.wait(dve)
                misc.tick(dve.tensor_scalar(gain_a[:], gain_a[:], ROOT_D, None, ALU.mult))
                misc.wait(dve)

            def gains_post(s, weight):
                gate = ada[:, (3 * s + 2) * DC:(3 * s + 3) * DC]
                post = col1[:, 72 + (2 * s + 1) * DC:72 + (2 * s + 2) * DC]
                misc.tick(dve.scalar_tensor_tensor(gain_g[:], gate, weight * ROOT_D, post, ALU.mult, ALU.mult))
                misc.wait(dve)

            def modulate(s, before_low=()):
                shift = s * 3 * DC
                r = job_result(dve, ("r", "pre", s))

                base = (0, DC, 3 * DC)[s]

                def low(cch):
                    if cch in before_low:
                        before_low[cch]()
                    dve.wait_ge(u_hi_ready, base + cch + 1)
                    dve.scalar_tensor_tensor(u_lo[:, cch, :], wt[cch % 2][:], ada[:, shift + cch:shift + cch + 1],
                                             u_hi[:, cch, :].bitcast(F32), ALU.add, ALU.subtract).then_inc(u_ready, 1)
                for cch in range(DC):
                    if cch >= 2:
                        low(cch - 2)
                        dve.wait_ge(u_ready, base + cch - 1)
                    dve.scalar_tensor_tensor(wt[cch % 2][:], h[:, cch, :], gain_a[:, cch:cch + 1], r,
                                             ALU.mult, ALU.mult).then_inc(w_scaled, 1)
                low(DC - 2)
                low(DC - 1)
                dve.wait_ge(w_scaled, (s + 1) * DC)
                dve.sem_inc(bank_free[plan.jobs[("r", "pre", s)][0]], 1)

            def ffn_up(f):
                def iteration(i, up_is_split=False):
                    if not up_is_split:
                        split_low(("up", f), i)
                    if f == 0:
                        sum_ada(("ada", "a"), i, 2 * i, 0)
                    split_low(("gate", f), i)
                    if f == 0:
                        sum_ada(("ada", "b"), i, 2 * i + 1, 1)
                    for j in range(2):
                        taken(dve, ("g", f, j), i)
                        src = job_result(dve, ("u", f, j), i)
                        job_read(dve.tensor_tensor(wt[j][:], src, sq[j][:], ALU.mult), ("u", f, j))
                    if f == 0:
                        take_ada(("ada", "ab"), i, 2 * i, 2)
                    for j in range(2):
                        dve.wait_ge(mid_hi_ready, (i + f * UP_ITERS) * 2 + j + 1)
                        at_ = bass.ds(2 * i + j, 1)
                        dve.tensor_tensor(mid_lo[:, at_, :], wt[j][:].rearrange("p (a t) -> p a t", a=1),
                                          mid_hi[:, at_, :].bitcast(F32), ALU.subtract).then_inc(mid_ready, 1)

                iteration(0, up_is_split=True)
                with dve.Fori(1, UP_ITERS) as i:
                    iteration(i)

            def ffn_down(f, next_name):
                for it in range(2):
                    for n in range(6):
                        if n == 3:
                            take_ada(("ada", f, 2), it, ada_number(f, it, 2))
                        if (it, n) != (1, 5):
                            nxt = ("d", f, it, n + 1) if n < 5 else ("d", f, 1, 0)
                            kk = (n + 1) % 3
                            split_low(nxt, 0, (DOWN_K[kk + 1] - DOWN_K[kk]) * COLS)
                        elif next_name is not None:
                            split_low(next_name, 0)
                        if has_ada(f, n + 1):
                            sum_ada(("ada", f, it, n + 1), 0, ada_number(f, it, n + 1))
                    if f == 0:
                        take_ada(("ada", f, 5), it, ada_number(f, it, 5))

            def update_h(post, y):
                r = job_result(dve, ("r", "post", post))
                taken(dve, *y_job(post, DC - 1))
                for cch in range(DC):
                    if cch >= 2:
                        h_updated(dve, post, cch - 2)
                    dve.scalar_tensor_tensor(wt[cch % 2][:], y[:, cch, :], gain_g[:, cch:cch + 1], r,
                                             ALU.mult, ALU.mult).then_inc(delta_ready, 1)
                    if cch % 2:
                        dve.wait_ge(delta_ready, post * DC + cch)
                        dve.tensor_tensor(h[:, cch - 1, :], h[:, cch - 1, :], wt[0][:], ALU.add).then_inc(h_ready[0], 1)
                dve.wait_ge(delta_ready, (post + 1) * DC)
                dve.sem_inc(bank_free[plan.jobs[("r", "post", post)][0]], 1)

            def mixer_low(name):
                nxt = after(name)
                size = GATE_ROWS * DC if nxt == ("gt",) else DC * COLS
                split_low(nxt, 0, size=size)

            def conv_taps(n, with_low=True):
                if with_low:
                    mixer_low(("qk", n))
                for tap in (2, 1, 0):
                    for j in range(2):
                        cch = 2 * n + j
                        dve.wait_ge(conv_first, cch + 1)
                        if tap < 2:
                            misc.wait(dve, misc.n - 1 if tap == 1 or j == 0 else misc.n)
                        src = PS[:, plan.jobs[("qk", cch)][0], :]
                        lag = 3 - tap
                        w = 8 * tap + cch
                        ins = dve.scalar_tensor_tensor(qkc[:, cch, lag:T], src[:, 0:T - lag], col2[:, w:w + 1],
                                                       qkc[:, cch, lag:T], ALU.mult, ALU.add)
                        if tap:
                            misc.tick(ins)
                        else:
                            job_read(ins, ("qk", cch))

            def mixer():
                conv_taps(0)
                mixer_low(("vsw",))
                for b in range(2):
                    src = job_result(dve, ("vsw", b)).rearrange("p (t a n) -> p t a n", t=2, a=2)
                    dve.wait_ge(mixer_consts, 1)
                    job_read(dve.tensor_copy(vsw[:, 2 * b:2 * b + 2, :, :], src), ("vsw", b))
                mixer_low(("gt",))
                mixer_low(("v", 0))
                src = job_result(dve, ("gT",))
                job_read(dve.tensor_copy(g_tok[:], src[:, 0:TT * GATE_N].rearrange("p (t n) -> p t n", t=TT)), ("gT",))
                mixer_low(("v", 1))
                mixer_low(("qk", 1))
                dve.wait_ge(soft_ready, 1)
                misc.tick(dve.scalar_tensor_tensor(row_f[:], row_f[:], 0.0, row_t[:], ALU.min, ALU.subtract))
                misc.wait(dve)
                misc.tick(dve.tensor_tensor_scan(row_s[:], row_f[:], row_z[:], 0.0, ALU.add, ALU.add))
                misc.wait(dve)
                misc.tick(dve.tensor_tensor(row_i[:], row_i[:], row_s[:], ALU.subtract))
                misc.wait(dve)
                misc.tick(dve.tensor_tensor_scan(row_m[:], row_i[:], row_i[:], 0.0, ALU.max, ALU.max))
                misc.wait(dve)
                dve.tensor_tensor(row_t[:], row_s[:], row_m[:], ALU.add).then_inc(m_ready, 1)
                for n in range(1, 4):
                    conv_taps(n, n > 1)
                def head_weights(hd):
                    neg = job_result(dve, ("negM", hd))
                    for j in range(TT + 1):
                        if j < TT:
                            n = T - j * P
                            if j >= 2:
                                taken(dve, ("S", hd, j - 2))
                            elif hd:
                                taken(dve, ("S", hd - 1, j + 2))
                            ins = dve.tensor_tensor(sq[j % 2][:, 0:n], neg[:, j * P:T], mask_row[:, 0:n], ALU.add)
                            ins.then_inc(arg_ready, 1)
                        if j:
                            i, n = j - 1, T - (j - 1) * P
                            src = job_result(dve, ("S", hd, i))
                            dve.wait_ge(e_ready, hd * TT + j)
                            job_read(dve.scalar_tensor_tensor(p_m[:, i, 0:n], src[:, 0:n], MD ** -0.5, sq[i % 2][:, 0:n],
                                                              ALU.mult, ALU.mult), ("S", hd, i))
                    dve.wait_ge(arg_ready, hd * TT + TT)
                    dve.sem_inc(bank_free[plan.jobs[("negM", hd)][0]], 1)

                def head_output(hd):
                    for b in range(2):
                        num = job_result(dve, ("num", hd, b))[:, 0:2 * (MD + 1)].rearrange("p (t e) -> p t e", t=2)
                        misc.tick(dve.tensor_copy(den[:, hd, 2 * b:2 * b + 2], num[:, :, MD]))
                    misc.wait(dve)
                    misc.tick(dve.scalar_tensor_tensor(max_c[:, 0:TT], den[:, hd, :], -1.0, cols[:, 1, :, hd], ALU.mult, ALU.max))
                    misc.wait(dve)
                    misc.tick(dve.tensor_tensor(den[:, hd, :], den[:, hd, :], max_c[:, 0:TT], ALU.max))
                    misc.wait(dve)
                    misc.tick(dve.reciprocal(den[:, hd, :], den[:, hd, :]))
                    misc.wait(dve)
                    h3 = hm[:, hd, :].rearrange("p (t e) -> p t e", t=TT)
                    for b in range(2):
                        num = job_result(dve, ("num", hd, b))[:, 0:2 * (MD + 1)].rearrange("p (t e) -> p t e", t=2)
                        job_read(dve.tensor_tensor(h3[:, 2 * b:2 * b + 2, :], num[:, :, 0:MD],
                                                   bcast(den[:, hd, 2 * b:2 * b + 2].unsqueeze(2), [P, 2, MD]), ALU.mult), ("num", hd, b))
                        taken(dve, ("num", hd, b))
                    dve.sem_inc(hm_ready, 1)

                mixer_low(("kcvc",))
                mixer_low(("o", 0))
                src = job_result(dve, ("colT",))
                job_read(dve.tensor_copy(cols[:].rearrange("p a t h -> p (a t h)"), src[:, 0:2 * TT * MH]), ("colT",))
                mixer_low(("o", 1))
                head_weights(0)
                head_weights(1)
                head_output(0)
                mixer_low(("kk",))
                head_weights(2)
                head_output(1)
                mixer_low(("qn", 0))
                mixer_low(("c1", 0, 0))
                head_weights(3)
                head_output(2)
                mixer_low(("c1", 0, 1))
                head_output(3)
                mixer_low(("qn", 1))
                dve.wait_ge(ssm_root, 1)
                misc.tick(dve.reciprocal(ssm[:], ssm[:]))
                misc.wait(dve)
                for hd in range(MH):
                    h3 = hm[:, hd, :].rearrange("p (t e) -> p t e", t=TT)
                    dve.tensor_tensor(h3, h3, bcast(ssm[:, hd, :].unsqueeze(2), [P, TT, MD]), ALU.mult).then_inc(hm_normed, 1)
                mixer_low(("c1", 1, 0))
                dve.wait_ge(sig_o_ready, 1)
                for hd in range(MH):
                    src = job_result(dve, ("hT", hd))
                    job_read(dve.scalar_tensor_tensor(hm[:, hd, :], src, col2[:, 40 + hd:41 + hd], sig_o[:, hd, :],
                                                      ALU.mult, ALU.mult), ("hT", hd))
                mixer_low(("c1", 1, 1))

                def hidden_copies():
                    taken(dve, ("hidT", 1))
                    for g in range(NG):
                        src = hid[:, 1, :, g * 32:(g + 1) * 32].unsqueeze(2)
                        misc.tick(dve.tensor_copy(hid_rep[:, :, g, :, :], bcast(src, [P, 2, HG, 32])))
                    misc.wait(dve)
                    dve.sem_inc(hid_rep_ready, 1)

                def compressed_values():
                    src = job_result(dve, ("vcmp",))[:, 0:NG * ND].rearrange("p (g e) -> p g e", g=NG)
                    job_read(dve.tensor_tensor(v_tmp[:], src, bcast(b2_row[:].unsqueeze(1), [P, NG, ND]), ALU.add), ("vcmp",))
                    taken(dve, ("vcmp",))
                    for n in range(HG):
                        misc.tick(dve.tensor_scalar(v_bd[:, :, n, :], v_tmp[:], bd[:, n:n + 1], None, ALU.mult))
                    misc.wait(dve)
                    dve.sem_inc(v_bd_ready, 1)

                def take_oc(t):
                    src = job_result(dve, ("oc", t))
                    job_read(dve.tensor_copy(o_acc[:, t, :], src), ("oc", t))

                for t in range(TT):
                    if t == 0:
                        hidden_copies()
                    src = job_result(dve, ("sc", t))[:, 0:NH * 32].rearrange("p (h g n) -> p g h n", g=NG, n=32)
                    p_t = p_cmp[t % 2]
                    if t >= 2:
                        job_done(dve, ("pcT", t - 2))
                    job_read(dve.tensor_tensor(p_t.rearrange("p (g h) n -> p g h n", g=NG), src,
                                               bcast(add_c[:, t:t + 1, :].unsqueeze(1), [P, NG, HG, 32]), ALU.add), ("sc", t))
                    taken(dve, ("sc", t))
                    misc.tick(dve.tensor_reduce(max_c[:], p_t, AX.X, ALU.max))
                    misc.wait(dve)
                    dve.tensor_tensor(p_t, p_t, bcast(max_c[:].unsqueeze(2), [P, NH, 32]), ALU.subtract).then_inc(arg_c_ready, 1)
                    dve.wait_ge(e_c_ready, t + 1)
                    misc.tick(dve.tensor_tensor(p_t, p_t, bcast(keep_c[:, t:t + 1, :], [P, NH, 32]), ALU.mult))
                    misc.wait(dve)
                    misc.tick(dve.tensor_reduce(sum_c[:], p_t, AX.X, ALU.add))
                    misc.wait(dve)
                    misc.tick(dve.tensor_scalar(sum_c[:], sum_c[:], 1e-30, None, ALU.max))
                    misc.wait(dve)
                    misc.tick(dve.reciprocal(sum_c[:], sum_c[:]))
                    misc.wait(dve)
                    if t == 0:
                        dve.wait_ge(sig_n_ready, 1)
                    misc.tick(dve.tensor_tensor(sum_c[:], sum_c[:], sig_n[:, t, :, 0], ALU.mult))
                    misc.wait(dve)
                    dve.tensor_tensor(p_t, p_t, bcast(sum_c[:].unsqueeze(2), [P, NH, 32]), ALU.mult).then_inc(p_c_ready, 1)
                    if t == 0:
                        compressed_values()
                    if t % 2 == 0:
                        mixer_low(GATES[t // 2])
                    if t:
                        take_oc(t - 1)
                take_oc(TT - 1)

                def scores_max(s):
                    t = STEPS[s][0]
                    for br, name in enumerate(("ss", "sw")):
                        n = P * len(blocks_of(t)[br])
                        src = job_result(dve, (name, s))
                        ins = dve.tensor_reduce(n_max[:, s, br:br + 1], src[:, 0:n], AX.X, ALU.max, negate=True)
                    ins.then_inc(n_max_ready, 1)

                scores_max(0)
                for s, (t, g, hh) in enumerate(STEPS):
                    if chunk_at.get(s, 1) % 2 == 0:
                        mixer_low(GATES[chunk_at[s] // 2])
                    if s + 1 < len(STEPS):
                        scores_max(s + 1)
                    n = P * len(blocks_of(t)[0])
                    src = job_result(dve, ("ts", s))
                    job_read(dve.tensor_copy(pt_s[s % 2][:, 0:n], src[:, 0:n]), ("ts", s))
                    if hh == 0 and s:
                        group_output(s - HG)
                group_output(len(STEPS) - HG)
                dve.sem_inc(o_acc_ready, 1)
                mixer_low(GATES[-1])
                for fc in range(4):
                    src = job_result(dve, ("oT", fc))
                    dve.wait_ge(o_hi_ready, fc + 1)
                    job_read(dve.tensor_tensor(o_lo[:, fc, :], src, o_hi[:, fc, :].bitcast(F32), ALU.subtract), ("oT", fc))
                dve.wait_ge(o_hi_ready, 5)
                dve.tensor_tensor(hm_lo[:], hm[:], hm_hi[:].bitcast(F32), ALU.subtract).then_inc(hm_lo_ready, 1)
                for j in range(2):
                    mixer_low(("um", j))
                    for n in range(4):
                        cch = 4 * j + n
                        src = job_result(dve, ("ym", cch))
                        if cch == 0:
                            dve.wait_ge(gates_ready, 1)
                        job_read(dve.tensor_tensor(sig_a[:, cch, :], sig_a[:, cch, :], src, ALU.mult), ("ym", cch))
                    mixer_low(("un", j))
                    for n in range(4):
                        cch = 4 * j + n
                        src = job_result(dve, ("yn", cch))
                        if cch == 0:
                            dve.wait_ge(gates_ready, 2)
                        if cch >= 2:
                            dve.wait_ge(u_ready, DC + DC + cch - 1)
                        job_read(dve.tensor_tensor(wt[n % 2][:], sig_b[:, cch, :], src, ALU.mult), ("yn", cch))
                        taken(dve, ("yn", cch))
                        dve.tensor_tensor(wt[n % 2][:], wt[n % 2][:], sig_a[:, cch, :], ALU.add).then_inc(merged, 1)
                        dve.wait_ge(u_hi_ready, 2 * DC + cch + 1)
                        dve.tensor_tensor(u_lo[:, cch, :], wt[n % 2][:], u_hi[:, cch, :].bitcast(F32), ALU.subtract).then_inc(u_ready, 1)
                for n in range(4):
                    mixer_low(("wo", n))

            def group_output(s0):
                t, g, _ = STEPS[s0]
                for s in range(s0, s0 + HG):
                    taken(dve, ("ss", s))
                    taken(dve, ("sw", s))
                misc.tick(dve.reciprocal(w_sw[:], sums[:, s0:s0 + HG, :]))
                misc.wait(dve)
                misc.tick(dve.tensor_tensor(w_sw[:], w_sw[:], sig_n[:, t, g * HG:(g + 1) * HG, 1:3], ALU.mult))
                misc.wait(dve)
                src = job_result(dve, ("o_nsa", t, g)).rearrange("p (h b e) -> p h b e", h=HG, b=2)
                ins = dve.tensor_tensor(o_tmp[:], src, bcast(w_sw[:].unsqueeze(3), [P, HG, 2, ND]), ALU.mult)
                job_read(ins, ("o_nsa", t, g))
                taken(dve, ("o_nsa", t, g))
                acc = o_acc[:, t, g * HG * ND:(g + 1) * HG * ND].rearrange("p (h e) -> p h e", h=HG)
                if g == 0:
                    taken(dve, ("oc", t))
                for br in range(2):
                    misc.tick(dve.tensor_tensor(acc, acc, o_tmp[:, :, br, :], ALU.add))
                    misc.wait(dve)

            src = job_result(dve, ("cols", 1))
            job_read(dve.tensor_copy(col1[:], src[:, 0:120]), ("cols", 1))
            src = job_result(dve, ("cols", 2))
            job_read(dve.tensor_copy(col2[:], src[:, 0:81]), ("cols", 2))
            dve.wait_ge(silu_c_ready, 1)

            def first_sum(cols, landed, done):
                for j in range(DC):
                    dve.wait_ge(landed(j), 16)
                    if j:
                        misc.wait(dve)
                        ins = dve.scalar_tensor_tensor(ada_acc0[:, cols], ada_w[:, j, cols], silu_c[:, j:j + 1],
                                                       ada_acc0[:, cols], ALU.mult, ALU.add)
                    else:
                        ins = dve.tensor_scalar(ada_acc0[:, cols], ada_w[:, 0, cols], silu_c[:, 0:1], None, ALU.mult)
                    misc.tick(ins) if j < DC - 1 else ins.then_inc(done, 1)

            first_sum(SCALE, lambda j: scale_landed[j], first_summed)
            inverse_rms(("pre", 0))
            first_sum(SHIFT_A, lambda j: shift_landed[0][j * 2 // DC], first_summed)

            def take_first(part, cols):
                cols = slice(cols.start // P, cols.stop // P)
                src = job_result(dve, ("ada0", part))
                ins = dve.tensor_tensor(ada[:, cols], src[:, 0:cols.stop - cols.start], col1[:, cols], ALU.add)
                job_read(ins, ("ada0", part))

            def shift_a_and_weights():
                take_first("a", SHIFT_A)
                split_low(("g0", 0))

            def shift_bc():
                first_sum(SHIFT_B, lambda j: shift_landed[1][j * 2 // DC], ada_summed)
                split_low(("up", 0))
                take_first("bc", slice(SHIFT_B.start, SHIFT_C.stop))
                taken(dve, ("ada0", "bc"))

            taken(dve, ("cols", 1))
            take_first("scale", SCALE)
            taken(dve, ("ada0", "scale"))
            gains(0)
            modulate(0, {0: shift_a_and_weights, 4: shift_bc})
            ffn_up(0)
            ffn_down(0, ("qk", 0))
            taken(dve, ("ada", 0, 5), 1)
            gains_post(0, 0.5)
            gains(1)
            inverse_rms(("post", 0))
            update_h(0, y_ffn)
            inverse_rms(("pre", 1))
            modulate(1)
            mixer()
            gains_post(1, 1.0)
            gains(2)
            inverse_rms(("post", 1))
            update_h(1, y_mix)
            inverse_rms(("pre", 2))
            modulate(2, {6: lambda: split_low(("up", 1))})
            ffn_up(1)
            ffn_down(1, None)
            taken(dve, ("ada", 1, 2), 1)
            gains_post(2, 0.5)
            inverse_rms(("post", 2))
            update_h(2, y_ffn)

        @block.tensor
        def _(pe):
            def three_passes(ps, pairs):
                total = len(pairs)
                for n, (wh, wl, ah, al) in enumerate(pairs):
                    pe.matmul(ps, wh, ah, start=(n == 0), stop=False)
                    pe.matmul(ps, wh, al, start=False, stop=False)
                    ins = pe.matmul(ps, wl, ah, start=False, stop=(n == total - 1))
                return ins

            def unit_ready(name, i=0):
                n, slot = w_number(name, i)
                pe.wait_ge(lo_ready, n)
                return w_hi[slot], w_lo[slot]

            def k_pairs(unit, j, kn, ahi, alo, k0=0, first=True, width=COLS):
                wh, wl = unit
                return [(wh[:, k * width + j * P:k * width + (j + 1) * P], wl[:, k * width + j * P:k * width + (j + 1) * P],
                         ahi[:, k0 + k, :], alo[:, k0 + k, :]) for k in range(kn)]

            def token_sums(ps, squares, first, last):
                for t in range(TT):
                    ins = pe.matmul(ps[:, t:t + 1], chunk(squares, t), ones[:, 0:1], start=first and t == 0,
                                    stop=last and t == TT - 1)
                return ins

            def spread_inverse(kind, s):
                ps = job_start(pe, ("r", kind, s))
                pe.wait_ge(inv_ready, 2 * s + (kind == "post") + 1)
                for t in range(TT):
                    ins = pe.matmul(chunk(ps, t), bcast(inv_t[:, t:t + 1], [P, P]), ident[:], start=True, stop=True)
                job_end(ins, ("r", kind, s))

            def pre_norm(s):
                ps = job_start(pe, ("pre", s))
                for cch in range(DC):
                    pe.wait_ge(sq_ready, s * DC + cch + 1)
                    ins = pe.matmul(ps, ones[:], sq[cch % 2][:], start=(cch == 0), stop=(cch == DC - 1))
                    if cch < DC - 1:
                        ins.then_inc(sq_used, 1)
                job_end(ins, ("pre", s))

            def post_norm(s):
                ps = job_start(pe, ("post", s))
                pe.wait_ge(ysum_ready, (s + 1) * (DC - 2))
                token_sums(ps, rs, True, False)
                for cch in (DC - 2, DC - 1):
                    pe.wait_ge(ysq_ready, s * DC + cch + 1)
                    ins = token_sums(ps, sq[cch % 2], False, cch == DC - 1)
                job_end(ins, ("post", s))
                spread_inverse("post", s)

            def ada_columns(name, i, number, units=1):
                ps = job_start(pe, name, i)
                pe.wait_ge(ada_summed, number + 1 + units)
                for u in range(units):
                    for j in range(2):
                        ins = pe.matmul(ps[:, 2 * u + j:2 * u + j + 1], ada_acc[:, u, j * P:(j + 1) * P], ones[:, 0:1],
                                        start=True, stop=True)
                job_end(ins, name)

            def chunks_as_they_come(unit, jobs, i, u_base, at_half=None):
                wh, wl = unit
                ps = [job_start(pe, job, i) for job in jobs]
                for k in range(DC):
                    if k == DC // 2 and at_half is not None:
                        at_half()
                    pe.wait_ge(u_ready, u_base + k + 1)
                    for j, job in enumerate(jobs):
                        at_ = slice(k * COLS + j * P, k * COLS + (j + 1) * P)
                        pe.matmul(ps[j], wh[:, at_], u_hi[:, k, :], start=(k == 0), stop=False)
                        pe.matmul(ps[j], wh[:, at_], u_lo[:, k, :], start=False, stop=False)
                        ins = pe.matmul(ps[j], wl[:, at_], u_hi[:, k, :], start=False, stop=(k == DC - 1))
                        if k == DC - 1:
                            job_end(ins, job)

            def ffn_up(f, at_half=None):
                u_base = 3 * f * DC
                n0, slot = w_number(("g0", f))

                def iteration(i, at_half):
                    pe.wait_ge(lo_ready, n0 + 2 * i)
                    chunks_as_they_come((w_hi[slot], w_lo[slot]), [("g", f, 0), ("g", f, 1)], i, u_base, at_half)
                    unit = unit_ready(("up", f), i)
                    for j in range(2):
                        ps = job_start(pe, ("u", f, j), i)
                        ins = three_passes(ps, k_pairs(unit, j, DC, u_hi, u_lo))
                        job_end(ins, ("u", f, j))
                    if f == 0:
                        ada_columns(("ada", "ab"), i, 2 * i, 2)

                if at_half is not None:
                    iteration(0, at_half)
                with pe.Fori(0 if at_half is None else 1, UP_ITERS) as i:
                    iteration(i, None)

            def ffn_down(f):
                pe.wait_ge(mid_ready, (f + 1) * FC - 2)
                base_n, _ = w_number(("gate", f))
                base_n += 2 * (UP_ITERS - 1)
                with pe.Fori(0, 2) as i:
                    for n in range(6):
                        pe.wait_ge(lo_ready, base_n + 6 * i + n)
                        if n == 2:
                            pe.wait_ge(mid_ready, (f + 1) * FC)
                        slot = (base_n + n - 1) % 2
                        k0, k1 = DOWN_K[n % 3], DOWN_K[n % 3 + 1]
                        for j in range(2):
                            name = ("y", f, n // 3 * 2 + j)
                            if n % 3 == 0:
                                ps = job_start(pe, name, i)
                            else:
                                ps = PS[:, plan.jobs[name][0], :]
                            for k in range(k1 - k0):
                                wh, wl = (w[slot][:, k * COLS + j * P:k * COLS + (j + 1) * P] for w in (w_hi, w_lo))
                                f_at = k0 + k
                                pe.matmul(ps, wh, mid_hi[:, f_at, :], start=(f_at == 0), stop=False)
                                pe.matmul(ps, wh, mid_lo[:, f_at, :], start=False, stop=False)
                                ins = pe.matmul(ps, wl, mid_hi[:, f_at, :], start=False, stop=(f_at == FC - 1))
                            if n % 3 == 2:
                                job_end(ins, name)
                        if n % 3 < 2:
                            ins.then_inc(w_used, 1)
                        if has_ada(f, n):
                            ada_columns(("ada", f, n), i, ada_number(f, i, n))

            def mixer():
                def unit(name):
                    return unit_ready(name)

                def last_of(ins, name):
                    if unit_end[name] is None:
                        ins.then_inc(w_used, 1)

                def feature_unit(name, jobs, act_hi=u_hi, act_lo=u_lo, kn=DC, width=COLS):
                    w = unit(name)
                    for j, job in enumerate(jobs):
                        feature_chunk(w, j, job, act_hi, act_lo, kn, width)

                def feature_chunk(w, j, job, act_hi=u_hi, act_lo=u_lo, kn=DC, width=COLS):
                    ps = job_start(pe, job)
                    job_end(three_passes(ps, k_pairs(w, j, kn, act_hi, act_lo, width=width)), job)

                def token_unit(name, jobs, n):
                    wh, wl = unit(name)
                    per = TT // len(jobs)
                    for b, job in enumerate(jobs):
                        ps = job_start(pe, job)
                        for i in range(per):
                            t = b * per + i
                            pairs = [(u_hi[:, k, t * P:(t + 1) * P], u_lo[:, k, t * P:(t + 1) * P],
                                      wh[:, k * n:(k + 1) * n], wl[:, k * n:(k + 1) * n]) for k in range(DC)]
                            ins = three_passes(ps[:, i * n:(i + 1) * n], pairs)
                        job_end(ins, job)

                chunks_as_they_come(unit(("qk", 0)), [("qk", 0), ("qk", 1)], 0, DC)
                pe.wait_ge(mixer_consts, 1)
                token_unit(("vsw",), [("vsw", 0), ("vsw", 1)], COLS)
                wh, wl = unit(("gt",))
                ps = job_start(pe, ("gt",))
                pairs = [(wh[:, k * GATE_ROWS:(k + 1) * GATE_ROWS], wl[:, k * GATE_ROWS:(k + 1) * GATE_ROWS],
                          u_hi[:, k, :], u_lo[:, k, :]) for k in range(DC)]
                job_end(three_passes(ps[0:GATE_ROWS, :], pairs), ("gt",))
                token_unit(("v", 0), [("v", 0, 0), ("v", 0, 1)], COLS)
                ps = job_start(pe, ("gT",))
                taken(pe, ("gt",))
                for t in range(TT):
                    ins = pe.transpose(ps[:, t * GATE_N:(t + 1) * GATE_N], g_rows[:, t * P:(t + 1) * P],
                                       ident[64:64 + GATE_N, 64:64 + GATE_N])
                job_end(ins, ("gT",))
                token_unit(("v", 1), [("v", 1, 0), ("v", 1, 1)], COLS)
                for n in range(1, 4):
                    feature_unit(("qk", n), [("qk", 2 * n), ("qk", 2 * n + 1)])
                def column_gates():
                    ps = job_start(pe, ("colT",))
                    pe.wait_ge(m_ready, 1)
                    pe.wait_ge(em_ready, 1)
                    for a, row in enumerate((row_i, row_t)):
                        for t in range(TT):
                            at_ = (a * TT + t) * MH
                            ins = pe.transpose(ps[:, at_:at_ + MH], row[:, t * P:(t + 1) * P], ident[0:MH, 0:MH])
                    job_end(ins, ("colT",))

                def head_scores(hd):
                    ps = job_start(pe, ("negM", hd))
                    job_end(pe.matmul(ps, pick[:, hd, :], row_m[:], start=True, stop=True), ("negM", hd))
                    pe.wait_ge(qk_ready, MH + hd + 1)
                    for j in range(TT):
                        ps = job_start(pe, ("S", hd, j))
                        job_end(pe.matmul(ps[:, 0:T - j * P], qkc[:, MH + hd, j * P:(j + 1) * P], qkc[:, hd, j * P:T],
                                          start=True, stop=True), ("S", hd, j))

                def head_values(hd):
                    for b in range(2):
                        ps = job_start(pe, ("num", hd, b))
                        for i in range(2):
                            t = 2 * b + i
                            for j in range(t + 1):
                                taken(pe, ("S", hd, j))
                                ins = pe.matmul(ps[:, i * (MD + 1):(i + 1) * (MD + 1)], p_m[:, j, (t - j) * P:(t - j + 1) * P],
                                                v_aug[:, j, hd, :], start=(j == 0), stop=(j == t))
                        job_end(ins, ("num", hd, b))

                def hidden(kv, a):
                    wh, wl = unit(("c1", kv, a))
                    if a == 0:
                        pe.wait_ge(blk_lo_ready, kv + 1)
                    job = ("hid", kv)
                    ps = job_start(pe, job) if a == 0 else PS[:, plan.jobs[job][0], :]
                    bh, bl = (x_[:, a * DC:(a + 1) * DC, :, :].rearrange("p l g n -> p l (g n)") for x_ in (blk_hi, blk_lo))
                    for k in range(DC):
                        at_ = slice(k * COLS, (k + 1) * COLS)
                        pe.matmul(ps[0:64, 0:COLS], bh[:, k, :], wh[:, at_], start=(a == 0 and k == 0), stop=False)
                        pe.matmul(ps[0:64, 0:COLS], bl[:, k, :], wh[:, at_], start=False, stop=False)
                        ins = pe.matmul(ps[0:64, 0:COLS], bh[:, k, :], wl[:, at_], start=False, stop=(a == 1 and k == DC - 1))
                    if a == 1:
                        job_end(ins, job)
                    last_of(ins, ("c1", kv, a))

                def hidden_features(kv):
                    ps = job_start(pe, ("hidT", kv))
                    taken(pe, ("hid", kv))
                    for half in range(2):
                        ins = pe.transpose(ps[:, half * 64:(half + 1) * 64], hid_t[:, kv, half * P:(half + 1) * P],
                                           ident[0:64, 0:64])
                    job_end(ins, ("hidT", kv))

                feature_unit(("kcvc",), [("kcvc", "a"), ("kcvc", "b")])
                feature_unit(("o", 0), [("o", 0), ("o", 1)])
                column_gates()
                taken(pe, ("v", 1, 1))
                head_scores(0)
                feature_unit(("o", 1), [("o", 2), ("o", 3)])
                head_values(0)
                head_scores(1)
                feature_unit(("kk",), [("kk", "a"), ("kk", "b")])
                head_values(1)
                head_scores(2)
                feature_unit(("qn", 0), [("qn", 0, "a"), ("qn", 0, "b")])
                head_values(2)
                head_scores(3)
                hidden(0, 0)
                hidden(0, 1)
                head_values(3)
                hidden_features(0)
                feature_unit(("qn", 1), [("qn", 1, "a"), ("qn", 1, "b")])
                ps = job_start(pe, ("kcmp",))
                taken(pe, ("hidT", 0))
                for g in range(NG):
                    for half in range(2):
                        ins = pe.matmul(ps[g * ND:(g + 1) * ND, 0:32], w2[:, 0, half, :], hid[:, 0, half, g * 32:(g + 1) * 32],
                                        start=(half == 0), stop=(half == 1))
                job_end(ins, ("kcmp",))
                for hd in range(MH):
                    ps = job_start(pe, ("hT", hd))
                    pe.wait_ge(hm_normed, hd + 1)
                    for t in range(TT):
                        ins = pe.transpose(ps[:, t * P:(t + 1) * P], hm[:, hd, t * P:(t + 1) * P], ident[:])
                    job_end(ins, ("hT", hd))
                hidden(1, 0)
                hidden(1, 1)

                def compressed_values():
                    ps = job_start(pe, ("vcmp",))
                    pe.wait_ge(hid_rep_ready, 1)
                    for g in range(NG):
                        for half in range(2):
                            ins = pe.matmul(ps[:, g * ND:(g + 1) * ND], hid_rep[:, half, g, :, :].rearrange("p h n -> p (h n)"),
                                            w2[:, 1, half, :], start=(half == 0), stop=(half == 1))
                    job_end(ins, ("vcmp",))

                taken(pe, ("kcmp",))
                taken(pe, ("qn", 1, "b"))
                taken(pe, ("kk", "b"))

                def cmp_scores(t):
                    ps = job_start(pe, ("sc", t))
                    for hh in range(HG):
                        ins = pe.matmul(ps[:, hh * 64:(hh + 1) * 64], qn[:, hh, t * P:(t + 1) * P],
                                        k_cmp[:].rearrange("p g n -> p (g n)"), start=True, stop=True)
                    job_end(ins, ("sc", t))

                def gate_chunk(cch):
                    if cch % 2 == 0:
                        gate_parts[:] = unit(GATES[cch // 2])
                    feature_chunk(gate_parts, cch % 2, gate_job(cch))

                gate_parts = []
                def compressed_output(t):
                    ps = job_start(pe, ("oc", t))
                    taken(pe, ("pcT", t))
                    pe.wait_ge(v_bd_ready, 1)
                    for g in range(NG):
                        ins = pe.matmul(ps[:, g * COLS:(g + 1) * COLS], pt_c[:, g, :], v_bd[:, g, :, :].rearrange("p h e -> p (h e)"),
                                        start=True, stop=True)
                    job_end(ins, ("oc", t))

                cmp_scores(0)
                hidden_features(1)
                for t in range(TT):
                    if t + 1 < TT:
                        cmp_scores(t + 1)
                    gate_chunk(t)
                    if t == 0:
                        compressed_values()
                    if t:
                        compressed_output(t - 1)
                    ps = job_start(pe, ("pcT", t))
                    pe.wait_ge(p_c_ready, t + 1)
                    for g in range(NG):
                        ins = pe.transpose(ps[:, g * P:(g + 1) * P], p_cmp[t % 2][:, 4 * g:4 * g + 4, :].rearrange("p h n -> p (h n)"), ident[:])
                    job_end(ins, ("pcT", t))

                def nsa_scores(s):
                    t, g, hh = STEPS[s]
                    rows = slice(g * ND, (g + 1) * ND)
                    for br, name in enumerate(("ss", "sw")):
                        blocks = blocks_of(t)[br]
                        n = P * len(blocks)
                        ps = job_start(pe, (name, s))
                        pe.matmul(ps[:, 0:n], qn[rows, hh, t * P:(t + 1) * P], ksw[rows, br, blocks[0] * P:(t + 1) * P],
                                  start=True, stop=False)
                        if br == 1 and t - blocks[0] == WINDOW // P:
                            pe.matmul(ps[:, 0:P], ident_b[:], left_b[:], start=False, stop=False)
                        job_end(pe.matmul(ps[:, n - P:n], ident_b[:], diag_b[:], start=False, stop=True), (name, s))

                def nsa_transposes(s):
                    t = STEPS[s][0]
                    for br, (name, score, p) in enumerate((("ts", "ss", p_s), ("tw", "sw", p_w))):
                        ps = job_start(pe, (name, s))
                        taken(pe, (score, s))
                        for j in range(len(blocks_of(t)[br])):
                            ins = pe.transpose(ps[:, j * P:(j + 1) * P], p[s % 2][:, j * P:(j + 1) * P], ident[:])
                        job_end(ins, (name, s))

                def nsa_values(s):
                    t, g, hh = STEPS[s]
                    job = ("o_nsa", t, g)
                    ps = job_start(pe, job) if hh == 0 else PS[:, plan.jobs[job][0], :]
                    for br, (name, pt) in enumerate((("ts", pt_s), ("tw", pt_w))):
                        taken(pe, (name, s))
                        blocks = blocks_of(t)[br]
                        at_ = (2 * hh + br) * ND
                        for n, j in enumerate(blocks):
                            ins = pe.matmul(ps[:, at_:at_ + ND], pt[s % 2][:, n * P:(n + 1) * P], vsw[:, j, br, g * ND:(g + 1) * ND],
                                            start=(n == 0), stop=(n == len(blocks) - 1))
                    if hh == HG - 1:
                        job_end(ins, job)

                pe.wait_ge(mixer_consts, 1)
                nsa_scores(0)
                compressed_output(TT - 1)
                for s in range(len(STEPS)):
                    if s + 1 < len(STEPS):
                        nsa_scores(s + 1)
                    if s in chunk_at:
                        gate_chunk(chunk_at[s])
                    nsa_transposes(s)
                    if s:
                        nsa_values(s - 1)
                nsa_values(len(STEPS) - 1)
                gate_chunk(2 * DC - 2)
                pe.wait_ge(o_acc_ready, 1)
                for fc in range(4):
                    ps = job_start(pe, ("oT", fc))
                    for t in range(TT):
                        ins = pe.transpose(ps[:, t * P:(t + 1) * P], o_acc[:, t, fc * P:(fc + 1) * P], ident[:])
                    job_end(ins, ("oT", fc))
                gate_chunk(2 * DC - 1)
                pe.wait_ge(hm_lo_ready, 1)
                for fc in range(4):
                    taken(pe, ("oT", fc))
                for j in range(2):
                    feature_unit(("um", j), [("ym", 4 * j + n) for n in range(4)], hm_hi, hm_lo, 4, T)
                    feature_unit(("un", j), [("yn", 4 * j + n) for n in range(4)], o_hi, o_lo, 4, T)
                chunks_as_they_come(unit(("wo", 0)), [("y1", 0), ("y1", 1)], 0, 2 * DC)
                for n in range(1, 4):
                    feature_unit(("wo", n), [("y1", 2 * n), ("y1", 2 * n + 1)])

            pe.wait_ge(consts_ready, 1)
            pe.wait_ge(x_landed, 16)
            for cch in range(DC):
                ps = job_start(pe, ("x", cch))
                for t in range(TT):
                    ins = pe.transpose(ps[:, t * P:(t + 1) * P], x_tok[:, t, cch * P:(cch + 1) * P], ident[:])
                job_end(ins, ("x", cch))
            pe.wait_ge(rows_landed, 16 * 9)
            ps = job_start(pe, ("cols", 1))
            job_end(pe.transpose(ps[:, 0:120], rows1[:], ident[0:120, 0:120]), ("cols", 1))
            ps = job_start(pe, ("cols", 2))
            job_end(pe.transpose(ps[:, 0:81], rows2[:], ident[0:81, 0:81]), ("cols", 2))
            pre_norm(0)

            def first_columns(part, cols):
                ps = job_start(pe, ("ada0", part))
                for n, j in enumerate(range(cols.start // P, cols.stop // P)):
                    ins = pe.matmul(ps[:, n:n + 1], chunk(ada_acc0, j), ones[:, 0:1], start=True, stop=True)
                job_end(ins, ("ada0", part))

            pe.wait_ge(first_summed, 1)
            first_columns("scale", SCALE)
            spread_inverse("pre", 0)
            pe.wait_ge(first_summed, 2)
            first_columns("a", SHIFT_A)

            def shift_bc():
                pe.wait_ge(ada_summed, 1)
                pe.wait_ge(shift_c_summed, 1)
                first_columns("bc", slice(SHIFT_B.start, SHIFT_C.stop))

            ffn_up(0, shift_bc)
            ffn_down(0)
            post_norm(0)
            pre_norm(1)
            spread_inverse("pre", 1)
            mixer()
            post_norm(1)
            pre_norm(2)
            spread_inverse("pre", 2)
            ffn_up(1)
            ffn_down(1)
            post_norm(2)
            for cch in range(DC):
                h_updated(pe, 2, cch)
                ps = job_start(pe, ("out", cch))
                for t in range(TT):
                    ins = pe.transpose(ps[:, t * P:(t + 1) * P], h[:, cch, t * P:(t + 1) * P], ident[:])
                job_end(ins, ("out", cch))


_INS = ['x', 'c', 'w_ada', 'b_ada', 'norm_gains', 'ffn_wg', 'ffn_wu', 'ffn_wd', 'w_in', 'mlstm_conv_w', 'mlstm_conv_b', 'mlstm_gate_b', 'mlstm_head_gain', 'cmp_pe', 'cmp_w1', 'cmp_b1', 'cmp_w2', 'cmp_b2', 'w_up_mlstm', 'w_up_nsa', 'w_out']
_OUTS = [((1, 512, 1024), 'float32')]


def kernel(**inputs):
    import numpy as _np
    import concourse.bacc as _bacc
    from concourse import mybir as _mybir
    from concourse.bass_utils import run_bass_kernel_spmd as _run

    nc = _bacc.Bacc("TRN2", target_bir_lowering=False, num_devices=1)
    arrays, args = {}, []
    for name in _INS:
        a = _np.ascontiguousarray(inputs[name])
        if a.dtype.kind in "iu":
            a = a.astype(_np.int64)
        arrays[f"in_{name}_dram"] = a
        args.append(nc.dram_tensor(f"in_{name}_dram", a.shape, _mybir.dt.from_np(a.dtype), kind="ExternalInput").ap())
    for i, (shape, dtype) in enumerate(_OUTS):
        dt = _mybir.dt.from_np(_np.dtype(dtype))
        args.append(nc.dram_tensor(f"out_{i}_dram", shape, dt, kind="ExternalOutput").ap())
    build_layer(nc, *args)
    r = _run(nc, [arrays], core_ids=[0])
    got = tuple(r.results[0][f"out_{i}_dram"] for i in range(len(_OUTS)))
    return got[0]
```
